# Optimizing a Trainium2 kernel written in Bass

```python
import math
import jax, jax.numpy as jnp
from jax import lax
import numpy as np

D_MODEL = 1024
BATCH = 1
SEQ = 256
DEPTH = 2
DEC_BATCH = 8
DEC_SEQ = 1
PAST_LEN = 1024
PAGE_SIZE = 128

PLE_DIM = 256
SSD_EXPAND = 2
SSD_D_INNER = SSD_EXPAND * D_MODEL
SSD_HEADDIM = 64
SSD_HEADS = SSD_D_INNER // SSD_HEADDIM
SSD_GROUPS = 4
SSD_HPG = SSD_HEADS // SSD_GROUPS
SSD_STATE = 128
SSD_CONV = 4
SSD_CHUNK = 128
SSD_CONV_DIM = SSD_D_INNER + 2 * SSD_GROUPS * SSD_STATE
SSD_IN_DIM = SSD_D_INNER + SSD_CONV_DIM + SSD_HEADS
NSA_HEADS = 16
NSA_KV_HEADS = 4
NSA_REP = NSA_HEADS // NSA_KV_HEADS
NSA_HEAD_DIM = D_MODEL // NSA_HEADS
NSA_BLOCK = 64
NSA_TOP_BLOCKS = 16
NSA_WINDOW = 512
NSA_QBLK = 16
NSA_KV_SLOTS = 4
NSA_IN_DIM = NSA_HEADS * NSA_HEAD_DIM + 6 * NSA_KV_HEADS * NSA_HEAD_DIM + 3 * NSA_HEADS
N_EXPERTS = 16
N_EXPERT_GROUPS = 4
EXPERTS_PER_GROUP = N_EXPERTS // N_EXPERT_GROUPS
MOE_TOP_K = 2
D_FF_EXPERT = 512
N_SSD_LAYERS = (DEPTH + 1) // 2
N_NSA_LAYERS = DEPTH // 2
DEEPNORM_ALPHA = (2.0 * DEPTH) ** 0.25
DEEPNORM_BETA = (8.0 * DEPTH) ** -0.25
LN_EPS = 1e-5
NEG_INF = -1e30

kernel_name = "ssd_nsa_hybrid_decode_step"

def layer_norm(x, g, b):
    xf = x.astype(jnp.float32)
    mu = xf.mean(-1, keepdims=True)
    var = jnp.square(xf - mu).mean(-1, keepdims=True)
    return ((xf - mu) * lax.rsqrt(var + LN_EPS) * g + b).astype(x.dtype)

def masked_softmax(s, mask):
    s = jnp.where(mask, s.astype(jnp.float32), NEG_INF)
    m = s.max(-1, keepdims=True)
    e = jnp.exp(s - m) * mask
    return e / jnp.maximum(e.sum(-1, keepdims=True), 1e-30)

def alibi_slopes():
    return 2.0 ** (-8.0 * jnp.arange(1, NSA_HEADS + 1, dtype=jnp.float32) / NSA_HEADS)

def ssd_chunk_step(state, xs, a_heads):
    x, dt, bm, cm = xs
    q = x.shape[1]
    cum = jnp.cumsum(dt * a_heads, axis=1)
    causal = jnp.tril(jnp.ones((q, q), dtype=bool))[None, :, :, None, None]
    seg = cum[:, :, None] - cum[:, None, :]
    decay = jnp.where(causal, jnp.exp(jnp.where(causal, seg, 0.0)), 0.0)
    cb = jnp.einsum('btgn,bsgn->btsg', cm, bm)
    xdt = x * dt[..., None]
    y = jnp.einsum('btsgr,bsgrp->btgrp', cb[..., None] * decay, xdt)
    y = y + jnp.einsum('btgn,bgrpn->btgrp', cm, state) * jnp.exp(cum)[..., None]
    to_end = jnp.exp(cum[:, -1:] - cum)
    new_state = state * jnp.exp(cum[:, -1])[..., None, None] + jnp.einsum('bsgrp,bsgn->bgrpn', xdt * to_end[..., None], bm)
    return new_state, y

def ssd_mixer(h, conv_state, ssm_state, w_in, conv_w, conv_b, dt_bias, a_log, d_skip, norm_g, w_out):
    bsz, t, _ = h.shape
    f32 = jnp.float32
    proj = h @ w_in
    z = proj[..., :SSD_D_INNER]
    xbc = proj[..., SSD_D_INNER:SSD_D_INNER + SSD_CONV_DIM]
    dt_raw = proj[..., SSD_D_INNER + SSD_CONV_DIM:]
    xpad = jnp.concatenate([conv_state.astype(xbc.dtype), xbc], axis=1)
    conv = conv_b + xpad[:, 0:t] * conv_w[0]
    for k in range(1, SSD_CONV):
        conv = conv + xpad[:, k:k + t] * conv_w[k]
    conv = jax.nn.silu(conv)
    new_conv_state = xpad[:, t:]
    nbc = SSD_GROUPS * SSD_STATE
    xs = conv[..., :SSD_D_INNER].reshape(bsz, t, SSD_GROUPS, SSD_HPG, SSD_HEADDIM).astype(f32)
    bm = conv[..., SSD_D_INNER:SSD_D_INNER + nbc].reshape(bsz, t, SSD_GROUPS, SSD_STATE).astype(f32)
    cm = conv[..., SSD_D_INNER + nbc:].reshape(bsz, t, SSD_GROUPS, SSD_STATE).astype(f32)
    dt = jax.nn.softplus(dt_raw.astype(f32) + dt_bias).reshape(bsz, t, SSD_GROUPS, SSD_HPG)
    a_heads = -jnp.exp(a_log.astype(f32)).reshape(SSD_GROUPS, SSD_HPG)
    q = SSD_CHUNK if t % SSD_CHUNK == 0 else t
    nc = t // q

    def to_chunks(a):
        return jnp.moveaxis(a.reshape(bsz, nc, q, *a.shape[2:]), 1, 0)

    state0 = ssm_state.astype(f32).reshape(bsz, SSD_GROUPS, SSD_HPG, SSD_HEADDIM, SSD_STATE)
    state, y = lax.scan(lambda s, c: ssd_chunk_step(s, c, a_heads), state0,
                        (to_chunks(xs), to_chunks(dt), to_chunks(bm), to_chunks(cm)))
    y = jnp.moveaxis(y, 0, 1).reshape(bsz, t, SSD_GROUPS, SSD_HPG, SSD_HEADDIM)
    y = y + d_skip.reshape(SSD_GROUPS, SSD_HPG)[..., None] * xs
    y = y.reshape(bsz, t, SSD_GROUPS, SSD_HPG * SSD_HEADDIM) * jax.nn.silu(z.astype(f32)).reshape(bsz, t, SSD_GROUPS, SSD_HPG * SSD_HEADDIM)
    y = y * lax.rsqrt(jnp.mean(y * y, -1, keepdims=True) + 1e-5)
    y = (y.reshape(bsz, t, SSD_D_INNER) * norm_g).astype(h.dtype)
    new_state = state.reshape(bsz, SSD_HEADS, SSD_HEADDIM, SSD_STATE).astype(h.dtype)
    return y @ w_out, new_conv_state, new_state

def nsa_project(h, w_in):
    bsz, t, _ = h.shape
    proj = h @ w_in
    qd = NSA_HEADS * NSA_HEAD_DIM
    kvd = NSA_KV_HEADS * NSA_HEAD_DIM
    q = proj[..., :qd].reshape(bsz, t, NSA_KV_HEADS, NSA_REP, NSA_HEAD_DIM) * (NSA_HEAD_DIM ** -0.5)
    kv = proj[..., qd:qd + 6 * kvd].reshape(bsz, t, 6, NSA_KV_HEADS, NSA_HEAD_DIM)
    gates = jax.nn.sigmoid(proj[..., qd + 6 * kvd:].astype(jnp.float32)).reshape(bsz, t, NSA_KV_HEADS, NSA_REP, 3)
    return q, kv[:, :, 0:4], kv[:, :, 4:6], gates

def nsa_compress(kv_cmp, pos_w):
    bsz, s = kv_cmp.shape[:2]
    blocks = kv_cmp.reshape(bsz, s // NSA_BLOCK, NSA_BLOCK, 2, NSA_KV_HEADS, NSA_HEAD_DIM)
    w = jax.nn.softmax(pos_w.astype(jnp.float32), axis=1).astype(kv_cmp.dtype)
    kvc = jnp.einsum('bnlckd,clk->bnckd', blocks, w)
    return kvc[:, :, 0], kvc[:, :, 1]

def nsa_attend(q, gates, q_pos, kc, vc, gather_sel, kw, vw, w_pos, slopes):
    bsz, tq = q.shape[:2]
    nb = kc.shape[1]
    slope = slopes.reshape(NSA_KV_HEADS, NSA_REP)
    blk = jnp.arange(nb)
    dist_c = (q_pos[:, None] - ((blk + 1) * NSA_BLOCK - 1)[None, :]).astype(jnp.float32)
    s_c = jnp.einsum('btkrd,bnkd->btkrn', q, kc).astype(jnp.float32) - slope[None, None, :, :, None] * dist_c[None, :, None, None, :]
    p_c = masked_softmax(s_c, (dist_c >= 0)[None, :, None, None, :])
    o_c = jnp.einsum('btkrn,bnkd->btkrd', p_c.astype(vc.dtype), vc)
    cur = q_pos // NSA_BLOCK
    imp = p_c.sum(axis=3)
    forced = (blk[None, :] == cur[:, None]) | (blk[None, :] == 0)
    imp = jnp.where(forced[None, :, None, :], 1e4, imp)
    imp = jnp.where((blk[None, :] > cur[:, None])[None, :, None, :], -1.0, imp)
    n_sel = min(NSA_TOP_BLOCKS, nb)
    _, idx = lax.top_k(imp, n_sel)
    ks, vs = gather_sel(idx)
    s_pos = idx[..., None] * NSA_BLOCK + jnp.arange(NSA_BLOCK)
    dist_s = (q_pos[None, :, None, None, None] - s_pos).astype(jnp.float32)
    s_s = jnp.einsum('btkrd,btknld->btkrnl', q, ks).astype(jnp.float32) - slope[None, None, :, :, None, None] * dist_s[:, :, :, None]
    s_s = s_s.reshape(bsz, tq, NSA_KV_HEADS, NSA_REP, n_sel * NSA_BLOCK)
    mask_s = (dist_s >= 0).reshape(bsz, tq, NSA_KV_HEADS, 1, n_sel * NSA_BLOCK)
    p_s = masked_softmax(s_s, mask_s).reshape(bsz, tq, NSA_KV_HEADS, NSA_REP, n_sel, NSA_BLOCK)
    o_s = jnp.einsum('btkrnl,btknld->btkrd', p_s.astype(vs.dtype), vs)
    dist_w = q_pos[:, None] - w_pos[None, :]
    mask_w = (dist_w >= 0) & (dist_w < NSA_WINDOW) & (w_pos >= 0)[None, :]
    s_w = jnp.einsum('btkrd,bskd->btkrs', q, kw).astype(jnp.float32) - slope[None, None, :, :, None] * dist_w.astype(jnp.float32)[None, :, None, None, :]
    p_w = masked_softmax(s_w, mask_w[None, :, None, None, :])
    o_w = jnp.einsum('btkrs,bskd->btkrd', p_w.astype(vw.dtype), vw)
    o = gates[..., 0:1] * o_c + gates[..., 1:2] * o_s + gates[..., 2:3] * o_w
    return o.astype(q.dtype)

def nsa_prompt(h, w_in, pos_w, w_out, slopes):
    bsz, t, _ = h.shape
    q, kv4, kvw, gates = nsa_project(h, w_in)
    s_pad = -(-t // NSA_BLOCK) * NSA_BLOCK
    kv4p = jnp.pad(kv4, ((0, 0), (0, s_pad - t), (0, 0), (0, 0), (0, 0)))
    kc, vc = nsa_compress(kv4p[:, :, 0:2], pos_w)
    sel_blocks = kv4p.reshape(bsz, s_pad // NSA_BLOCK, NSA_BLOCK, NSA_KV_SLOTS, NSA_KV_HEADS, NSA_HEAD_DIM)
    bi = jnp.arange(bsz)[:, None, None, None]
    ki = jnp.arange(NSA_KV_HEADS)[None, None, :, None]

    def gather_sel(idx):
        g = sel_blocks[bi, idx, :, 2:4, ki]
        return g[..., 0, :], g[..., 1, :]

    kwp = jnp.pad(kvw, ((0, 0), (NSA_WINDOW, 0), (0, 0), (0, 0), (0, 0)))
    nq = t // NSA_QBLK

    def block(args):
        qb, gb, start = args
        q_pos = start + jnp.arange(NSA_QBLK)
        win = lax.dynamic_slice_in_dim(kwp, start, NSA_WINDOW + NSA_QBLK, axis=1)
        w_pos = start - NSA_WINDOW + jnp.arange(NSA_WINDOW + NSA_QBLK)
        return nsa_attend(qb, gb, q_pos, kc, vc, gather_sel, win[:, :, 0], win[:, :, 1], w_pos, slopes)

    qb = jnp.moveaxis(q.reshape(bsz, nq, NSA_QBLK, NSA_KV_HEADS, NSA_REP, NSA_HEAD_DIM), 1, 0)
    gb = jnp.moveaxis(gates.reshape(bsz, nq, NSA_QBLK, NSA_KV_HEADS, NSA_REP, 3), 1, 0)
    starts = jnp.arange(nq, dtype=jnp.int32) * NSA_QBLK
    o = lax.map(block, (qb, gb, starts))
    o = jnp.moveaxis(o, 0, 1).reshape(bsz, t, NSA_HEADS * NSA_HEAD_DIM)
    w_keep = min(NSA_WINDOW, t)
    return o @ w_out, kv4, kvw[:, t - w_keep:]

def nsa_sample(h, kv_pool, page_table, win_cache, w_in, pos_w, w_out, slopes):
    bsz, t, _ = h.shape
    q, kv4, kvw, gates = nsa_project(h, w_in)
    total = PAST_LEN + t
    s_pad = -(-total // NSA_BLOCK) * NSA_BLOCK
    past_cmp = kv_pool[page_table, :, 0:2].reshape(bsz, PAST_LEN, 2, NSA_KV_HEADS, NSA_HEAD_DIM)
    cmp_rows = jnp.concatenate([past_cmp.astype(kv4.dtype), kv4[:, :, 0:2]], axis=1)
    cmp_rows = jnp.pad(cmp_rows, ((0, 0), (0, s_pad - total), (0, 0), (0, 0), (0, 0)))
    kc, vc = nsa_compress(cmp_rows, pos_w)
    nb_past = PAST_LEN // NSA_BLOCK
    bpp = PAGE_SIZE // NSA_BLOCK
    pool_blocks = kv_pool.reshape(kv_pool.shape[0], bpp, NSA_BLOCK, NSA_KV_SLOTS, NSA_KV_HEADS, NSA_HEAD_DIM)
    new_len = s_pad - PAST_LEN
    new_blocks = jnp.pad(kv4, ((0, 0), (0, new_len - t), (0, 0), (0, 0), (0, 0))).reshape(
        bsz, new_len // NSA_BLOCK, NSA_BLOCK, NSA_KV_SLOTS, NSA_KV_HEADS, NSA_HEAD_DIM)
    bi = jnp.arange(bsz)[:, None, None, None]
    ki = jnp.arange(NSA_KV_HEADS)[None, None, :, None]

    def gather_sel(idx):
        past_idx = jnp.minimum(idx, nb_past - 1)
        phys = page_table[bi, past_idx // bpp]
        g_past = pool_blocks[phys, past_idx % bpp, :, 2:4, ki]
        g_new = new_blocks[bi, jnp.clip(idx - nb_past, 0, new_blocks.shape[1] - 1), :, 2:4, ki]
        g = jnp.where((idx >= nb_past)[..., None, None, None], g_new, g_past.astype(g_new.dtype))
        return g[..., 0, :], g[..., 1, :]

    win_rows = jnp.concatenate([win_cache.astype(kvw.dtype), kvw], axis=1)
    w_buf = win_cache.shape[1]
    w_pos = PAST_LEN - w_buf + jnp.arange(w_buf + t)
    q_pos = PAST_LEN + jnp.arange(t)
    o = nsa_attend(q, gates, q_pos, kc, vc, gather_sel, win_rows[:, :, 0], win_rows[:, :, 1], w_pos, slopes)
    o = o.reshape(bsz, t, NSA_HEADS * NSA_HEAD_DIM)
    return o @ w_out, kv4, win_rows[:, t:]

def moe(h, router_w, router_bias, w_gate, w_up, w_down):
    score = jax.nn.sigmoid((h @ router_w).astype(jnp.float32))
    sel = score + router_bias
    grp = sel.reshape(*sel.shape[:-1], N_EXPERT_GROUPS, EXPERTS_PER_GROUP)
    grp_score = lax.top_k(grp, 2)[0].sum(-1)
    best = jnp.argmax(grp_score, axis=-1)
    in_group = (jnp.arange(N_EXPERTS) // EXPERTS_PER_GROUP) == best[..., None]
    _, idx = lax.top_k(jnp.where(in_group, sel, NEG_INF), MOE_TOP_K)
    w = jnp.take_along_axis(score, idx, axis=-1)
    w = w / w.sum(-1, keepdims=True)
    gate = (jax.nn.one_hot(idx, N_EXPERTS, dtype=jnp.float32) * w[..., None]).sum(-2).astype(h.dtype)
    out = jnp.zeros_like(h)
    for e in range(N_EXPERTS):
        hid = jax.nn.silu(h @ w_gate[e]) * (h @ w_up[e])
        out = out + gate[..., e:e + 1] * (hid @ w_down[e])
    return out

def layer_tail(x, mix, p_i, ln1_g, ln1_b, ln2_g, ln2_b, router_w, router_bias, w_gate, w_up, w_down, ple_proj, ple_gate):
    h = layer_norm(DEEPNORM_ALPHA * x + mix, ln1_g, ln1_b)
    h = layer_norm(DEEPNORM_ALPHA * h + moe(h, router_w, router_bias, w_gate, w_up, w_down), ln2_g, ln2_b)
    return h + jax.nn.sigmoid(h @ ple_gate) * (p_i @ ple_proj)

def setup_inputs(seed: int = 0) -> dict:
    key = jax.random.key(seed)
    ks = iter(jax.random.split(key, 48))
    f32 = jnp.float32

    def nrm(shape, scale):
        return scale * jax.random.normal(next(ks), shape, f32)

    n_pages = PAST_LEN // PAGE_SIZE
    n_pool = (DEC_BATCH * n_pages * 5 + 3) // 4
    w_buf = min(NSA_WINDOW, PAST_LEN)
    beta = DEEPNORM_BETA
    x_prompt = nrm((BATCH, SEQ, D_MODEL), 1.0)
    x_sample = nrm((DEC_BATCH, DEC_SEQ, D_MODEL), 1.0)
    state_ssm = nrm((N_SSD_LAYERS, DEC_BATCH, SSD_HEADS, SSD_HEADDIM, SSD_STATE), 0.5)
    state_conv = nrm((N_SSD_LAYERS, DEC_BATCH, SSD_CONV - 1, SSD_CONV_DIM), 1.0)
    cache_kv = nrm((N_NSA_LAYERS, n_pool, PAGE_SIZE, NSA_KV_SLOTS, NSA_KV_HEADS, NSA_HEAD_DIM), 1.0)
    cache_win = nrm((N_NSA_LAYERS, DEC_BATCH, w_buf, 2, NSA_KV_HEADS, NSA_HEAD_DIM), 1.0)
    page_table = jax.random.permutation(next(ks), n_pool)[:DEC_BATCH * n_pages].reshape(DEC_BATCH, n_pages).astype(jnp.int32)
    p_prompt = nrm((DEPTH, BATCH, SEQ, PLE_DIM), 1.0)
    p_sample = nrm((DEPTH, DEC_BATCH, DEC_SEQ, PLE_DIM), 1.0)
    ssd_w_in = nrm((N_SSD_LAYERS, D_MODEL, SSD_IN_DIM), D_MODEL ** -0.5)
    ssd_conv_w = nrm((N_SSD_LAYERS, SSD_CONV, SSD_CONV_DIM), SSD_CONV ** -0.5)
    ssd_conv_b = nrm((N_SSD_LAYERS, SSD_CONV_DIM), 0.02)
    dt0 = jnp.exp(jax.random.uniform(next(ks), (N_SSD_LAYERS, SSD_HEADS), f32, math.log(1e-3), math.log(1e-1)))
    ssd_dt_bias = dt0 + jnp.log(-jnp.expm1(-dt0))
    ssd_a_log = jnp.log(jax.random.uniform(next(ks), (N_SSD_LAYERS, SSD_HEADS), f32, 1.0, 16.0))
    ssd_d = 1.0 + nrm((N_SSD_LAYERS, SSD_HEADS), 0.02)
    ssd_norm_g = 1.0 + nrm((N_SSD_LAYERS, SSD_D_INNER), 0.02)
    ssd_w_out = nrm((N_SSD_LAYERS, SSD_D_INNER, D_MODEL), SSD_D_INNER ** -0.5 * beta)
    kvd = NSA_KV_HEADS * NSA_HEAD_DIM
    slot_scale = jnp.repeat(jnp.array([1.0, beta, 1.0, beta, 1.0, beta], f32), kvd)
    col_scale = jnp.concatenate([jnp.ones((NSA_HEADS * NSA_HEAD_DIM,), f32), slot_scale, jnp.ones((3 * NSA_HEADS,), f32)])
    nsa_w_in = nrm((N_NSA_LAYERS, D_MODEL, NSA_IN_DIM), D_MODEL ** -0.5) * col_scale
    nsa_pos_w = nrm((N_NSA_LAYERS, 2, NSA_BLOCK, NSA_KV_HEADS), 0.5)
    nsa_w_out = nrm((N_NSA_LAYERS, NSA_HEADS * NSA_HEAD_DIM, D_MODEL), (NSA_HEADS * NSA_HEAD_DIM) ** -0.5 * beta)
    ln1_g = 1.0 + nrm((DEPTH, D_MODEL), 0.02)
    ln1_b = nrm((DEPTH, D_MODEL), 0.02)
    ln2_g = 1.0 + nrm((DEPTH, D_MODEL), 0.02)
    ln2_b = nrm((DEPTH, D_MODEL), 0.02)
    router_w = nrm((D_MODEL, N_EXPERTS), D_MODEL ** -0.5)
    router_bias = nrm((N_EXPERTS,), 0.01)
    moe_w_gate = nrm((DEPTH, N_EXPERTS, D_MODEL, D_FF_EXPERT), D_MODEL ** -0.5)
    moe_w_up = nrm((DEPTH, N_EXPERTS, D_MODEL, D_FF_EXPERT), D_MODEL ** -0.5 * beta)
    moe_w_down = nrm((DEPTH, N_EXPERTS, D_FF_EXPERT, D_MODEL), D_FF_EXPERT ** -0.5 * beta)
    ple_proj = nrm((DEPTH, PLE_DIM, D_MODEL), PLE_DIM ** -0.5 * beta)
    ple_gate = nrm((DEPTH, D_MODEL, D_MODEL), D_MODEL ** -0.5)
    return {"x_prompt": x_prompt, "x_sample": x_sample, "state_ssm": state_ssm, "state_conv": state_conv,
            "cache_kv": cache_kv, "cache_win": cache_win, "page_table": page_table,
            "p_prompt": p_prompt, "p_sample": p_sample,
            "ssd_w_in": ssd_w_in, "ssd_conv_w": ssd_conv_w, "ssd_conv_b": ssd_conv_b, "ssd_dt_bias": ssd_dt_bias,
            "ssd_a_log": ssd_a_log, "ssd_d": ssd_d, "ssd_norm_g": ssd_norm_g, "ssd_w_out": ssd_w_out,
            "nsa_w_in": nsa_w_in, "nsa_pos_w": nsa_pos_w, "nsa_w_out": nsa_w_out,
            "ln1_g": ln1_g, "ln1_b": ln1_b, "ln2_g": ln2_g, "ln2_b": ln2_b,
            "router_w": router_w, "router_bias": router_bias,
            "moe_w_gate": moe_w_gate, "moe_w_up": moe_w_up, "moe_w_down": moe_w_down,
            "ple_proj": ple_proj, "ple_gate": ple_gate}

def reference(x_prompt, x_sample, state_ssm, state_conv, cache_kv, cache_win, page_table, p_prompt, p_sample,
              ssd_w_in, ssd_conv_w, ssd_conv_b, ssd_dt_bias, ssd_a_log, ssd_d, ssd_norm_g, ssd_w_out,
              nsa_w_in, nsa_pos_w, nsa_w_out, ln1_g, ln1_b, ln2_g, ln2_b, router_w, router_bias,
              moe_w_gate, moe_w_up, moe_w_down, ple_proj, ple_gate):
    slopes = alibi_slopes()
    xp, xs = x_prompt, x_sample
    bp = xp.shape[0]
    ssm_p, conv_p, kv_p, win_p = [], [], [], []
    ssm_s, conv_s, kv_s, win_s = [], [], [], []
    for i in range(DEPTH):
        j = i // 2
        if i % 2 == 0:
            ssd_w = (ssd_w_in[j], ssd_conv_w[j], ssd_conv_b[j], ssd_dt_bias[j], ssd_a_log[j], ssd_d[j], ssd_norm_g[j], ssd_w_out[j])
            zero_conv = jnp.zeros((bp, SSD_CONV - 1, SSD_CONV_DIM), xp.dtype)
            zero_ssm = jnp.zeros((bp, SSD_HEADS, SSD_HEADDIM, SSD_STATE), xp.dtype)
            mix_p, c_new, s_new = ssd_mixer(xp, zero_conv, zero_ssm, *ssd_w)
            conv_p.append(c_new)
            ssm_p.append(s_new)
            mix_s, c_new, s_new = ssd_mixer(xs, state_conv[j], state_ssm[j], *ssd_w)
            conv_s.append(c_new)
            ssm_s.append(s_new)
        else:
            mix_p, r_new, w_new = nsa_prompt(xp, nsa_w_in[j], nsa_pos_w[j], nsa_w_out[j], slopes)
            kv_p.append(r_new)
            win_p.append(w_new)
            mix_s, r_new, w_new = nsa_sample(xs, cache_kv[j], page_table, cache_win[j], nsa_w_in[j], nsa_pos_w[j], nsa_w_out[j], slopes)
            kv_s.append(r_new)
            win_s.append(w_new)
        tail_w = (ln1_g[i], ln1_b[i], ln2_g[i], ln2_b[i], router_w, router_bias,
                  moe_w_gate[i], moe_w_up[i], moe_w_down[i], ple_proj[i], ple_gate[i])
        xp = layer_tail(xp, mix_p, p_prompt[i], *tail_w)
        xs = layer_tail(xs, mix_s, p_sample[i], *tail_w)
    y_prompt = xp
    y_sample = xs
    new_ssm_prompt = jnp.stack(ssm_p)
    new_conv_prompt = jnp.stack(conv_p)
    new_kv_prompt = jnp.stack(kv_p)
    new_win_prompt = jnp.stack(win_p)
    new_ssm_sample = jnp.stack(ssm_s)
    new_conv_sample = jnp.stack(conv_s)
    new_kv_sample = jnp.stack(kv_s)
    new_win_sample = jnp.stack(win_s)
    return (y_prompt, y_sample, new_ssm_prompt, new_conv_prompt, new_kv_prompt, new_win_prompt,
            new_ssm_sample, new_conv_sample, new_kv_sample, new_win_sample)


_drawn_inputs = setup_inputs


def setup_inputs(seed=0):
    import zlib

    import numpy as np

    out = dict(_drawn_inputs(seed))
    spreads = {}
    factors = {'ssd_d': 6.379, 'ssd_norm_g': 5.539, 'nsa_pos_w': 3.021}
    for name, (base, spread) in spreads.items():
        noise = np.random.default_rng([zlib.crc32(name.encode()), seed]).standard_normal(out[name].shape)
        drawn = base * np.exp(spread * noise) if base else spread * noise
        out[name] = __import__('jax').numpy.asarray(drawn.astype(out[name].dtype))
    for name, factor in factors.items():
        out[name] = (out[name] * factor).astype(out[name].dtype)
    return out
```

```python
from contextlib import ExitStack

import numpy as np

import concourse.bass as bass
from concourse import mybir

F32 = mybir.dt.float32
I32 = mybir.dt.int32
ALU = mybir.AluOpType
ACT = mybir.ActivationFunctionType
AX = mybir.AxisListType

P = 128
D = 1024
KD = D // P
SEQ = 256
DB = 8
T = SEQ + DB
QT = SEQ // P
DI, HD, NH, NG, NS, NCONV = 2048, 64, 32, 4, 128, 4
CD = DI + 2 * NG * NS
JX = DI // P
JC = CD // P
AH, AKV, REP, BLK, WIN, PAST, PAGE = 16, 4, 4, 64, 512, 1024, 128
NPG = PAST // PAGE
NBP = PAST // BLK
QS = 64 ** -0.5
KVT = 6 * AKV * 64 // P
NE, FF, EG = 16, 512, 4
CH = 4096
ALPHA = 4.0 ** 0.25
EPS = 1e-5
NEG = -1e30


class Chain:

    def __init__(self, sem):
        self.sem, self.n = sem, 0

    def __call__(self, eng, ins):
        self.n += 1
        ins.then_inc(self.sem, 1)
        eng.wait_ge(self.sem, self.n)


def trunk(nc, I, O):
    root = ExitStack()
    with root:
        def sem(name):
            return root.enter_context(nc.semaphore(name))

        def keep(name, shape, dt=F32):
            return root.enter_context(nc.sbuf_tensor(name, shape, dt))

        ring = keep("expert_ring", [P, 2, 3 * CH])
        xT = keep("xT", [P, KD, T])
        ident = keep("ident", [P, P])
        ones = keep("ones", [P, P])
        m384 = keep("m384", [P, 3 * P])
        lnp = keep("lnp", [P, 2, 4, KD])
        rw = keep("router_w", [P, KD, NE])
        rbias = keep("router_bias", [P, NE])
        epst = keep("eps", [P, 1])
        lower4 = keep("lower4", [P, EG, EG])
        dve_step, act_step, pool_step = (Chain(sem(n)) for n in ("dve_step", "act_step", "pool_step"))
        ld_const, ld_wg, ld_wu, ld_wd = sem("ld_const"), [sem("ld_wg0"), sem("ld_wg1")], \
            [sem("ld_wu0"), sem("ld_wu1")], [sem("ld_wd0"), sem("ld_wd1")]
        ld_chunk = [sem("ld_chunk0"), sem("ld_chunk1"), sem("ld_chunk2")]
        chunk_count = [0, 0, 0]
        stored = sem("stored")
        n_stored = [0]

        chunk = [ring[:, 1, c * CH:(c + 1) * CH] for c in range(3)]

        def load_chunk(sp, c, src):
            n = 1
            for v in src.shape[1:]:
                n *= v
            sp.dma_start(chunk[c][0:src.shape[0], 0:n].rearrange("p (a b) -> p a b", b=src.shape[2]), src)\
              .then_inc(ld_chunk[c], 16)

        def store(eng, dst, src):
            n_stored[0] += 16
            eng.dma_start(dst, src).then_inc(stored, 16)

        def load_expert(sp, e, s):
            g = lambda w, k: w[bass.ds(e, 1)].rearrange("a (k p) n -> p (a k) n", p=P)
            sp.dma_start(ring[:, s, 0:CH].rearrange("p (k n) -> p k n", k=KD), g(I["moe_w_gate"], KD)).then_inc(ld_wg[s], 16)
            sp.dma_start(ring[:, s, CH:2 * CH].rearrange("p (k n) -> p k n", k=KD), g(I["moe_w_up"], KD)).then_inc(ld_wu[s], 16)
            sp.dma_start(ring[:, s, 2 * CH:3 * CH].rearrange("p (k n) -> p k n", k=FF // P), g(I["moe_w_down"], 4)).then_inc(ld_wd[s], 16)

        with ExitStack() as ssd:
            def sb(name, shape, dt=F32):
                return ssd.enter_context(nc.sbuf_tensor(name, shape, dt))

            zs = sb("z_silu", [P, JX, T])
            cv = sb("conv_out", [P, JC, T])
            dtr = sb("dt_raw", [NH, T])
            heads = sb("head_params", [NH, 3])
            normg = sb("norm_g", [P, JX])

            with ExitStack() as st:
                raw = st.enter_context(nc.sbuf_tensor("xbc_raw", [P, 2, SEQ + 3], F32))
                taps = st.enter_context(nc.sbuf_tensor("taps", [P, JC, NCONV, DB], F32))
                cacc = st.enter_context(nc.sbuf_tensor("conv_acc", [P, 2, T], F32))
                lastp = st.enter_context(nc.sbuf_tensor("last_prompt", [P, JC, 3], F32))
                convp = st.enter_context(nc.sbuf_tensor("conv_params", [P, JC, NCONV + 1], F32))
                bank = [st.enter_context(nc.psum_tensor(f"pj{i}", [P, 512], F32)) for i in range(8)]
                tile_done, tile_taken, conv_done, silu_done, pads, out_ready = (
                    sem(n) for n in ("s_tile_done", "s_tile_taken", "s_conv_done", "s_silu_done", "s_pads", "s_convout"))
                NT = JX + JC + 1
                taken = lambda m: m + 1 if m < JX else JX + 2 * (m - JX + 1)
                nchunk = (NT + 3) // 4

                with nc.Block() as block:
                    @block.sync
                    def _(sp):
                        sp.dma_start(xT[:], I["xT"].rearrange("(k p) t -> p k t", p=P)).then_inc(ld_const, 16)
                        w = I["ssd_w_in"].rearrange("(k p) n -> p k n", p=P)
                        for c in range(nchunk):
                            lo, hi = c * 512, min(c * 512 + 512, w.shape[2])
                            if c >= 2:
                                sp.wait_ge(tile_done, 4 * (c - 1))
                            load_chunk(sp, c % 2, w[:, :, lo:hi])
                            if c == 0:
                                for dst, name in ((convp[:], "conv_params"), (taps[:, :, 0:3, :], "conv_state"),
                                                  (ident[:], "ident"), (ones[:], "ones"), (m384[:], "m384"), (lnp[:], "lnp"),
                                                  (rw[:], "router_w"), (rbias[:], "router_bias"),
                                                  (epst[:], "eps"), (lower4[:], "lower4"), (heads[:], "heads"), (normg[:], "norm_g")):
                                    sp.dma_start(dst, I[name]).then_inc(ld_const, 16)
                        load_expert(sp, 0, 0)
                        sp.wait_ge(conv_done, JC)
                        store(sp, O["conv_prompt"], lastp[:])
                        store(sp, O["conv_sample"], taps[:, :, 1:4, :])
                        sp.wait_ge(stored, n_stored[0])

                    @block.tensor
                    def _(pe):
                        pe.wait_ge(ld_const, 16 * 13)
                        for m in range(NT):
                            c, s = m // 4, (m // 4) % 2
                            if m % 4 == 0:
                                pe.wait_ge(ld_chunk[s], 16 * (c // 2 + 1))
                            if m >= 8:
                                pe.wait_ge(tile_taken, taken(m - 8))
                            M = P if m < NT - 1 else NH
                            wc = chunk[s][:, 0:KD * (512 if m < NT - 1 else NH)].rearrange("p (k n) -> p k n", k=KD)
                            for k in range(KD):
                                last = nc.tensor.matmul(bank[m % 8][0:M, 0:T], wc[:, k, (m % 4) * P:(m % 4) * P + M],
                                                        xT[:, k, :], start=k == 0, stop=k == KD - 1)
                            last.then_inc(tile_done, 1)

                    @block.scalar
                    def _(act):
                        def silu(j):
                            act.wait_ge(conv_done, j + 1)
                            nc.scalar.activation(cv[:, j, :], cacc[:, j % 2, :], ACT.Silu).then_inc(silu_done, 1)
                        act.wait_ge(ld_const, 16 * 13)
                        act.wait_ge(pads, 1)
                        for m in range(NT):
                            act.wait_ge(tile_done, m + 1)
                            j = m - JX
                            if m < JX:
                                nc.scalar.activation(zs[:, m, :], bank[m % 8][:, 0:T], ACT.Silu).then_inc(tile_taken, 1)
                            elif j < JC:
                                if j >= 2:
                                    act.wait_ge(conv_done, j - 1)
                                nc.scalar.activation(raw[:, j % 2, 3:SEQ + 3], bank[m % 8][:, 0:SEQ], ACT.Copy).then_inc(tile_taken, 1)
                                nc.scalar.activation(taps[:, j, 3, :], bank[m % 8][:, SEQ:T], ACT.Copy).then_inc(tile_taken, 1)
                                if j >= 1:
                                    silu(j - 1)
                            else:
                                nc.scalar.activation(dtr[:], bank[m % 8][0:NH, 0:T], ACT.Identity, bias=heads[:, 0:1]).then_inc(tile_taken, 1)
                                silu(JC - 1)

                    @block.vector
                    def _(dve):
                        nc.vector.memset(raw[:, :, 0:3], 0.0).then_inc(pads, 1)
                        dve.wait_ge(ld_const, 16 * 13)
                        for j in range(JC):
                            dve.wait_ge(tile_taken, taken(JX + j))
                            if j >= 2:
                                dve.wait_ge(silu_done, j - 1)
                            r, a = raw[:, j % 2, :], cacc[:, j % 2, :]
                            nc.vector.tensor_copy(lastp[:, j, :], r[:, SEQ:SEQ + 3])
                            nc.vector.tensor_scalar(a[:, 0:SEQ], r[:, 0:SEQ], convp[:, j, 0:1], convp[:, j, 4:5], ALU.mult, ALU.add)
                            dve_step(dve, nc.vector.tensor_scalar(a[:, SEQ:T], taps[:, j, 0, :], convp[:, j, 0:1], convp[:, j, 4:5], ALU.mult, ALU.add))
                            for k in range(1, NCONV):
                                nc.vector.scalar_tensor_tensor(a[:, 0:SEQ], r[:, k:k + SEQ], convp[:, j, k:k + 1], a[:, 0:SEQ], ALU.mult, ALU.add)
                                i2 = nc.vector.scalar_tensor_tensor(a[:, SEQ:T], taps[:, j, k, :], convp[:, j, k:k + 1], a[:, SEQ:T], ALU.mult, ALU.add)
                                if k < NCONV - 1:
                                    dve_step(dve, i2)
                            i2.then_inc(conv_done, 1)
                chunk_count[0] = (nchunk + 1) // 2
                chunk_count[1] = nchunk // 2

            with ExitStack() as st:
                def sb2(name, shape, dt=F32):
                    return st.enter_context(nc.sbuf_tensor(name, shape, dt))

                hsel = ring[0:NH, 1, 0:DI]
                sp_t = sb2("softplus_tmp", [NH, 2, T])
                dt = sb2("dt", [NH, T])
                dta = sb2("dta", [NH, T])
                na = sb2("neg_a", [NH, 1])
                expin = sb2("expand_in", [NH, 2 * DB + 1])
                ex = sb2("expanded", [P, JX, 2 * DB + 1])
                dtt = sb2("dt_tok", [P, QT, NH])
                dtat = sb2("dta_tok", [P, QT, NH])
                cumt = sb2("cum_tok", [P, QT, NH])
                cumh = sb2("cum_head", [NH, SEQ])
                toend = sb2("to_end", [P, QT, NH])
                xd = ring[:, 1, CH:2 * CH].rearrange("p (q f) -> p q f", q=QT)
                btok = sb2("b_tok", [P, QT, NG * NS])
                bcd = sb2("bc_dec", [DB, 2, NG * NS])
                cbm = sb2("cb_masked", [P, 2, 3 * P])
                seg = sb2("seg", [P, 2, 3 * P])
                dec = sb2("decay", [P, 2, 3 * P])
                mm_ = sb2("weights_sbm", [P, 2, 3 * P])
                stp = ring[:, 1, 2 * CH:2 * CH + JX * NS].rearrange("p (j n) -> p j n", j=JX)
                std = sb2("state_dec", [P, 2, JX, NS])
                yd = sb2("y_dec", [P, JX, DB])
                junk = sb2("junk", [P, 4, NS])
                pt = [st.enter_context(nc.psum_tensor(f"ss{i}", [P, 512], F32)) for i in range(8)]
                (ld_hsel, sc_dt, dt_ready, da_ready, tr_done, tr_taken, cum_pe, cum_ready, cb_done, cb_ready, bc_done, seg_done,
                 exp_done, w_done, y_done, y_taken, exp_pe, ex_ready, xe_ready, st_done, st_taken, bcb_done, dec_read, new_state, sd_scaled) = (
                    sem("ss_" + n) for n in (
                        "ld_hsel", "sc_dt", "dt_ready", "da_ready", "tr_done", "tr_taken", "cum_pe", "cum_ready", "cb_done", "cb_ready",
                        "bc_done", "seg_done", "exp_done", "w_done", "y_done", "y_taken", "exp_pe", "ex_ready", "xe_ready", "st_done", "st_taken",
                        "bcb_done", "dec_read", "new_state", "sd_scaled"))
                st_out = [sem("ss_out0"), sem("ss_out1")]
                ld_sd = [sem("ss_ld_sd0"), sem("ss_ld_sd1")]
                NTR = 4 + 8 + 2 + 2

                with nc.Block() as block:
                    @block.sync
                    def _(sp):
                        sp.dma_start(hsel, I["hsel"]).then_inc(ld_hsel, 16)
                        for b in range(DB):
                            if b >= 2:
                                sp.wait_ge(st_out[b % 2], 16 * (b // 2))
                            sp.dma_start(std[:, b % 2], I["state_ssm"][b].rearrange("(j p) n -> p j n", p=P)).then_inc(ld_sd[b % 2], 16)
                            if b == 0:
                                sp.wait_ge(st_taken, 4)
                                store(sp, O["ssm_prompt"].rearrange("(j p) n -> p j n", p=P), stp)
                            sp.wait_ge(new_state, 16 * (b + 1))
                            sp.dma_start(O["ssm_sample"][b].rearrange("(j p) n -> p j n", p=P), std[:, b % 2]).then_inc(st_out[b % 2], 16)
                        for s in range(2):
                            sp.wait_ge(st_out[s], 16 * (DB // 2))
                        sp.wait_ge(stored, n_stored[0])

                    @block.scalar
                    def _(act):
                        act_step(act, nc.scalar.activation(sp_t[:, 0, :], dtr[:], ACT.Abs))
                        act_step(act, nc.scalar.activation(sp_t[:, 1, :], sp_t[:, 0, :], ACT.Exp, scale=-1.0))
                        nc.scalar.activation(sp_t[:, 0, :], sp_t[:, 1, :], ACT.Ln, bias=ones[0:NH, 0:1]).then_inc(sc_dt, 1)
                        nc.scalar.activation(na[:], heads[:, 1:2], ACT.Exp).then_inc(sc_dt, 1)
                        act.wait_ge(dt_ready, 1)
                        nc.scalar.activation(expin[:, DB:2 * DB], dta[:, SEQ:T], ACT.Exp).then_inc(da_ready, 1)
                        act.wait_ge(cum_ready, 3)
                        nc.scalar.activation(toend[:], toend[:], ACT.Exp).then_inc(cum_ready, 1)
                        for h in range(NH):
                            act.wait_ge(seg_done, 2 * h + 2)
                            if h >= 2:
                                act.wait_ge(w_done, h - 1)
                            nc.scalar.activation(dec[:, h % 2, :], seg[:, h % 2, :], ACT.Exp).then_inc(exp_done, 1)
                        for g in range(4):
                            act.wait_ge(st_done, g + 1)
                            nc.scalar.activation(stp[:, 4 * g:4 * g + 4, :], pt[g][:].rearrange("p (j n) -> p j n", j=4), ACT.Copy).then_inc(st_taken, 1)
                        act.wait_ge(ex_ready, 1)
                        for b in range(DB):
                            act.wait_ge(ld_sd[b % 2], 16 * (b // 2 + 1))
                            for j in range(JX):
                                nc.scalar.activation(std[:, b % 2, j, :], std[:, b % 2, j, :], ACT.Copy, scale=ex[:, j, DB + b:DB + b + 1]).then_inc(sd_scaled, 1)

                    @block.tensor
                    def _(pe):
                        tr = nc.tensor.transpose
                        pe.wait_ge(dt_ready, 1)
                        for q in range(QT):
                            tr(pt[0][:, q * NH:(q + 1) * NH], dt[:, q * P:(q + 1) * P], ident[0:NH, 0:NH])
                            last = tr(pt[0][:, (2 + q) * NH:(3 + q) * NH], dta[:, q * P:(q + 1) * P], ident[0:NH, 0:NH])
                        last.then_inc(tr_done, 1)
                        pe.wait_ge(tr_taken, 1)
                        tri = m384[:, 0:P]
                        mm = nc.tensor.matmul
                        mm(pt[1][:, 0:NH], tri, dtat[:, 0, :], start=True, stop=True)
                        mm(pt[1][:, NH:2 * NH], tri, dtat[:, 1, :], start=True, stop=False)
                        mm(pt[1][:, NH:2 * NH], ones[:], dtat[:, 0, :], start=False, stop=True)
                        mm(pt[1][:, 2 * NH:3 * NH], ones[:], dtat[:, 0, :], start=True, stop=False)
                        mm(pt[1][:, 2 * NH:3 * NH], ones[:], dtat[:, 1, :], start=False, stop=True)
                        mm(pt[2][0:NH, 0:SEQ], dtat[:, 0, :], m384[:, 0:SEQ], start=True, stop=False, skip_group_check=True)
                        mm(pt[2][0:NH, P:SEQ], dtat[:, 1, :], tri, start=False, stop=True, skip_group_check=True).then_inc(cum_pe, 1)
                        for n in range(12):
                            bk = pt[3 + n % 3]
                            if n >= 3:
                                pe.wait_ge(tr_taken, 1 + n - 2)
                            for a in range(4):
                                if n < 8:
                                    last = tr(bk[:, a * P:(a + 1) * P], cv[:, 4 * (n // 2) + a, (n % 2) * P:(n % 2 + 1) * P], ident[:])
                                elif n < 10:
                                    last = tr(bk[:, a * P:(a + 1) * P], cv[:, JX + a, (n - 8) * P:(n - 7) * P], ident[:])
                                else:
                                    last = tr(bk[0:DB, a * P:(a + 1) * P], cv[:, JX + NG * (n - 10) + a, SEQ:T], ident[:])
                            last.then_inc(tr_done, 1)
                        pe.wait_ge(da_ready, 1)
                        pe.wait_ge(ld_hsel, 16)
                        for j in range(JX):
                            last = mm(pt[6][:, j * (2 * DB + 1):(j + 1) * (2 * DB + 1)], hsel[:, j * P:(j + 1) * P], expin[:], start=True, stop=True)
                        last.then_inc(exp_pe, 1)
                        pe.wait_ge(cum_ready, 2)
                        pe.wait_ge(tr_taken, 13)

                        def cb(g):
                            if g == 0:
                                pe.wait_ge(ex_ready, 1)
                            if g >= 2:
                                pe.wait_ge(cb_ready, g - 1)
                            bk = pt[6 + g % 2]
                            mm(bk[:, 0:SEQ], cv[:, JX + g, 0:P], cv[:, JX + NG + g, 0:SEQ], start=True, stop=True)
                            mm(bk[:, SEQ:3 * P], cv[:, JX + g, P:SEQ], cv[:, JX + NG + g, P:SEQ], start=True, stop=True).then_inc(cb_done, 1)

                        def spread(h):
                            if h >= 3:
                                pe.wait_ge(seg_done, 2 * (h - 2))
                            mm(pt[h % 3][:, 0:SEQ], ident[0:NH, h:h + 1].to_broadcast([NH, P]), cumh[:], start=True, stop=True).then_inc(bc_done, 1)

                        cb(0)
                        spread(0)
                        spread(1)
                        for h in range(NH):
                            if h % 8 == 4 and h // 8 + 1 < NG:
                                cb(h // 8 + 1)
                            if h + 2 < NH:
                                spread(h + 2)
                            j, half = h // 2, 64 * (h % 2)
                            pe.wait_ge(w_done, h + 1)
                            if h % 2 == 0 and j >= 3:
                                pe.wait_ge(y_taken, j - 2)
                            yb = pt[3 + j % 3]
                            mm(yb[half:half + 64, 0:SEQ], xd[:, 0, h * HD:(h + 1) * HD], mm_[:, h % 2, 0:SEQ], start=True, stop=False, skip_group_check=True)
                            mm(yb[half:half + 64, P:SEQ], xd[:, 1, h * HD:(h + 1) * HD], mm_[:, h % 2, SEQ:3 * P], start=False, stop=True,
                               skip_group_check=True).then_inc(y_done, 1)
                        pe.wait_ge(xe_ready, 2)
                        pe.wait_ge(y_taken, JX)
                        for j in range(JX):
                            g = j // 4
                            for q in range(QT):
                                last = mm(pt[g][:, (j % 4) * NS:(j % 4 + 1) * NS], xd[:, q, j * P:(j + 1) * P],
                                          btok[:, q, g * NS:(g + 1) * NS], start=q == 0, stop=q == QT - 1)
                            if j % 4 == 3:
                                last.then_inc(st_done, 1)
                        for b in range(DB):
                            if b >= 2:
                                pe.wait_ge(dec_read, JX * (b - 1))
                            for c in range(2):
                                last = mm(pt[4 + 2 * (b % 2) + c][:], ident[0:DB, b:b + 1].to_broadcast([DB, P]), bcd[:, c, :], start=True, stop=True)
                            last.then_inc(bcb_done, 1)

                    @block.vector
                    def _(dve):
                        V = nc.vector
                        dve.wait_ge(sc_dt, 2)
                        V.tensor_scalar(na[:], na[:], -1.0, None, ALU.mult)
                        dve_step(dve, V.tensor_scalar(sp_t[:, 1, :], dtr[:], 0.0, None, ALU.max))
                        dve_step(dve, V.tensor_tensor(dt[:], sp_t[:, 0, :], sp_t[:, 1, :], ALU.add))
                        V.tensor_copy(expin[:, 0:DB], dt[:, SEQ:T])
                        V.tensor_copy(expin[:, 2 * DB:2 * DB + 1], heads[:, 2:3])
                        V.tensor_scalar(dta[:], dt[:], na[:, 0:1], None, ALU.mult).then_inc(dt_ready, 1)
                        dve.wait_ge(tr_done, 1)
                        V.tensor_copy(dtt[:], pt[0][:, 0:2 * NH].rearrange("p (q h) -> p q h", q=QT))
                        V.tensor_copy(dtat[:], pt[0][:, 2 * NH:4 * NH].rearrange("p (q h) -> p q h", q=QT)).then_inc(tr_taken, 1)
                        dve.wait_ge(tr_taken, 1)
                        dve.wait_ge(cum_pe, 1)
                        V.tensor_copy(cumt[:], pt[1][:, 0:2 * NH].rearrange("p (q h) -> p q h", q=QT)).then_inc(cum_ready, 1)
                        V.tensor_copy(cumh[:], pt[2][0:NH, 0:SEQ]).then_inc(cum_ready, 1)
                        dve.wait_ge(cum_ready, 2)
                        V.tensor_tensor(toend[:], pt[1][:, 2 * NH:3 * NH].unsqueeze(1).to_broadcast([P, QT, NH]), cumt[:], ALU.subtract).then_inc(cum_ready, 1)
                        for n in range(12):
                            dve.wait_ge(tr_done, n + 2)
                            bk = pt[3 + n % 3]
                            if n < 8:
                                g, q = n // 2, n % 2
                                V.tensor_tensor(xd[:, q, g * 512:(g + 1) * 512].rearrange("p (h d) -> p h d", d=HD), bk[:].rearrange("p (h d) -> p h d", d=HD),
                                                dtt[:, q, 8 * g:8 * g + 8].unsqueeze(2).to_broadcast([P, 8, HD]), ALU.mult).then_inc(tr_taken, 1)
                            elif n < 10:
                                V.tensor_copy(btok[:, n - 8, :], bk[:]).then_inc(tr_taken, 1)
                            else:
                                V.tensor_copy(bcd[:, n - 10, :], bk[0:DB, :]).then_inc(tr_taken, 1)
                        dve.wait_ge(exp_pe, 1)
                        V.tensor_copy(ex[:], pt[6][:, 0:JX * (2 * DB + 1)].rearrange("p (j c) -> p j c", j=JX)).then_inc(ex_ready, 1)
                        dve.wait_ge(ex_ready, 1)
                        def mask_cb(g):
                            dve.wait_ge(cb_done, g + 1)
                            V.tensor_tensor(cbm[:, g % 2, :], pt[6 + g % 2][:, 0:3 * P], m384[:], ALU.mult).then_inc(cb_ready, 1)
                        def segments(h):
                            dve.wait_ge(bc_done, h + 1)
                            if h >= 2:
                                dve.wait_ge(exp_done, h - 1)
                            V.tensor_scalar(seg[:, h % 2, 0:SEQ], pt[h % 3][:, 0:SEQ], cumt[:, 0, h:h + 1], 0.0, ALU.subtract, ALU.min).then_inc(seg_done, 1)
                            V.tensor_scalar(seg[:, h % 2, SEQ:3 * P], pt[h % 3][:, P:SEQ], cumt[:, 1, h:h + 1], 0.0, ALU.subtract, ALU.min).then_inc(seg_done, 1)
                        def y_out(j):
                            dve.wait_ge(y_done, 2 * j + 2)
                            dve_step(dve, V.scalar_tensor_tensor(cv[:, j, 0:SEQ], cv[:, j, 0:SEQ], ex[:, j, 2 * DB:2 * DB + 1], pt[3 + j % 3][:, 0:SEQ], ALU.mult, ALU.add))
                            V.tensor_tensor(cv[:, j, 0:SEQ], cv[:, j, 0:SEQ], zs[:, j, 0:SEQ], ALU.mult).then_inc(y_taken, 1)
                        mask_cb(0)
                        segments(0)
                        for h in range(NH):
                            if h % 8 == 7 and h // 8 + 1 < NG:
                                mask_cb(h // 8 + 1)
                            if h + 1 < NH:
                                segments(h + 1)
                            dve.wait_ge(exp_done, h + 1)
                            dve.wait_ge(cb_ready, h // 8 + 1)
                            if h >= 2:
                                dve.wait_ge(y_done, h - 1)
                            V.tensor_tensor(mm_[:, h % 2, :], dec[:, h % 2, :], cbm[:, (h // 8) % 2, :], ALU.mult).then_inc(w_done, 1)
                            if h % 2 == 1 and h >= 3:
                                y_out(h // 2 - 1)
                        y_out(JX - 1)
                        dve.wait_ge(cum_ready, 4)
                        for q in range(QT):
                            x3 = xd[:, q, :].rearrange("p (h d) -> p h d", d=HD)
                            V.tensor_tensor(x3, x3, toend[:, q, :].unsqueeze(2).to_broadcast([P, NH, HD]), ALU.mult).then_inc(xe_ready, 1)
                        V.tensor_tensor(yd[:], cv[:, 0:JX, SEQ:T], ex[:, :, 0:DB], ALU.mult).then_inc(dve_step.sem, 1)
                        dve_step.n += 1
                        dve.wait_ge(dve_step.sem, dve_step.n)
                        for b in range(DB):
                            dve.wait_ge(bcb_done, b + 1)
                            for j in range(JX):
                                g, s = j // 4, std[:, b % 2, j, :]
                                dve.wait_ge(sd_scaled, JX * b + j + 1)
                                V.scalar_tensor_tensor(s, pt[4 + 2 * (b % 2)][:, g * NS:(g + 1) * NS], yd[:, j, b:b + 1], s, ALU.mult, ALU.add).then_inc(new_state, 1)
                            for j in range(JX):
                                g, s = j // 4, std[:, b % 2, j, :]
                                dve.wait_ge(new_state, JX * b + j + 1)
                                if JX * b + j >= 4:
                                    dve.wait_ge(dec_read, JX * b + j - 3)
                                V.tensor_tensor_reduce(junk[:, j % 4, :], s, pt[5 + 2 * (b % 2)][:, g * NS:(g + 1) * NS], 1.0, 0.0, ALU.mult, ALU.add,
                                                       yd[:, j, b:b + 1]).then_inc(dec_read, 1)
                        dve.wait_ge(dec_read, JX * DB)
                        c3 = cv[:, 0:JX, SEQ:T]
                        dve_step(dve, V.tensor_tensor(c3, c3, ex[:, :, 2 * DB:2 * DB + 1].to_broadcast([P, JX, DB]), ALU.mult))
                        dve_step(dve, V.tensor_tensor(c3, c3, yd[:], ALU.add))
                        dve_step(dve, V.tensor_tensor(c3, c3, zs[:, :, SEQ:T], ALU.mult))

            with ExitStack() as st:
                rr = st.enter_context(nc.sbuf_tensor("rms", [P, NG, T], F32))
                bank = [st.enter_context(nc.psum_tensor(f"on{i}", [P, 512], F32)) for i in range(8)]
                sq_done, ms_done, sqrt_done, y_ready, o_done, o_taken = (sem("so_" + n) for n in ("sq", "ms", "sqrt", "y", "done", "taken"))
                base = [c * 16 for c in chunk_count]
                with nc.Block() as block:
                    @block.sync
                    def _(sp):
                        w = I["ssd_w_out"].rearrange("(k p) n -> p k n", p=P)
                        for c in range(4):
                            if c >= 2:
                                sp.wait_ge(o_done, 2 * (c - 1))
                            load_chunk(sp, c % 2, w[:, :, c * 256:(c + 1) * 256])

                    @block.scalar
                    def _(act):
                        for j in range(JX):
                            nc.scalar.activation(zs[:, j, :], cv[:, j, :], ACT.Square).then_inc(sq_done, 1)
                        for g in range(NG):
                            act.wait_ge(ms_done, g + 1)
                            nc.scalar.activation(rr[:, g, :], bank[g][:, 0:T], ACT.Sqrt, scale=1.0 / 512, bias=epst[:, 0:1]).then_inc(sqrt_done, 1)

                    @block.tensor
                    def _(pe):
                        for j in range(JX):
                            pe.wait_ge(sq_done, j + 1)
                            last = nc.tensor.matmul(bank[j // 4][:, 0:T], ones[:], zs[:, j, :], start=j % 4 == 0, stop=j % 4 == 3)
                            if j % 4 == 3:
                                last.then_inc(ms_done, 1)
                        pe.wait_ge(y_ready, JX)
                        for m in range(KD):
                            c = m // 2
                            if m % 2 == 0:
                                pe.wait_ge(ld_chunk[c % 2], base[c % 2] + 16 * (c // 2 + 1))
                            if m >= 4:
                                pe.wait_ge(o_taken, m - 3)
                            wc = chunk[c % 2].rearrange("p (k n) -> p k n", k=JX)
                            for k in range(JX):
                                last = nc.tensor.matmul(bank[4 + m % 4][:, 0:T], wc[:, k, (m % 2) * P:(m % 2 + 1) * P], cv[:, k, :],
                                                        start=k == 0, stop=k == JX - 1)
                            last.then_inc(o_done, 1)

                    @block.vector
                    def _(dve):
                        V = nc.vector
                        for g in range(NG):
                            dve.wait_ge(sqrt_done, g + 1)
                            dve_step(dve, V.reciprocal(rr[:, g, :], rr[:, g, :]))
                            for j in range(4 * g, 4 * g + 4):
                                V.scalar_tensor_tensor(cv[:, j, :], cv[:, j, :], normg[:, j:j + 1], rr[:, g, :], ALU.mult, ALU.mult).then_inc(y_ready, 1)
                        for m in range(KD):
                            dve.wait_ge(o_done, m + 1)
                            V.scalar_tensor_tensor(xT[:, m, :], xT[:, m, :], ALPHA, bank[4 + m % 4][:, 0:T], ALU.mult, ALU.add).then_inc(o_taken, 1)
                for c in range(2):
                    chunk_count[c] += 2

        ln_sems = [sem("ln_" + n) for n in ("mean", "cent", "sq", "var", "sqrt", "norm")]

        def layer_norm(L, which, src, dst, tag):
            use = 2 * L + which
            with ExitStack() as st:
                sq = st.enter_context(nc.sbuf_tensor("ln_sq_" + tag, [P, KD, T], F32))
                rs = st.enter_context(nc.sbuf_tensor("ln_rs_" + tag, [P, 2, T], F32))
                pm = st.enter_context(nc.psum_tensor("ln_m_" + tag, [P, 512], F32))
                pv = st.enter_context(nc.psum_tensor("ln_v_" + tag, [P, 512], F32))
                s_mean, s_cent, s_sq, s_var, s_sqrt, s_rs = ln_sems
                g, b = lnp[:, L, 2 * which, :], lnp[:, L, 2 * which + 1, :]
                with nc.Block() as block:
                    @block.tensor
                    def _(pe):
                        for k in range(KD):
                            last = nc.tensor.matmul(pm[:, 0:T], ones[:], src[:, k, :], start=k == 0, stop=k == KD - 1)
                        last.then_inc(s_mean, 1)
                        for k in range(KD):
                            pe.wait_ge(s_sq, KD * use + k + 1)
                            last = nc.tensor.matmul(pv[:, 0:T], ones[:], sq[:, k, :], start=k == 0, stop=k == KD - 1)
                        last.then_inc(s_var, 1)

                    @block.scalar
                    def _(act):
                        for k in range(KD):
                            act.wait_ge(s_cent, KD * use + k + 1)
                            nc.scalar.activation(sq[:, k, :], src[:, k, :], ACT.Square).then_inc(s_sq, 1)
                        act.wait_ge(s_var, use + 1)
                        nc.scalar.activation(rs[:, 1, :], pv[:, 0:T], ACT.Sqrt, scale=1.0 / D, bias=epst[:, 0:1]).then_inc(s_sqrt, 1)
                        for k in range(KD):
                            act.wait_ge(s_rs, KD * use + k + 1)
                            nc.scalar.activation(dst[:, k, :], src[:, k, :], ACT.Identity, scale=g[:, k:k + 1], bias=b[:, k:k + 1])

                    @block.vector
                    def _(dve):
                        V = nc.vector
                        dve.wait_ge(s_mean, use + 1)
                        dve_step(dve, V.tensor_scalar(rs[:, 0, :], pm[:, 0:T], 1.0 / D, None, ALU.mult))
                        for k in range(KD):
                            V.tensor_tensor(src[:, k, :], src[:, k, :], rs[:, 0, :], ALU.subtract).then_inc(s_cent, 1)
                        dve.wait_ge(s_sqrt, use + 1)
                        dve_step(dve, V.reciprocal(rs[:, 0, :], rs[:, 1, :]))
                        dve.wait_ge(s_sq, KD * use + KD)
                        for k in range(KD):
                            V.tensor_tensor(src[:, k, :], src[:, k, :], rs[:, 0, :], ALU.mult).then_inc(s_rs, 1)

        router_sems = [sem("r_" + n) for n in ("log", "init", "sig", "gate", "tr", "gT", "bc", "out")]
        ple_sems = [sem("e_" + n) for n in ("ld", "done", "sig", "out")]
        moe_sems = [sem("m_" + n) for n in ("gu", "silu", "mul", "hid", "down", "acc")]

        def tail(L, out=None):
            layer_norm(L, 0, xT, xT, f"a{L}")
            with ExitStack() as outer:
                acc = outer.enter_context(nc.sbuf_tensor(f"acc{L}", [P, KD, T], F32))
                tile3 = [(0, P), (P, P), (SEQ, DB)]
                with ExitStack() as moe:
                    gateb = moe.enter_context(nc.sbuf_tensor(f"gate_b{L}", [P, NE, T], F32))
                    with ExitStack() as st:
                        def sb3(name, shape):
                            return st.enter_context(nc.sbuf_tensor(f"{name}{L}", shape, F32))
                        score, sel, cmp5, eq5, rank, insel, gs, best = (
                            sb3("score", [P, 3, NE]), sb3("sel", [P, 3, NE]), sb3("cmp", [P, 3, EG, EG, EG]), sb3("eq", [P, 3, EG, EG, EG]),
                            sb3("rank", [P, 3, NE]), sb3("insel", [P, 3, NE]), sb3("gs", [P, 3, EG]), sb3("best", [P, 3, EG]))
                        wsum = sb3("wsum", [P, 3])
                        gT = sb3("gT", [NE, T])
                        pr = st.enter_context(nc.psum_tensor(f"pr{L}", [P, 512], F32))
                        pg = [st.enter_context(nc.psum_tensor(f"pg{L}{i}", [P, 512], F32)) for i in range(4)]
                        r_log, r_init, r_sig, r_gate, r_tr, r_gT, r_bc, r_out = router_sems
                        with nc.Block() as block:
                            @block.sync
                            def _(sp):
                                load_expert(sp, NE * L + 1, 1)

                            @block.tensor
                            def _(pe):
                                for q, (t0, n) in enumerate(tile3):
                                    for k in range(KD):
                                        last = nc.tensor.matmul(pr[0:n, q * NE:(q + 1) * NE], xT[:, k, t0:t0 + n], rw[:, k, :], start=k == 0, stop=k == KD - 1)
                                last.then_inc(r_log, 1)
                                pe.wait_ge(r_gate, L + 1)
                                for q, (t0, n) in enumerate(tile3):
                                    last = nc.tensor.transpose(pg[0][0:NE, t0:t0 + n], rank[0:n, q, :], ident[0:n, 0:n])
                                last.then_inc(r_tr, 1)
                                pe.wait_ge(r_gT, L + 1)
                                for e in range(NE):
                                    if e >= 4:
                                        pe.wait_ge(r_out, NE * L + e - 3)
                                    nc.tensor.matmul(pg[e % 4][:, 0:T], ident[0:NE, e:e + 1].to_broadcast([NE, P]), gT[:], start=True, stop=True).then_inc(r_bc, 1)

                            @block.scalar
                            def _(act):
                                act.wait_ge(r_log, L + 1)
                                act.wait_ge(r_init, L + 1)
                                nc.scalar.activation(score[:, 0:2, :], pr[:, 0:2 * NE].rearrange("p (q e) -> p q e", q=2), ACT.Sigmoid).then_inc(r_sig, 1)
                                nc.scalar.activation(score[0:DB, 2, :], pr[0:DB, 2 * NE:3 * NE], ACT.Sigmoid).then_inc(r_sig, 1)
                                for e in range(NE):
                                    act.wait_ge(r_bc, NE * L + e + 1)
                                    nc.scalar.activation(gateb[:, e, :], pg[e % 4][:, 0:T], ACT.Copy).then_inc(r_out, 1)

                            @block.vector
                            def _(dve):
                                V = nc.vector
                                V.memset(score[:], 0.5).then_inc(r_init, 1)
                                V.tensor_scalar(acc[:], xT[:], ALPHA, None, ALU.mult)
                                dve.wait_ge(r_sig, 2 * L + 2)
                                dve_step(dve, V.tensor_tensor(sel[:], score[:], rbias[:].unsqueeze(1).to_broadcast([P, 3, NE]), ALU.add))
                                low = lower4[:].unsqueeze(1).to_broadcast([P, 3 * EG, EG, EG])
                                c4, e4 = (t[:].rearrange("p q g j i -> p (q g) j i") for t in (cmp5, eq5))
                                s3 = sel[:].rearrange("p q (g j) -> p (q g) j", j=EG)
                                si, sj = s3.unsqueeze(2).to_broadcast([P, 3 * EG, EG, EG]), s3.unsqueeze(3).to_broadcast([P, 3 * EG, EG, EG])
                                V.tensor_tensor(c4, si, sj, ALU.is_gt)
                                dve_step(dve, V.tensor_tensor(e4, si, sj, ALU.is_equal))
                                dve_step(dve, V.tensor_tensor(e4, e4, low, ALU.mult))
                                dve_step(dve, V.tensor_tensor(c4, c4, e4, ALU.add))
                                dve_step(dve, V.tensor_reduce(rank[:].rearrange("p q (g j) -> p (q g) j", j=EG), c4, AX.X, ALU.add))
                                dve_step(dve, V.tensor_scalar(insel[:], rank[:], 1.5, None, ALU.is_lt))
                                dve_step(dve, V.tensor_tensor(rank[:], sel[:], insel[:], ALU.mult))
                                dve_step(dve, V.tensor_reduce(gs[:].rearrange("p q g -> p (q g)"), rank[:].rearrange("p q (g j) -> p (q g) j", j=EG), AX.X, ALU.add))
                                gi, gj = gs[:].unsqueeze(2).to_broadcast([P, 3, EG, EG]), gs[:].unsqueeze(3).to_broadcast([P, 3, EG, EG])
                                cg, eg = cmp5[:, :, 0, :, :], eq5[:, :, 0, :, :]
                                V.tensor_tensor(cg, gi, gj, ALU.is_gt)
                                dve_step(dve, V.tensor_tensor(eg, gi, gj, ALU.is_equal))
                                dve_step(dve, V.tensor_tensor(eg, eg, lower4[:].unsqueeze(1).to_broadcast([P, 3, EG, EG]), ALU.mult))
                                dve_step(dve, V.tensor_tensor(cg, cg, eg, ALU.add))
                                dve_step(dve, V.tensor_reduce(best[:], cg, AX.X, ALU.add))
                                dve_step(dve, V.tensor_scalar(best[:], best[:], 0.5, None, ALU.is_lt))
                                i3 = insel[:].rearrange("p q (g j) -> p (q g) j", j=EG)
                                dve_step(dve, V.tensor_tensor(i3, i3, best[:].rearrange("p q g -> p (q g)").unsqueeze(2).to_broadcast([P, 3 * EG, EG]), ALU.mult))
                                dve_step(dve, V.tensor_tensor(insel[:], insel[:], score[:], ALU.mult))
                                dve_step(dve, V.tensor_reduce(wsum[:], insel[:], AX.X, ALU.add))
                                dve_step(dve, V.reciprocal(wsum[:], wsum[:]))
                                V.tensor_tensor(rank[:], insel[:], wsum[:].unsqueeze(2).to_broadcast([P, 3, NE]), ALU.mult).then_inc(r_gate, 1)
                                dve.wait_ge(r_tr, L + 1)
                                V.tensor_copy(gT[:], pg[0][0:NE, 0:T]).then_inc(r_gT, 1)
                    sg = moe.enter_context(nc.sbuf_tensor(f"silu_gate{L}", [P, 2, T], F32))
                    hu = moe.enter_context(nc.sbuf_tensor(f"hid_up{L}", [P, 2, T], F32))
                    hid = moe.enter_context(nc.sbuf_tensor(f"hid{L}", [P, 2, FF // P, T], F32))
                    gu = [[moe.enter_context(nc.psum_tensor(f"gu{L}{n}{w}", [P, 512], F32)) for w in range(2)] for n in range(2)]
                    dn = [moe.enter_context(nc.psum_tensor(f"dn{L}{n}", [P, 512], F32)) for n in range(4)]
                    gu_done, silu_ok, mul_ok, hid_ok, down_done, acc_ok = moe_sems
                    n0, d0 = NE * (FF // P) * L, NE * KD * L
                    NF = FF // P
                    loads_before = 8 * L

                    def pairs(eng, body):
                        body(0, True, False)
                        with eng.Fori(1, NE // 2 - 1) as i:
                            body(i, False, False)
                        body(NE // 2 - 1, False, True)

                    with nc.Block() as block:
                        @block.sync
                        def _(sp):
                            def body(i, first, last):
                                for s in range(2):
                                    if last and (s == 1 or L == 1):
                                        continue
                                    e = 2 * i + s
                                    nxt = NE * L + 2 + e
                                    sp.wait_ge(gu_done, 8 * i + 4 * s + 4 + n0)
                                    k = lambda w: w[bass.ds(nxt, 1)].rearrange("a (k p) n -> p (a k) n", p=P)
                                    sp.dma_start(ring[:, s, 0:CH].rearrange("p (k n) -> p k n", k=KD), k(I["moe_w_gate"])).then_inc(ld_wg[s], 16)
                                    sp.dma_start(ring[:, s, CH:2 * CH].rearrange("p (k n) -> p k n", k=KD), k(I["moe_w_up"])).then_inc(ld_wu[s], 16)
                                    sp.wait_ge(down_done, 16 * i + 8 * s + 8 + d0)
                                    sp.dma_start(ring[:, s, 2 * CH:3 * CH].rearrange("p (k n) -> p k n", k=NF), k(I["moe_w_down"])).then_inc(ld_wd[s], 16)
                            pairs(sp, body)

                        @block.tensor
                        def _(pe):
                            def gate_up(i, s, f, skip_wait):
                                n = 8 * i + 4 * s + f
                                if f == 0:
                                    pe.wait_ge(ld_wg[s], 16 * i + 16 * (loads_before + 1))
                                    pe.wait_ge(ld_wu[s], 16 * i + 16 * (loads_before + 1))
                                if not skip_wait:
                                    pe.wait_ge(hid_ok, n - 1 + n0)
                                for w in range(2):
                                    wt = ring[:, s, w * CH:(w + 1) * CH].rearrange("p (k n) -> p k n", k=KD)
                                    for k in range(KD):
                                        last = nc.tensor.matmul(gu[f % 2][w][:, 0:T], wt[:, k, f * P:(f + 1) * P], xT[:, k, :], start=k == 0, stop=k == KD - 1)
                                last.then_inc(gu_done, 1)

                            def down(i, s, first):
                                pe.wait_ge(ld_wd[s], 16 * i + 16 * (loads_before + 1))
                                pe.wait_ge(hid_ok, 8 * i + 4 * s + 4 + n0)
                                wt = ring[:, s, 2 * CH:3 * CH].rearrange("p (k n) -> p k n", k=NF)
                                for d in range(KD):
                                    if not (first and s == 0 and d < 4):
                                        pe.wait_ge(acc_ok, 16 * i + 8 * s + d - 3 + d0)
                                    for k in range(NF):
                                        last = nc.tensor.matmul(dn[d % 4][:, 0:T], wt[:, k, d * P:(d + 1) * P], hid[:, s, k, :], start=k == 0, stop=k == NF - 1)
                                    last.then_inc(down_done, 1)

                            def body(i, first, last):
                                if first:
                                    gate_up(i, 0, 0, True)
                                for s in range(2):
                                    for f in range(1, NF):
                                        gate_up(i, s, f, first and s == 0 and f < 2)
                                    if s == 0:
                                        gate_up(i, 1, 0, False)
                                    elif not last:
                                        gate_up(i + 1, 0, 0, False)
                                    down(i, s, first)
                            pairs(pe, body)

                        @block.scalar
                        def _(act):
                            def body(i, first, last):
                                for n in range(8):
                                    act.wait_ge(gu_done, 8 * i + n + 1 + n0)
                                    if not (first and n < 2):
                                        act.wait_ge(mul_ok, 8 * i + n - 1 + n0)
                                    nc.scalar.activation(sg[:, n % 2, :], gu[n % 2][0][:, 0:T], ACT.Silu).then_inc(silu_ok, 1)
                            pairs(act, body)

                        @block.vector
                        def _(dve):
                            V = nc.vector

                            def hidden(i, s, f):
                                n = 8 * i + 4 * s + f
                                dve.wait_ge(silu_ok, n + 1 + n0)
                                V.tensor_tensor(hu[:, f % 2, :], gu[f % 2][1][:, 0:T], sg[:, f % 2, :], ALU.mult).then_inc(mul_ok, 1)
                                dve.wait_ge(mul_ok, n + 1 + n0)
                                gb = gateb[:, bass.ds(2 * i + s, 1), :].rearrange("p a t -> p (a t)")
                                V.tensor_tensor(hid[:, s, f, :], hu[:, f % 2, :], gb, ALU.mult).then_inc(hid_ok, 1)

                            def add(i, s):
                                for d in range(KD):
                                    dve.wait_ge(down_done, 16 * i + 8 * s + d + 1 + d0)
                                    V.tensor_tensor(acc[:, d, :], acc[:, d, :], dn[d % 4][:, 0:T], ALU.add).then_inc(acc_ok, 1)

                            def body(i, first, last):
                                if first:
                                    hidden(i, 0, 0)
                                for s in range(2):
                                    for f in range(1, NF):
                                        hidden(i, s, f)
                                    if s == 0:
                                        hidden(i, 1, 0)
                                    elif not last:
                                        hidden(i + 1, 0, 0)
                                    add(i, s)
                            pairs(dve, body)

                layer_norm(L, 1, acc, acc, f"b{L}")
                with ExitStack() as st:
                    pT = st.enter_context(nc.sbuf_tensor(f"pT{L}", [P, 2, T], F32))
                    sgm = st.enter_context(nc.sbuf_tensor(f"sgm{L}", [P, 2, T], F32))
                    pa = [st.enter_context(nc.psum_tensor(f"pa{L}{i}", [P, 512], F32)) for i in range(2)]
                    pb = [st.enter_context(nc.psum_tensor(f"pb{L}{i}", [P, 512], F32)) for i in range(2)]
                    ld_p, e_done, e_sig, e_out = ple_sems
                    cnt = [16 * c for c in chunk_count]
                    with nc.Block() as block:
                        @block.sync
                        def _(sp):
                            sp.dma_start(pT[:], I["pT"][L].rearrange("(k p) t -> p k t", p=P)).then_inc(ld_p, 16)
                            load_chunk(sp, 2, I["ple_proj"][L].rearrange("(k p) n -> p k n", p=P))
                            w = I["ple_gate"][L].rearrange("(k p) n -> p k n", p=P)
                            for c in range(2):
                                load_chunk(sp, c, w[:, :, 512 * c:512 * c + 512])
                            if out is not None:
                                sp.wait_ge(e_out, KD * L + KD)
                                store(sp, out, xT[:])

                        @block.tensor
                        def _(pe):
                            pe.wait_ge(ld_p, 16 * L + 16)
                            pe.wait_ge(ld_chunk[2], cnt[2] + 16)
                            wp = chunk[2][:, 0:2 * D].rearrange("p (k n) -> p k n", k=2)
                            for m in range(KD):
                                if m % 4 == 0:
                                    pe.wait_ge(ld_chunk[m // 4], cnt[m // 4] + 16)
                                if m >= 2:
                                    pe.wait_ge(e_out, KD * L + m - 1)
                                wc = chunk[m // 4].rearrange("p (k n) -> p k n", k=KD)
                                for k in range(KD):
                                    nc.tensor.matmul(pa[m % 2][:, 0:T], wc[:, k, (m % 4) * P:(m % 4 + 1) * P], acc[:, k, :], start=k == 0, stop=k == KD - 1)
                                for k in range(2):
                                    last = nc.tensor.matmul(pb[m % 2][:, 0:T], wp[:, k, m * P:(m + 1) * P], pT[:, k, :], start=k == 0, stop=k == 1)
                                last.then_inc(e_done, 1)

                        @block.scalar
                        def _(act):
                            for m in range(KD):
                                act.wait_ge(e_done, KD * L + m + 1)
                                if m >= 2:
                                    act.wait_ge(e_out, KD * L + m - 1)
                                nc.scalar.activation(sgm[:, m % 2, :], pa[m % 2][:, 0:T], ACT.Sigmoid).then_inc(e_sig, 1)

                        @block.vector
                        def _(dve):
                            for m in range(KD):
                                dve.wait_ge(e_sig, KD * L + m + 1)
                                dve_step(dve, nc.vector.tensor_tensor(sgm[:, m % 2, :], sgm[:, m % 2, :], pb[m % 2][:, 0:T], ALU.mult))
                                nc.vector.tensor_tensor(xT[:, m, :], sgm[:, m % 2, :], acc[:, m, :], ALU.add).then_inc(e_out, 1)
                    for c in range(3):
                        chunk_count[c] += 1

        tail(0)
        with ExitStack() as nsa:
            def sb(name, shape, dt=F32):
                return nsa.enter_context(nc.sbuf_tensor(name, shape, dt))

            qT = sb("q_T", [P, KD, T])
            kvT = sb("kv_T", [P, KVT, T])
            oT = sb("o_T", [P, KD, T])
            gT_ = sb("gates_T", [3 * AH, T])
            vtok = sb("v_tok", [P, QT, 512])
            vnew = sb("v_new", [DB, 512])
            gtok = sb("gates_tok", [P, QT, 3 * AH])
            wb = sb("pos_softmax", [P, 4, BLK])
            kcd = sb("cmp_dec", [P, 4, DB, NBP])
            vcd = sb("vc_dec", [NBP, DB, 256])
            ptab = sb("page_table", [1, DB * NPG], I32)
            K_CMP, V_CMP, K_SEL, V_SEL, K_WIN, V_WIN = range(0, KVT, 2)
            ld_ptab, n_base = sem("ld_ptab"), [16 * c for c in chunk_count]

            with ExitStack() as st:
                bank = [st.enter_context(nc.psum_tensor(f"np{i}", [P, 512], F32)) for i in range(8)]
                tile_done, tile_taken = sem("n_tile_done"), sem("n_tile_taken")
                NT = KD + KVT + 1
                nchunk = (NT + 3) // 4
                with nc.Block() as block:
                    @block.sync
                    def _(sp):
                        w = I["nsa_w_in"].rearrange("(k p) n -> p k n", p=P)
                        for c in range(nchunk):
                            if c >= 2:
                                sp.wait_ge(tile_done, 4 * (c - 1))
                            load_chunk(sp, c % 2, w[:, :, c * 512:min(c * 512 + 512, w.shape[2])])
                        sp.dma_start(wb[:], I["pos_w"]).then_inc(ld_ptab, 16)
                        sp.dma_start(ptab[:], I["page_table"]).then_inc(ld_ptab, 16)
                        store(sp, O["win_old"], I["cache_win"][:, 1:, :])

                    @block.tensor
                    def _(pe):
                        for m in range(NT):
                            c, s = m // 4, (m // 4) % 2
                            if m % 4 == 0:
                                pe.wait_ge(ld_chunk[s], n_base[s] + 16 * (c // 2 + 1))
                            if m >= 8:
                                pe.wait_ge(tile_taken, m - 7)
                            M = P if m < NT - 1 else 3 * AH
                            wc = chunk[s][:, 0:KD * (512 if m < NT - 1 else M)].rearrange("p (k n) -> p k n", k=KD)
                            for k in range(KD):
                                last = nc.tensor.matmul(bank[m % 8][0:M, 0:T], wc[:, k, (m % 4) * P:(m % 4) * P + M],
                                                        xT[:, k, :], start=k == 0, stop=k == KD - 1)
                            last.then_inc(tile_done, 1)

                    @block.scalar
                    def _(act):
                        for m in range(NT):
                            act.wait_ge(tile_done, m + 1)
                            if m < KD:
                                nc.scalar.activation(qT[:, m, :], bank[m % 8][:, 0:T], ACT.Copy, scale=QS).then_inc(tile_taken, 1)
                            elif m < NT - 1:
                                nc.scalar.activation(kvT[:, m - KD, :], bank[m % 8][:, 0:T], ACT.Copy).then_inc(tile_taken, 1)
                            else:
                                nc.scalar.activation(gT_[:], bank[m % 8][0:3 * AH, 0:T], ACT.Sigmoid).then_inc(tile_taken, 1)
                chunk_count[0] += (nchunk + 1) // 2
                chunk_count[1] += nchunk // 2

            with ExitStack() as st:
                def sb2(name, shape, dt=F32):
                    return st.enter_context(nc.sbuf_tensor(name, shape, dt))

                dm = sb2("dist_masked", [P, 3 * P])
                cbias, cmask = sb2("cmp_bias", [P, QT, AH, 4]), sb2("cmp_mask", [P, QT, AH, 4])
                wst = sb2("pos_stat", [P, 4])
                ctmp = sb2("cmp_tmp", [P, 4, SEQ])
                kc = sb2("cmp_prompt", [P, 4, 4])
                vx = sb2("vc_spread", [P, 580])
                vci = sb2("vc_blockdiag", [4 * AH, KD, P])
                pc = sb2("cmp_probs", [P, QT, AH, 4])
                pst = sb2("cmp_stat", [P, QT, AH])
                pct = sb2("cmp_probs_T", [4 * AH, SEQ])
                sbuf = sb2("scores", [P, 3, 3 * P])
                nm, sm, wgt = sb2("neg_max", [P, 3, 2]), sb2("row_sum", [P, 3, 2]), sb2("row_scale", [P, 3, 2])
                pts = sb2("probs_T", [P, 2, 3 * P])
                pt = [st.enter_context(nc.psum_tensor(f"at{i}", [P, 512], F32)) for i in range(8)]
                ld_ac, pos_d, pos_a, kc_ok, pre_tr, pre_tk, csc, cexp_in, cexp, pc_ok, pc_tr, pct_ok = (
                    sem("h_" + n) for n in ("ld", "pos_d", "pos_a", "kc", "pre_tr", "pre_tk", "csc", "cexp_in", "cexp", "pc", "pc_tr", "pct"))
                score_done, soft_done, ex_done, wgt_ok, scaled, tr_ok, pts_ok, pv_ok, ot_ok = (
                    sem("u_" + n) for n in ("score", "soft", "exp", "wgt", "scaled", "tr", "pts", "pv", "ot"))
                NU = 4 * KD

                def unit(u):
                    i, half, v = u // 4, (u // 2) % 2, u % 2
                    return i, 64 * half, v, 8 * (i // 4) + i % 4 + 4 * half, 2 * (i // 4) + half

                with nc.Block() as block:
                    @block.sync
                    def _(sp):
                        for dst, n in ((dm, "dist_masked"), (cbias, "cmp_bias"), (cmask, "cmp_mask")):
                            sp.dma_start(dst[:], I[n]).then_inc(ld_ac, 16)
                        store(sp, O["kv"], kvT[:])
                        w = I["nsa_w_out"].rearrange("(k p) n -> p k n", p=P)
                        for c in range(2):
                            load_chunk(sp, c, w[:, :, c * 512:(c + 1) * 512])

                    @block.gpsimd
                    def _(pool):
                        for u in range(NU):
                            pool.wait_ge(wgt_ok, u + 1)
                            s = sbuf[:, u % 3, :]
                            nc.gpsimd.tensor_scalar(s[:, 0:P], s[:, 0:P], wgt[:, u % 3, 0:1], None, ALU.mult).then_inc(scaled, 1)
                            nc.gpsimd.tensor_scalar(s[:, P:3 * P], s[:, P:3 * P], wgt[:, u % 3, 1:2], None, ALU.mult).then_inc(scaled, 1)

                    @block.tensor
                    def _(pe):
                        tr, mm = nc.tensor.transpose, nc.tensor.matmul
                        vt = (V_SEL, V_SEL + 1, V_WIN, V_WIN + 1)
                        for q in range(QT):
                            for a, t in enumerate(vt):
                                last = tr(pt[q][:, a * P:(a + 1) * P], kvT[:, t, q * P:(q + 1) * P], ident[:])
                            last.then_inc(pre_tr, 1)
                        for a, t in enumerate(vt):
                            last = tr(pt[2][0:DB, a * P:(a + 1) * P], kvT[:, t, SEQ:T], ident[:])
                        last.then_inc(pre_tr, 1)
                        for q in range(QT):
                            last = tr(pt[3][:, q * 48:(q + 1) * 48], gT_[:, q * P:(q + 1) * P], ident[0:48, 0:48])
                        last.then_inc(pre_tr, 1)
                        pe.wait_ge(kc_ok, 1)
                        for i in range(KD):
                            for half in range(2):
                                r, h = slice(64 * half, 64 * half + 64), 8 * (i // 4) + i % 4 + 4 * half
                                for q in range(QT):
                                    last = mm(pt[4 + half][:, (q * AH + h) * 4:(q * AH + h) * 4 + 4], qT[r, i, q * P:(q + 1) * P], kc[r, i // 4, :], start=True, stop=True)
                        last.then_inc(csc, 1)
                        pe.wait_ge(kc_ok, 2)
                        pe.wait_ge(pre_tk, 1)
                        for i in range(KD):
                            last = tr(pt[6 * (i // 4)][0:64, (i % 4) * P:(i % 4 + 1) * P], vx[:, i * 64:(i + 1) * 64], ident[:])
                        last.then_inc(pre_tr, 1)
                        pe.wait_ge(pc_ok, 1)
                        for q in range(QT):
                            last = tr(pt[7][0:64, q * P:(q + 1) * P], pc[:, q].rearrange("p h n -> p (h n)"), ident[:])
                        last.then_inc(pc_tr, 1)
                        pe.wait_ge(pct_ok, 1)
                        pe.wait_ge(pre_tk, 5)

                        def score(u):
                            i, lo, v, h, kv = unit(u)
                            if u >= 2:
                                pe.wait_ge(soft_done, 2 * (u - 1))
                            r, kt = slice(lo, lo + 64), (K_WIN if v else K_SEL) + i // 4
                            mm(pt[u % 2][:, 0:P], qT[r, i, 0:P], kvT[r, kt, 0:P], start=True, stop=True)
                            mm(pt[u % 2][:, P:3 * P], qT[r, i, P:SEQ], kvT[r, kt, 0:SEQ], start=True, stop=True).then_inc(score_done, 1)

                        def turn(u):
                            pe.wait_ge(scaled, 2 * u + 2)
                            if u >= 2:
                                pe.wait_ge(pts_ok, u - 1)
                            for a in range(3):
                                last = tr(pt[2 + u % 2][:, a * P:(a + 1) * P], sbuf[:, u % 3, a * P:(a + 1) * P], ident[:])
                            last.then_inc(tr_ok, 1)

                        def values(u):
                            i, lo, v, h, kv = unit(u)
                            ob = pt[4 + i % 2]
                            if u % 4 == 0:
                                if i >= 2:
                                    pe.wait_ge(ot_ok, i - 1)
                                mm(ob[:, 0:SEQ], vci[:, i, :], pct[:], start=True, stop=False, skip_group_check=True)
                            pe.wait_ge(pts_ok, u + 1)
                            vw = slice(v * 256 + kv * 64, v * 256 + kv * 64 + 64)
                            mm(ob[lo:lo + 64, 0:SEQ], vtok[:, 0, vw], pts[:, u % 2, 0:SEQ], start=False, stop=False, skip_group_check=True)
                            mm(ob[lo:lo + 64, P:SEQ], vtok[:, 1, vw], pts[:, u % 2, SEQ:3 * P], start=False, stop=u % 4 >= 1, skip_group_check=True).then_inc(pv_ok, 1)

                        score(0)
                        score(1)
                        for u in range(NU):
                            turn(u)
                            if u + 2 < NU:
                                score(u + 2)
                            if u >= 1:
                                values(u - 1)
                        values(NU - 1)

                    @block.scalar
                    def _(act):
                        A_ = nc.scalar.activation
                        act.wait_ge(pos_d, 1)
                        A_(wb[:], wb[:], ACT.Exp).then_inc(pos_a, 1)
                        act.wait_ge(cexp_in, 1)
                        A_(pc[:], pc[:], ACT.Exp).then_inc(cexp, 1)

                        def exps(u):
                            act.wait_ge(soft_done, 2 * u + 2)
                            if u >= 3:
                                act.wait_ge(wgt_ok, u - 2)
                            s = sbuf[:, u % 3, :]
                            A_(s[:, 0:P], s[:, 0:P], ACT.Exp, bias=nm[:, u % 3, 0:1], accum_out=sm[:, u % 3, 0:1]).then_inc(ex_done, 1)
                            A_(s[:, P:3 * P], s[:, P:3 * P], ACT.Exp, bias=nm[:, u % 3, 1:2], accum_out=sm[:, u % 3, 1:2]).then_inc(ex_done, 1)

                        exps(0)
                        for u in range(NU):
                            if u + 1 < NU:
                                exps(u + 1)
                            act.wait_ge(tr_ok, u + 1)
                            if u >= 2:
                                act.wait_ge(pv_ok, u - 1)
                            A_(pts[:, u % 2, :], pt[2 + u % 2][:, 0:3 * P], ACT.Copy).then_inc(pts_ok, 1)

                    @block.vector
                    def _(dve):
                        V = nc.vector
                        dve.wait_ge(ld_ptab, 32)
                        dve_step(dve, V.tensor_reduce(wst[:], wb[:], AX.X, ALU.max))
                        V.tensor_tensor(wb[:], wb[:], wst[:].unsqueeze(2).to_broadcast([P, 4, BLK]), ALU.subtract).then_inc(pos_d, 1)
                        dve.wait_ge(pos_a, 1)
                        dve_step(dve, V.tensor_reduce(wst[:], wb[:], AX.X, ALU.add))
                        dve_step(dve, V.reciprocal(wst[:], wst[:]))
                        dve_step(dve, V.tensor_tensor(wb[:], wb[:], wst[:].unsqueeze(2).to_broadcast([P, 4, BLK]), ALU.mult))
                        for a in range(4):
                            i1 = V.tensor_tensor(ctmp[:, a, :].rearrange("p (n l) -> p n l", l=BLK), kvT[:, a, 0:SEQ].rearrange("p (n l) -> p n l", l=BLK),
                                                 wb[:, a:a + 1, :].to_broadcast([P, 4, BLK]), ALU.mult)
                        dve_step(dve, i1)
                        V.tensor_reduce(kc[:].rearrange("p a n -> p (a n)"), ctmp[:].rearrange("p a (n l) -> p (a n) l", l=BLK), AX.X, ALU.add).then_inc(kc_ok, 1)
                        dve_step(dve, V.memset(vx[:], 0.0))
                        dve.wait_ge(kc_ok, 1)
                        for p in range(2):
                            for half in range(2):
                                r, base = slice(64 * half, 64 * half + 64), 288 * p + 16 * half
                                i1 = V.tensor_copy(vx[r, base:base + 272].rearrange("q (r c) -> q r c", c=68)[:, :, 0:4],
                                                   kc[r, 2 + p:3 + p, :].to_broadcast([64, 4, 4]))
                        i1.then_inc(kc_ok, 1)
                        for q in range(QT):
                            dve.wait_ge(pre_tr, q + 1)
                            V.tensor_copy(vtok[:, q, :], pt[q][:]).then_inc(pre_tk, 1)
                        dve.wait_ge(pre_tr, 3)
                        V.tensor_copy(vnew[:], pt[2][0:DB, :]).then_inc(pre_tk, 1)
                        dve.wait_ge(pre_tr, 4)
                        dve_step(dve, V.tensor_copy(gtok[:], pt[3][:, 0:96].rearrange("p (q c) -> p q c", q=QT)))
                        dve.wait_ge(csc, 1)
                        dve.wait_ge(ld_ac, 48)
                        f = lambda t: t[:].rearrange("p q h n -> p (q h) n")
                        g = lambda t: t[:].rearrange("p q h -> p (q h)")
                        bc = g(pst).unsqueeze(2).to_broadcast([P, QT * AH, 4])
                        e = lambda t, half: t.rearrange("p (a f c) -> p a f c", f=2, c=16)[:, :, half, :]
                        w = lambda t: t[:].rearrange("p q h n -> p (q h n)")
                        V.tensor_tensor(e(w(pc), 0), e(pt[4][:, 0:QT * AH * 4], 0), e(w(cbias), 0), ALU.add)
                        dve_step(dve, V.tensor_tensor(e(w(pc), 1), e(pt[5][:, 0:QT * AH * 4], 1), e(w(cbias), 1), ALU.add))
                        dve_step(dve, V.tensor_reduce(g(pst), f(pc), AX.X, ALU.max))
                        V.tensor_tensor(f(pc), f(pc), bc, ALU.subtract).then_inc(cexp_in, 1)
                        dve.wait_ge(cexp, 1)
                        dve_step(dve, V.tensor_tensor(f(pc), f(pc), f(cmask), ALU.mult))
                        dve_step(dve, V.tensor_reduce(g(pst), f(pc), AX.X, ALU.add))
                        dve_step(dve, V.tensor_scalar(g(pst), g(pst), 1e-30, None, ALU.max))
                        dve_step(dve, V.reciprocal(g(pst), g(pst)))
                        g3 = gtok[:].rearrange("p q (h c) -> p q h c", c=3)
                        dve_step(dve, V.tensor_tensor(pst[:], pst[:], g3[:, :, :, 0], ALU.mult))
                        V.tensor_tensor(f(pc), f(pc), bc, ALU.mult).then_inc(pc_ok, 1)
                        dve.wait_ge(pre_tr, 5)
                        for a in range(2):
                            i1 = V.tensor_copy(vci[:, 4 * a:4 * a + 4, :], pt[6 * a][0:64, :].rearrange("p (i m) -> p i m", i=4))
                        i1.then_inc(pre_tk, 1)
                        dve.wait_ge(pc_tr, 1)
                        V.tensor_copy(pct[:], pt[7][0:64, 0:SEQ]).then_inc(pre_tk, 1)
                        dve.wait_ge(pre_tk, 5)
                        dve_step(dve, V.memset(wgt[:], 0.0))
                        V.tensor_copy(nm[:], wgt[:]).then_inc(pct_ok, 1)
                        dve.wait_ge(pct_ok, 1)

                        def soft(u):
                            i, lo, v, h, kv = unit(u)
                            dve.wait_ge(score_done, u + 1)
                            if u >= 3:
                                dve.wait_ge(tr_ok, u - 2)
                            s = sbuf[:, u % 3, :]
                            dve_step(dve, V.scalar_tensor_tensor(s, dm[:], -2.0 ** (-8.0 * (h + 1) / AH), pt[u % 2][:, 0:3 * P], ALU.mult, ALU.add))
                            V.tensor_reduce(nm[:, u % 3, 0:1], s[:, 0:P], AX.X, ALU.max, negate=True).then_inc(soft_done, 1)
                            V.tensor_reduce(nm[:, u % 3, 1:2], s[:, P:3 * P], AX.X, ALU.max, negate=True).then_inc(soft_done, 1)

                        def scale(u):
                            i, lo, v, h, kv = unit(u)
                            dve.wait_ge(ex_done, 2 * u + 2)
                            if u >= 3:
                                dve.wait_ge(scaled, 2 * (u - 2))
                            dve_step(dve, V.reciprocal(wgt[:, u % 3, :], sm[:, u % 3, :]))
                            V.tensor_tensor(wgt[:, u % 3, :], wgt[:, u % 3, :], g3[:, :, h, 1 + v], ALU.mult).then_inc(wgt_ok, 1)

                        def out_tile(i):
                            dve.wait_ge(pv_ok, 4 * i + 4)
                            V.tensor_copy(oT[:, i, 0:SEQ], pt[4 + i % 2][:, 0:SEQ]).then_inc(ot_ok, 1)

                        soft(0)
                        for u in range(NU):
                            if u + 1 < NU:
                                soft(u + 1)
                            scale(u)
                            if u >= 5 and (u - 5) % 4 == 0:
                                out_tile((u - 5) // 4)
                        out_tile(KD - 1)

            with ExitStack() as st:
                cpg = st.enter_context(nc.sbuf_tensor("cmp_pages", [P, 2, NPG, 4, PAGE], F32))
                pv = [st.enter_context(nc.psum_tensor(f"vc{i}", [P, 512], F32)) for i in range(4)]
                ld_c, c_used, c_tr = [sem("c_ld0"), sem("c_ld1")], sem("c_used"), sem("c_tr")
                with nc.Block() as block:
                    @block.sync
                    def _(sp):
                        sp.wait_ge(ld_ptab, 32)
                        for b in range(DB):
                            if b >= 2:
                                sp.wait_ge(c_used, b - 1)
                            for n in range(NPG):
                                page = sp.value_load(ptab[0:1, b * NPG + n:b * NPG + n + 1], min_val=0, max_val=I["cmp_pages"].shape[0] - 1)
                                sp.dma_start(cpg[:, b % 2, n], I["cmp_pages"][bass.ds(page, 1)].rearrange("a p c t -> (a p) c t")).then_inc(ld_c[b % 2], 16)

                    @block.vector
                    def _(dve):
                        V = nc.vector
                        for b in range(DB):
                            dve.wait_ge(ld_c[b % 2], 16 * NPG * (b // 2 + 1))
                            for a in range(4):
                                x = cpg[:, b % 2, :, a, :].rearrange("p n (c l) -> p n c l", l=BLK)
                                i1 = V.tensor_tensor(x, x, wb[:, a:a + 1, :].unsqueeze(1).to_broadcast([P, NPG, 2, BLK]), ALU.mult)
                            dve_step(dve, i1)
                            for a in range(4):
                                x = cpg[:, b % 2, :, a, :].rearrange("p n (c l) -> p n c l", l=BLK)
                                i1 = V.tensor_reduce(kcd[:, a, b, :].rearrange("p (n c) -> p n c", c=2), x, AX.X, ALU.add)
                            i1.then_inc(c_used, 1)
                        dve.wait_ge(c_tr, 1)
                        for n in range(4):
                            V.tensor_copy(vcd[:, 2 * n:2 * n + 2, :].rearrange("p b d -> p (b d)"), pv[n][0:NBP, :])

                    @block.tensor
                    def _(pe):
                        pe.wait_ge(c_used, DB)
                        for b in range(DB):
                            for p in range(2):
                                last = nc.tensor.transpose(pv[b // 2][0:NBP, ((b % 2) * 2 + p) * P:((b % 2) * 2 + p + 1) * P], kcd[:, 2 + p, b, :], ident[:])
                        last.then_inc(c_tr, 1)

            with ExitStack() as st:
                def sb2(name, shape, dt=F32):
                    return st.enter_context(nc.sbuf_tensor(name, shape, dt))

                qbd = ring[:, 1, 2 * CH:2 * CH + 2 * DB * 144].rearrange("p (a c) -> p a c", a=2)
                kvb = sb2("kv_ring", [P, 2, 3072])
                biasd, biasw, cbd, g4, idx, mb = (sb2(n, s) for n, s in (("bias_dec", [P, PAST]), ("bias_win", [P, WIN]), ("bias_cmp", [P, NBP]),
                                                                       ("same_group", [P, P]), ("block_idx", [P, NBP]), ("batch_mask", [P, DB])))
                gmask, gsel = sb2("gate_mask", [48, AH]), sb2("gate_sel", [48, 3])
                gl = sb2("gate_spread", [48, DB, AH])
                gd = sb2("gate_dec", [P, 3])
                ss, sw = sb2("s_sel", [P, PAST + 1]), sb2("s_win", [P, WIN + 1])
                sc, pcn, nb, tmp = sb2("s_cmp", [P, NBP]), sb2("p_cmp", [P, NBP]), sb2("block_bias", [P, NBP]), sb2("imp_tmp", [P, NBP])
                nmx, sums, rcp, ex_ = sb2("d_negmax", [P, 3]), sb2("d_sum", [P, 3]), sb2("d_rcp", [P, 3]), sb2("excluded", [P, 2])
                pnd = sb2("p_new_diag", [P, 2, DB])
                ptd = sb2("d_probs_T", [P, 12, P])
                pcd, pnt = sb2("d_pcmp_T", [NBP, P]), sb2("d_pnew_T", [DB, 2, P])
                pt = [st.enter_context(nc.psum_tensor(f"dt{i}", [P, 512], F32)) for i in range(8)]
                ld_dc, kv_used, q_zero, q_ok, gl_ok, s_all, imp_in, imp_ok, to_exp, exped, p_ok, t_ok, t_taken = (
                    sem("d_" + n) for n in ("ldc", "kv_used", "q_zero", "q_ok", "gl", "s_all", "imp_in", "imp", "to_exp", "exped", "p", "t", "tk"))
                ld_kv = [sem("d_ldkv0"), sem("d_ldkv1")]

                with nc.Block() as block:
                    @block.sync
                    def _(sp):
                        cl = (("bias_dec", biasd), ("bias_win", biasw), ("bias_cmp", cbd), ("same_group", g4), ("block_idx", idx), ("batch_mask", mb),
                              ("gate_mask", gmask), ("gate_sel", gsel))
                        for n, (name, dst) in enumerate(cl):
                            sp.dma_start(dst[:], I[name]).then_inc(ld_dc, 16)
                        for n in range(2 * DB):
                            b, s = n % DB, n % 2
                            if n >= 2:
                                sp.wait_ge(kv_used, n - 1)
                            for g in range(NPG):
                                page = sp.value_load(ptab[0:1, b * NPG + g:b * NPG + g + 1], min_val=0, max_val=I["cmp_pages"].shape[0] - 1)
                                src = I["ksel_pages" if n < DB else "vsel_pages"][bass.ds(page, 1)].rearrange("a p c -> (a p) c")
                                sp.dma_start(kvb[:, s, g * 256:(g + 1) * 256], src).then_inc(ld_kv[s], 16)
                            src = I["kwin"][b] if n < DB else I["vwin"][b]
                            sp.dma_start(kvb[:, s, 2048:3072].rearrange("p (a c) -> p a c", a=src.shape[1]), src).then_inc(ld_kv[s], 16)

                    @block.gpsimd
                    def _(pool):
                        nc.gpsimd.memset(qbd, 0.0).then_inc(q_zero, 1)

                    @block.tensor
                    def _(pe):
                        tr, mm = nc.tensor.transpose, nc.tensor.matmul
                        pe.wait_ge(q_ok, 1)
                        for b in range(DB):
                            pe.wait_ge(ld_kv[b % 2], 16 * (NPG + 1) * (b // 2 + 1))
                            k3 = kvb[:, b % 2, 0:2048].rearrange("p (g c t) -> p g c t", g=NPG, c=2)
                            kw = kvb[:, b % 2, 2048:3072].rearrange("p (c t) -> p c t", c=2)
                            for p in range(2):
                                q = qbd[:, p, b * P:(b + 1) * P]
                                st_, sp_ = b == 0 and p == 0, b == DB - 1 and p == 1
                                for a in range(2):
                                    mm(pt[a][:], q, k3[:, 4 * a:4 * a + 4, p, :], start=st_, stop=sp_)
                                last = mm(pt[2][:], q, kw[:, p, :], start=st_, stop=sp_)
                            last.then_inc(kv_used, 1)
                        for col, n, key in ((0, 1, lambda b, p: kvT[:, K_SEL + p, SEQ + b:SEQ + b + 1]), (1, 1, lambda b, p: kvT[:, K_WIN + p, SEQ + b:SEQ + b + 1]),
                                            (2, NBP, lambda b, p: kcd[:, p, b, :])):
                            for b in range(DB):
                                for p in range(2):
                                    mm(pt[3][:, col:col + n], qbd[:, p, b * P:(b + 1) * P], key(b, p), start=b == 0 and p == 0, stop=b == DB - 1 and p == 1)
                        pe.wait_ge(gl_ok, 1)
                        mm(pt[3][:, 18:21], gl[:].rearrange("k b h -> k (b h)"), gsel[:], start=True, stop=True).then_inc(s_all, 1)
                        pe.wait_ge(imp_in, 1)
                        mm(pt[4][:, 0:NBP], g4[:], pcn[:], start=True, stop=True).then_inc(imp_ok, 1)
                        pe.wait_ge(p_ok, 3)
                        for a in range(8):
                            last = tr(pt[5 * (a // 4)][:, (a % 4) * P:(a % 4 + 1) * P], ss[:, a * P:(a + 1) * P], ident[:])
                        for a in range(4):
                            last = tr(pt[1][:, a * P:(a + 1) * P], sw[:, a * P:(a + 1) * P], ident[:])
                        tr(pt[2][0:NBP, 0:P], sc[:], ident[:])
                        tr(pt[2][0:DB, P:2 * P], pnd[:, 0, :], ident[:])
                        tr(pt[2][0:DB, 2 * P:3 * P], pnd[:, 1, :], ident[:]).then_inc(t_ok, 1)
                        pe.wait_ge(t_taken, 1)
                        for p in range(2):
                            for v in range(2):
                                mm(pt[6 + p][:, 0:P], vnew[:, v * 256 + p * P:v * 256 + (p + 1) * P], pnt[:, v, :], start=v == 0, stop=False, skip_group_check=True)
                        for b in range(DB):
                            n = DB + b
                            pe.wait_ge(ld_kv[n % 2], 16 * (NPG + 1) * (n // 2 + 1))
                            v3 = kvb[:, n % 2, :].rearrange("p (g c) -> p g c", c=256)
                            for p in range(2):
                                cols = slice(b * AH + 8 * p, b * AH + 8 * p + 8)
                                mm(pt[6 + p][:, cols], vcd[:, b, p * P:(p + 1) * P], pcd[:, cols], start=False, stop=False, skip_group_check=True)
                                for g in range(12):
                                    last = mm(pt[6 + p][:, cols], v3[:, g, p * P:(p + 1) * P], ptd[:, g, cols], start=False, stop=g == 11, skip_group_check=True)
                            last.then_inc(kv_used, 1)

                    @block.scalar
                    def _(act):
                        A_ = nc.scalar.activation
                        act.wait_ge(to_exp, 1)
                        A_(sc[:], sc[:], ACT.Exp, bias=nmx[:, 0:1], accum_out=sums[:, 0:1]).then_inc(exped, 1)
                        act.wait_ge(to_exp, 2)
                        A_(sw[:], sw[:], ACT.Exp, bias=nmx[:, 2:3], accum_out=sums[:, 2:3]).then_inc(exped, 1)
                        act.wait_ge(to_exp, 3)
                        A_(ss[:], ss[:], ACT.Exp, bias=nmx[:, 1:2], accum_out=sums[:, 1:2]).then_inc(exped, 1)

                    @block.vector
                    def _(dve):
                        V = nc.vector
                        dve.wait_ge(q_zero, 1)
                        for p in range(2):
                            for half in range(2):
                                r = slice(64 * half, 64 * half + 64)
                                i1 = V.tensor_copy(qbd[r, p, :].rearrange("q (b c) -> q b c", c=144)[:, :, 8 * p + 4 * half:8 * p + 4 * half + 4],
                                                   qT[r, 4 * p:4 * p + 4, SEQ:T].rearrange("q r b -> q b r"))
                        i1.then_inc(q_ok, 1)
                        dve.wait_ge(ld_dc, 16 * 8)
                        V.tensor_tensor(gl[:], gT_[:, SEQ:T].unsqueeze(2).to_broadcast([48, DB, AH]), gmask[:].unsqueeze(1).to_broadcast([48, DB, AH]), ALU.mult).then_inc(gl_ok, 1)
                        dve.wait_ge(s_all, 1)
                        V.tensor_copy(gd[:], pt[3][:, 18:21])
                        dve_step(dve, V.tensor_tensor(sc[:], pt[3][:, 2:2 + NBP], cbd[:], ALU.add))
                        V.tensor_reduce(nmx[:, 0:1], sc[:], AX.X, ALU.max, negate=True).then_inc(to_exp, 1)
                        V.tensor_tensor(sw[:, 0:WIN], pt[2][:], biasw[:], ALU.add)
                        dve_step(dve, V.tensor_copy(sw[:, WIN:WIN + 1], pt[3][:, 1:2]))
                        V.tensor_reduce(nmx[:, 2:3], sw[:], AX.X, ALU.max, negate=True).then_inc(to_exp, 1)
                        V.tensor_copy(ss[:, PAST:PAST + 1], pt[3][:, 0:1])
                        V.tensor_tensor(ss[:, 0:512], pt[0][:], biasd[:, 0:512], ALU.add)
                        dve_step(dve, V.tensor_tensor(ss[:, 512:PAST], pt[1][:], biasd[:, 512:PAST], ALU.add))
                        dve.wait_ge(exped, 1)
                        dve_step(dve, V.reciprocal(rcp[:, 0:1], sums[:, 0:1]))
                        V.tensor_scalar(pcn[:], sc[:], rcp[:, 0:1], None, ALU.mult).then_inc(imp_in, 1)
                        dve.wait_ge(imp_in, 1)
                        V.tensor_scalar(sc[:], pcn[:], gd[:, 0:1], None, ALU.mult).then_inc(p_ok, 1)
                        dve.wait_ge(imp_ok, 1)
                        dve_step(dve, V.tensor_copy(tmp[:], pt[4][:, 0:NBP]))
                        dve_step(dve, V.tensor_reduce(ex_[:, 0:1], tmp[:, 1:NBP], AX.X, ALU.min))
                        dve_step(dve, V.tensor_scalar(nb[:], tmp[:], ex_[:, 0:1], None, ALU.is_equal))
                        dve_step(dve, V.tensor_tensor(nb[:], nb[:], idx[:], ALU.mult))
                        dve_step(dve, V.tensor_reduce(ex_[:, 1:2], nb[:, 1:NBP], AX.X, ALU.max))
                        dve_step(dve, V.tensor_scalar(nb[:], idx[:], ex_[:, 1:2], NEG, ALU.is_equal, ALU.mult))
                        s3 = ss[:, 0:PAST].rearrange("p (n l) -> p n l", l=BLK)
                        dve_step(dve, V.tensor_tensor(s3, s3, nb[:].unsqueeze(2).to_broadcast([P, NBP, BLK]), ALU.add))
                        V.tensor_reduce(nmx[:, 1:2], ss[:], AX.X, ALU.max, negate=True).then_inc(to_exp, 1)
                        for n, (x, v) in enumerate(((sw, 2), (ss, 1))):
                            dve.wait_ge(exped, 2 + n)
                            dve_step(dve, V.reciprocal(rcp[:, v:v + 1], sums[:, v:v + 1]))
                            dve_step(dve, V.tensor_tensor(rcp[:, v:v + 1], rcp[:, v:v + 1], gd[:, v:v + 1], ALU.mult))
                            dve_step(dve, V.tensor_scalar(x[:], x[:], rcp[:, v:v + 1], None, ALU.mult))
                            V.tensor_scalar(pnd[:, v - 1, :], mb[:], x[:, x.shape[1] - 1:x.shape[1]], None, ALU.mult).then_inc(p_ok, 1)
                        dve.wait_ge(t_ok, 1)
                        V.tensor_copy(ptd[:, 0:4, :], pt[0][:].rearrange("p (a c) -> p a c", a=4))
                        V.tensor_copy(ptd[:, 4:8, :], pt[5][:].rearrange("p (a c) -> p a c", a=4))
                        V.tensor_copy(ptd[:, 8:12, :], pt[1][:].rearrange("p (a c) -> p a c", a=4))
                        V.tensor_copy(pcd[:], pt[2][0:NBP, 0:P])
                        V.tensor_copy(pnt[:], pt[2][0:DB, P:3 * P].rearrange("p (a c) -> p a c", a=2)).then_inc(t_taken, 1)
                        dve.wait_ge(kv_used, 2 * DB)
                        for p in range(2):
                            for half in range(2):
                                r = slice(64 * half, 64 * half + 64)
                                V.tensor_copy(oT[r, 4 * p:4 * p + 4, SEQ:T],
                                              pt[6 + p][r, 0:P].rearrange("q (b c) -> q b c", c=AH)[:, :, 8 * p + 4 * half:8 * p + 4 * half + 4].rearrange("q b r -> q r b"))

            with ExitStack() as st:
                bank = [st.enter_context(nc.psum_tensor(f"no{i}", [P, 512], F32)) for i in range(4)]
                o_done, o_taken = sem("no_done"), sem("no_taken")
                base = [16 * c for c in chunk_count]
                with nc.Block() as block:
                    @block.tensor
                    def _(pe):
                        for m in range(KD):
                            if m % 4 == 0:
                                pe.wait_ge(ld_chunk[m // 4], base[m // 4] + 16)
                            if m >= 4:
                                pe.wait_ge(o_taken, m - 3)
                            wc = chunk[m // 4].rearrange("p (k n) -> p k n", k=KD)
                            for k in range(KD):
                                last = nc.tensor.matmul(bank[m % 4][:, 0:T], wc[:, k, (m % 4) * P:(m % 4 + 1) * P], oT[:, k, :], start=k == 0, stop=k == KD - 1)
                            last.then_inc(o_done, 1)

                    @block.vector
                    def _(dve):
                        for m in range(KD):
                            dve.wait_ge(o_done, m + 1)
                            nc.vector.scalar_tensor_tensor(xT[:, m, :], xT[:, m, :], ALPHA, bank[m % 4][:, 0:T], ALU.mult, ALU.add).then_inc(o_taken, 1)

                    @block.sync
                    def _(sp):
                        sp.wait_ge(stored, n_stored[0])
                for c in range(2):
                    chunk_count[c] += 1

        tail(1, out=O["y"])
        with nc.Block() as block:
            @block.sync
            def _(sp):
                sp.wait_ge(stored, n_stored[0])


def consts():
    c = {}
    r = np.arange(P)
    c["ident"] = np.eye(P, dtype=np.float32)
    c["ones"] = np.ones((P, P), np.float32)
    tri = (r[:, None] <= r[None, :]).astype(np.float32)
    c["m384"] = np.concatenate([tri, c["ones"], tri], 1)
    c["eps"] = np.full((P, 1), EPS, np.float32)
    i4 = np.arange(EG)
    c["lower4"] = np.ascontiguousarray(np.broadcast_to((i4[None, :] < i4[:, None]).astype(np.float32), (P, EG, EG)))
    c["hsel"] = np.repeat(np.eye(NH, dtype=np.float32), HD, axis=1)
    slope = 2.0 ** (-8.0 * np.arange(1, AH + 1) / AH)
    f32 = lambda a: np.ascontiguousarray(a, np.float32)
    far = lambda d: np.where(d >= 0, d, 1e33)
    c["dist_masked"] = f32(np.concatenate([far(r[:, None] - r[None, :]), far(P + r[:, None] - np.arange(SEQ)[None, :])], 1))
    d = (np.arange(QT)[None, :, None] * P + r[:, None, None] - ((np.arange(4) + 1) * BLK - 1)).astype(float)[:, :, None, :]
    c["cmp_mask"] = f32(np.broadcast_to(d >= 0, (P, QT, AH, 4)))
    c["cmp_bias"] = f32(np.where(d >= 0, -slope[None, None, :, None] * d, NEG))
    sl = slope[r % AH][:, None]
    pos = np.arange(PAST)[None, :]
    c["bias_dec"] = f32(-sl * (PAST - pos))
    c["bias_win"] = f32(np.where(np.arange(WIN) >= 1, -sl * (WIN - np.arange(WIN)), NEG))
    c["bias_cmp"] = f32(-sl * (PAST - ((np.arange(NBP) + 1) * BLK - 1)))
    c["same_group"] = f32(r[:, None] // REP == r[None, :] // REP)
    c["block_idx"] = f32(np.broadcast_to(np.arange(NBP), (P, NBP)))
    c["batch_mask"] = f32(r[:, None] // AH == np.arange(DB))
    k = np.arange(3 * AH)[:, None]
    c["gate_mask"], c["gate_sel"] = f32(k // 3 == np.arange(AH)), f32(k % 3 == np.arange(3))
    return c


def kernel(x_prompt, x_sample, state_ssm, state_conv, cache_kv, cache_win, page_table, p_prompt, p_sample,
           ssd_w_in, ssd_conv_w, ssd_conv_b, ssd_dt_bias, ssd_a_log, ssd_d, ssd_norm_g, ssd_w_out,
           nsa_w_in, nsa_pos_w, nsa_w_out, ln1_g, ln1_b, ln2_g, ln2_b, router_w, router_bias,
           moe_w_gate, moe_w_up, moe_w_down, ple_proj, ple_gate):
    import concourse.bacc as bacc
    from concourse.bass_utils import run_bass_kernel_spmd

    A = lambda a: np.asarray(a)
    tiles = lambda a: np.moveaxis(A(a).reshape(-1, P, *A(a).shape[1:]), 0, 1)
    cc = np.ascontiguousarray
    ins = consts()
    ins["xT"] = cc(np.concatenate([A(x_prompt)[0], A(x_sample)[:, 0]], 0).T)
    ins["pT"] = cc(np.concatenate([A(p_prompt)[:, 0], A(p_sample)[:, :, 0]], 1).transpose(0, 2, 1))
    ins["state_ssm"] = A(state_ssm)[0].reshape(DB, DI, NS)
    ins["conv_state"] = cc(tiles(A(state_conv)[0].transpose(2, 1, 0)))
    ins["conv_params"] = cc(tiles(np.concatenate([A(ssd_conv_w)[0], A(ssd_conv_b)], 0).T))
    ins["heads"] = cc(np.stack([A(ssd_dt_bias)[0], A(ssd_a_log)[0], A(ssd_d)[0]], 1))
    ins["norm_g"] = cc(tiles(A(ssd_norm_g)[0]))
    ins["lnp"] = cc(np.stack([A(ln1_g), A(ln1_b), A(ln2_g), A(ln2_b)], 1).reshape(2, 4, KD, P).transpose(3, 0, 1, 2))
    ins["router_w"] = cc(tiles(router_w))
    ins["router_bias"] = cc(np.broadcast_to(A(router_bias), (P, NE)))
    ins["ssd_w_in"], ins["ssd_w_out"] = A(ssd_w_in)[0], A(ssd_w_out)[0]
    for n, w in (("moe_w_gate", moe_w_gate), ("moe_w_up", moe_w_up), ("moe_w_down", moe_w_down)):
        ins[n] = A(w).reshape(2 * NE, *w.shape[2:])
    ins["ple_proj"], ins["ple_gate"] = A(ple_proj), A(ple_gate)
    order = [8 * (i // 4) + i % 4 + 4 * half for i in range(KD) for half in range(2)]
    cols = np.concatenate([np.arange(h * 64, h * 64 + 64) for h in order])
    w = A(nsa_w_in)[0]
    ins["nsa_w_in"] = np.concatenate([w[:, cols], w[:, D:]], 1)
    ins["nsa_w_out"] = A(nsa_w_out)[0][cols]
    pw = A(nsa_pos_w)[0].transpose(0, 2, 1).reshape(4, 2, BLK)
    ins["pos_w"] = cc(np.repeat(pw.transpose(1, 0, 2), 64, axis=0))
    ins["page_table"] = A(page_table).reshape(1, -1)
    kv = A(cache_kv)[0].reshape(-1, PAGE, 4, 256)
    ins["cmp_pages"] = cc(kv[:, :, 0:2].reshape(-1, PAGE, 4, P).transpose(0, 3, 2, 1))
    ins["ksel_pages"] = cc(kv[:, :, 2].reshape(-1, PAGE, 2, P).transpose(0, 3, 2, 1)).reshape(-1, P, 256)
    ins["vsel_pages"] = cc(kv[:, :, 3])
    cw = A(cache_win)[0].reshape(DB, WIN, 2, 256)
    ins["kwin"] = cc(cw[:, :, 0].reshape(DB, WIN, 2, P).transpose(0, 3, 2, 1))
    ins["vwin"] = cc(cw[:, :, 1].reshape(DB, 4, P, 256).transpose(0, 2, 1, 3))
    ins["cache_win"] = cw.reshape(DB, WIN, 512)

    outs = {"conv_prompt": (P, JC, 3), "conv_sample": (P, JC, 3, DB), "ssm_prompt": (DI, NS), "ssm_sample": (DB, DI, NS), "y": (P, KD, T)}
    outs |= {"kv": (P, KVT, T), "win_old": (DB, WIN - 1, 512)}
    nc = bacc.Bacc("TRN2", target_bir_lowering=False, num_devices=1)
    I = {n: nc.dram_tensor("in_" + n, a.shape, mybir.dt.from_np(a.dtype), kind="ExternalInput").ap() for n, a in ins.items()}
    O = {n: nc.dram_tensor("out_" + n, s, F32, kind="ExternalOutput").ap() for n, s in outs.items()}
    trunk(nc, I, O)
    r = run_bass_kernel_spmd(nc, [{"in_" + n: a for n, a in ins.items()}], core_ids=[0]).results[0]
    o = {n: A(r["out_" + n]) for n in outs}
    feat = lambda a: np.moveaxis(a, 1, 0).reshape(-1, *a.shape[2:])
    y = feat(o["y"]).T
    conv_p = feat(o["conv_prompt"]).T[None, None]
    conv_s = feat(o["conv_sample"]).transpose(2, 1, 0)[None]
    ssm_p = o["ssm_prompt"].reshape(1, 1, NH, HD, NS)
    ssm_s = o["ssm_sample"].reshape(1, DB, NH, HD, NS)
    kvo = feat(o["kv"]).T.reshape(T, 6, AKV, 64)
    win_s = np.concatenate([o["win_old"].reshape(DB, WIN - 1, 2, AKV, 64), kvo[SEQ:, None, 4:6]], 1)
    return (y[None, :SEQ], y[SEQ:, None], ssm_p, conv_p, kvo[None, None, :SEQ, 0:4], kvo[None, None, :SEQ, 4:6],
            ssm_s, conv_s, kvo[None, SEQ:, None, 0:4], win_s[None])
```

```python
from contextlib import ExitStack

import numpy as np

import concourse.bass as bass
from concourse import mybir

F32 = mybir.dt.float32
I32 = mybir.dt.int32
ALU = mybir.AluOpType
ACT = mybir.ActivationFunctionType
AX = mybir.AxisListType

P = 128
D = 1024
KD = D // P
SEQ = 256
DB = 8
T = SEQ + DB
QT = SEQ // P
DI, HD, NH, NG, NS, NCONV = 2048, 64, 32, 4, 128, 4
CD = DI + 2 * NG * NS
JX = DI // P
JC = CD // P
AH, AKV, REP, BLK, WIN, PAST, PAGE = 16, 4, 4, 64, 512, 1024, 128
NPG = PAST // PAGE
NBP = PAST // BLK
QS = 64 ** -0.5
KVT = 6 * AKV * 64 // P
NE, FF, EG = 16, 512, 4
CH = 4096
ALPHA = 4.0 ** 0.25
EPS = 1e-5
NEG = -1e30


class Chain:

    def __init__(self, sem):
        self.sem, self.n = sem, 0

    def __call__(self, eng, ins):
        self.n += 1
        ins.then_inc(self.sem, 1)
        eng.wait_ge(self.sem, self.n)


def trunk(nc, I, O):
    root = ExitStack()
    with root:
        def sem(name):
            return root.enter_context(nc.semaphore(name))

        def keep(name, shape, dt=F32):
            return root.enter_context(nc.sbuf_tensor(name, shape, dt))

        ring = keep("expert_ring", [P, 2, 3 * CH])
        xT = keep("xT", [P, KD, T])
        ident = keep("ident", [P, P])
        ones = keep("ones", [P, P])
        m384 = keep("m384", [P, 3 * P])
        lnp = keep("lnp", [P, 2, 4, KD])
        rw = keep("router_w", [P, KD, NE])
        rbias = keep("router_bias", [P, NE])
        epst = keep("eps", [P, 1])
        lower4 = keep("lower4", [P, EG, EG])
        iota64 = keep("slot_numbers", [P, 64])
        dve_step, act_step, pool_step = (Chain(sem(n)) for n in ("dve_step", "act_step", "pool_step"))
        ld_const, ld_wg, ld_wu, ld_wd = sem("ld_const"), [sem("ld_wg0"), sem("ld_wg1")], \
            [sem("ld_wu0"), sem("ld_wu1")], [sem("ld_wd0"), sem("ld_wd1")]
        ld_chunk = [sem("ld_chunk0"), sem("ld_chunk1"), sem("ld_chunk2")]
        chunk_count = [0, 0, 0]
        stored = sem("stored")
        n_stored = [0]

        chunk = [ring[:, 1, c * CH:(c + 1) * CH] for c in range(3)]

        def load_chunk(sp, c, src):
            n = 1
            for v in src.shape[1:]:
                n *= v
            sp.dma_start(chunk[c][0:src.shape[0], 0:n].rearrange("p (a b) -> p a b", b=src.shape[2]), src)\
              .then_inc(ld_chunk[c], 16)

        def store(eng, dst, src):
            n_stored[0] += 16
            eng.dma_start(dst, src).then_inc(stored, 16)

        def load_expert(sp, e, s):
            g = lambda w, k: w[bass.ds(e, 1)].rearrange("a (k p) n -> p (a k) n", p=P)
            sp.dma_start(ring[:, s, 0:CH].rearrange("p (k n) -> p k n", k=KD), g(I["moe_w_gate"], KD)).then_inc(ld_wg[s], 16)
            sp.dma_start(ring[:, s, CH:2 * CH].rearrange("p (k n) -> p k n", k=KD), g(I["moe_w_up"], KD)).then_inc(ld_wu[s], 16)
            sp.dma_start(ring[:, s, 2 * CH:3 * CH].rearrange("p (k n) -> p k n", k=FF // P), g(I["moe_w_down"], 4)).then_inc(ld_wd[s], 16)

        with ExitStack() as ssd:
            def sb(name, shape, dt=F32):
                return ssd.enter_context(nc.sbuf_tensor(name, shape, dt))

            zs = sb("z_silu", [P, JX, T])
            cv = sb("conv_out", [P, JC, T])
            dtr = sb("dt_raw", [NH, T])
            heads = sb("head_params", [NH, 3])
            normg = sb("norm_g", [P, JX])

            with ExitStack() as st:
                raw = st.enter_context(nc.sbuf_tensor("xbc_raw", [P, 2, SEQ + 3], F32))
                taps = st.enter_context(nc.sbuf_tensor("taps", [P, JC, NCONV, DB], F32))
                cacc = st.enter_context(nc.sbuf_tensor("conv_acc", [P, 2, T], F32))
                lastp = st.enter_context(nc.sbuf_tensor("last_prompt", [P, JC, 3], F32))
                convp = st.enter_context(nc.sbuf_tensor("conv_params", [P, JC, NCONV + 1], F32))
                bank = [st.enter_context(nc.psum_tensor(f"pj{i}", [P, 512], F32)) for i in range(8)]
                tile_done, tile_taken, conv_done, silu_done, pads, out_ready = (
                    sem(n) for n in ("s_tile_done", "s_tile_taken", "s_conv_done", "s_silu_done", "s_pads", "s_convout"))
                NT = JX + JC + 1
                taken = lambda m: m + 1 if m < JX else JX + 2 * (m - JX + 1)
                nchunk = (NT + 3) // 4

                with nc.Block() as block:
                    @block.sync
                    def _(sp):
                        sp.dma_start(xT[:], I["xT"].rearrange("(k p) t -> p k t", p=P)).then_inc(ld_const, 16)
                        w = I["ssd_w_in"].rearrange("(k p) n -> p k n", p=P)
                        for c in range(nchunk):
                            lo, hi = c * 512, min(c * 512 + 512, w.shape[2])
                            if c >= 2:
                                sp.wait_ge(tile_done, 4 * (c - 1))
                            load_chunk(sp, c % 2, w[:, :, lo:hi])
                            if c == 0:
                                for dst, name in ((convp[:], "conv_params"), (taps[:, :, 0:3, :], "conv_state"),
                                                  (ident[:], "ident"), (ones[:], "ones"), (m384[:], "m384"), (lnp[:], "lnp"),
                                                  (rw[:], "router_w"), (rbias[:], "router_bias"),
                                                  (epst[:], "eps"), (iota64[:], "slot_numbers"), (lower4[:], "lower4"), (heads[:], "heads"), (normg[:], "norm_g")):
                                    sp.dma_start(dst, I[name]).then_inc(ld_const, 16)
                        load_expert(sp, 0, 0)
                        sp.wait_ge(conv_done, JC)
                        store(sp, O["conv_prompt"], lastp[:])
                        store(sp, O["conv_sample"], taps[:, :, 1:4, :])
                        sp.wait_ge(stored, n_stored[0])

                    @block.tensor
                    def _(pe):
                        pe.wait_ge(ld_const, 16 * 14)
                        for m in range(NT):
                            c, s = m // 4, (m // 4) % 2
                            if m % 4 == 0:
                                pe.wait_ge(ld_chunk[s], 16 * (c // 2 + 1))
                            if m >= 8:
                                pe.wait_ge(tile_taken, taken(m - 8))
                            M = P if m < NT - 1 else NH
                            wc = chunk[s][:, 0:KD * (512 if m < NT - 1 else NH)].rearrange("p (k n) -> p k n", k=KD)
                            for k in range(KD):
                                last = nc.tensor.matmul(bank[m % 8][0:M, 0:T], wc[:, k, (m % 4) * P:(m % 4) * P + M],
                                                        xT[:, k, :], start=k == 0, stop=k == KD - 1)
                            last.then_inc(tile_done, 1)

                    @block.scalar
                    def _(act):
                        def silu(j):
                            act.wait_ge(conv_done, j + 1)
                            nc.scalar.activation(cv[:, j, :], cacc[:, j % 2, :], ACT.Silu).then_inc(silu_done, 1)
                        act.wait_ge(ld_const, 16 * 14)
                        act.wait_ge(pads, 1)
                        for m in range(NT):
                            act.wait_ge(tile_done, m + 1)
                            j = m - JX
                            if m < JX:
                                nc.scalar.activation(zs[:, m, :], bank[m % 8][:, 0:T], ACT.Silu).then_inc(tile_taken, 1)
                            elif j < JC:
                                if j >= 2:
                                    act.wait_ge(conv_done, j - 1)
                                nc.scalar.activation(raw[:, j % 2, 3:SEQ + 3], bank[m % 8][:, 0:SEQ], ACT.Copy).then_inc(tile_taken, 1)
                                nc.scalar.activation(taps[:, j, 3, :], bank[m % 8][:, SEQ:T], ACT.Copy).then_inc(tile_taken, 1)
                                if j >= 1:
                                    silu(j - 1)
                            else:
                                nc.scalar.activation(dtr[:], bank[m % 8][0:NH, 0:T], ACT.Identity, bias=heads[:, 0:1]).then_inc(tile_taken, 1)
                                silu(JC - 1)

                    @block.vector
                    def _(dve):
                        nc.vector.memset(raw[:, :, 0:3], 0.0).then_inc(pads, 1)
                        dve.wait_ge(ld_const, 16 * 14)
                        for j in range(JC):
                            dve.wait_ge(tile_taken, taken(JX + j))
                            if j >= 2:
                                dve.wait_ge(silu_done, j - 1)
                            r, a = raw[:, j % 2, :], cacc[:, j % 2, :]
                            nc.vector.tensor_copy(lastp[:, j, :], r[:, SEQ:SEQ + 3])
                            nc.vector.tensor_scalar(a[:, 0:SEQ], r[:, 0:SEQ], convp[:, j, 0:1], convp[:, j, 4:5], ALU.mult, ALU.add)
                            dve_step(dve, nc.vector.tensor_scalar(a[:, SEQ:T], taps[:, j, 0, :], convp[:, j, 0:1], convp[:, j, 4:5], ALU.mult, ALU.add))
                            for k in range(1, NCONV):
                                nc.vector.scalar_tensor_tensor(a[:, 0:SEQ], r[:, k:k + SEQ], convp[:, j, k:k + 1], a[:, 0:SEQ], ALU.mult, ALU.add)
                                i2 = nc.vector.scalar_tensor_tensor(a[:, SEQ:T], taps[:, j, k, :], convp[:, j, k:k + 1], a[:, SEQ:T], ALU.mult, ALU.add)
                                if k < NCONV - 1:
                                    dve_step(dve, i2)
                            i2.then_inc(conv_done, 1)
                chunk_count[0] = (nchunk + 1) // 2
                chunk_count[1] = nchunk // 2

            with ExitStack() as st:
                def sb2(name, shape, dt=F32):
                    return st.enter_context(nc.sbuf_tensor(name, shape, dt))

                hsel = ring[0:NH, 1, 0:DI]
                sp_t = sb2("softplus_tmp", [NH, 2, T])
                dt = sb2("dt", [NH, T])
                dta = sb2("dta", [NH, T])
                na = sb2("neg_a", [NH, 1])
                expin = sb2("expand_in", [NH, 2 * DB + 1])
                ex = sb2("expanded", [P, JX, 2 * DB + 1])
                dtt = sb2("dt_tok", [P, QT, NH])
                dtat = sb2("dta_tok", [P, QT, NH])
                cumt = sb2("cum_tok", [P, QT, NH])
                cumh = sb2("cum_head", [NH, SEQ])
                toend = sb2("to_end", [P, QT, NH])
                xd = ring[:, 1, CH:2 * CH].rearrange("p (q f) -> p q f", q=QT)
                btok = sb2("b_tok", [P, QT, NG * NS])
                bcd = sb2("bc_dec", [DB, 2, NG * NS])
                cbm = sb2("cb_masked", [P, 2, 3 * P])
                seg = sb2("seg", [P, 2, 3 * P])
                dec = sb2("decay", [P, 2, 3 * P])
                mm_ = sb2("weights_sbm", [P, 2, 3 * P])
                stp = ring[:, 1, 2 * CH:2 * CH + JX * NS].rearrange("p (j n) -> p j n", j=JX)
                std = sb2("state_dec", [P, 2, JX, NS])
                yd = sb2("y_dec", [P, JX, DB])
                junk = sb2("junk", [P, 4, NS])
                pt = [st.enter_context(nc.psum_tensor(f"ss{i}", [P, 512], F32)) for i in range(8)]
                (ld_hsel, sc_dt, dt_ready, da_ready, tr_done, tr_taken, cum_pe, cum_ready, cb_done, cb_ready, bc_done, seg_done,
                 exp_done, w_done, y_done, y_taken, exp_pe, ex_ready, xe_ready, st_done, st_taken, bcb_done, dec_read, new_state, sd_scaled) = (
                    sem("ss_" + n) for n in (
                        "ld_hsel", "sc_dt", "dt_ready", "da_ready", "tr_done", "tr_taken", "cum_pe", "cum_ready", "cb_done", "cb_ready",
                        "bc_done", "seg_done", "exp_done", "w_done", "y_done", "y_taken", "exp_pe", "ex_ready", "xe_ready", "st_done", "st_taken",
                        "bcb_done", "dec_read", "new_state", "sd_scaled"))
                st_out = [sem("ss_out0"), sem("ss_out1")]
                ld_sd = [sem("ss_ld_sd0"), sem("ss_ld_sd1")]
                NTR = 4 + 8 + 2 + 2

                with nc.Block() as block:
                    @block.sync
                    def _(sp):
                        sp.dma_start(hsel, I["hsel"]).then_inc(ld_hsel, 16)
                        for b in range(DB):
                            if b >= 2:
                                sp.wait_ge(st_out[b % 2], 16 * (b // 2))
                            sp.dma_start(std[:, b % 2], I["state_ssm"][b].rearrange("(j p) n -> p j n", p=P)).then_inc(ld_sd[b % 2], 16)
                            if b == 0:
                                sp.wait_ge(st_taken, 4)
                                store(sp, O["ssm_prompt"].rearrange("(j p) n -> p j n", p=P), stp)
                            sp.wait_ge(new_state, 16 * (b + 1))
                            sp.dma_start(O["ssm_sample"][b].rearrange("(j p) n -> p j n", p=P), std[:, b % 2]).then_inc(st_out[b % 2], 16)
                        for s in range(2):
                            sp.wait_ge(st_out[s], 16 * (DB // 2))
                        sp.wait_ge(stored, n_stored[0])

                    @block.scalar
                    def _(act):
                        act_step(act, nc.scalar.activation(sp_t[:, 0, :], dtr[:], ACT.Abs))
                        act_step(act, nc.scalar.activation(sp_t[:, 1, :], sp_t[:, 0, :], ACT.Exp, scale=-1.0))
                        nc.scalar.activation(sp_t[:, 0, :], sp_t[:, 1, :], ACT.Ln, bias=ones[0:NH, 0:1]).then_inc(sc_dt, 1)
                        nc.scalar.activation(na[:], heads[:, 1:2], ACT.Exp).then_inc(sc_dt, 1)
                        act.wait_ge(dt_ready, 1)
                        nc.scalar.activation(expin[:, DB:2 * DB], dta[:, SEQ:T], ACT.Exp).then_inc(da_ready, 1)
                        act.wait_ge(cum_ready, 3)
                        nc.scalar.activation(toend[:], toend[:], ACT.Exp).then_inc(cum_ready, 1)
                        for h in range(NH):
                            act.wait_ge(seg_done, 2 * h + 2)
                            if h >= 2:
                                act.wait_ge(w_done, h - 1)
                            nc.scalar.activation(dec[:, h % 2, :], seg[:, h % 2, :], ACT.Exp).then_inc(exp_done, 1)
                        for g in range(4):
                            act.wait_ge(st_done, g + 1)
                            nc.scalar.activation(stp[:, 4 * g:4 * g + 4, :], pt[g][:].rearrange("p (j n) -> p j n", j=4), ACT.Copy).then_inc(st_taken, 1)
                        act.wait_ge(ex_ready, 1)
                        for b in range(DB):
                            act.wait_ge(ld_sd[b % 2], 16 * (b // 2 + 1))
                            for j in range(JX):
                                nc.scalar.activation(std[:, b % 2, j, :], std[:, b % 2, j, :], ACT.Copy, scale=ex[:, j, DB + b:DB + b + 1]).then_inc(sd_scaled, 1)

                    @block.tensor
                    def _(pe):
                        tr = nc.tensor.transpose
                        pe.wait_ge(dt_ready, 1)
                        for q in range(QT):
                            tr(pt[0][:, q * NH:(q + 1) * NH], dt[:, q * P:(q + 1) * P], ident[0:NH, 0:NH])
                            last = tr(pt[0][:, (2 + q) * NH:(3 + q) * NH], dta[:, q * P:(q + 1) * P], ident[0:NH, 0:NH])
                        last.then_inc(tr_done, 1)
                        pe.wait_ge(tr_taken, 1)
                        tri = m384[:, 0:P]
                        mm = nc.tensor.matmul
                        mm(pt[1][:, 0:NH], tri, dtat[:, 0, :], start=True, stop=True)
                        mm(pt[1][:, NH:2 * NH], tri, dtat[:, 1, :], start=True, stop=False)
                        mm(pt[1][:, NH:2 * NH], ones[:], dtat[:, 0, :], start=False, stop=True)
                        mm(pt[1][:, 2 * NH:3 * NH], ones[:], dtat[:, 0, :], start=True, stop=False)
                        mm(pt[1][:, 2 * NH:3 * NH], ones[:], dtat[:, 1, :], start=False, stop=True)
                        mm(pt[2][0:NH, 0:SEQ], dtat[:, 0, :], m384[:, 0:SEQ], start=True, stop=False, skip_group_check=True)
                        mm(pt[2][0:NH, P:SEQ], dtat[:, 1, :], tri, start=False, stop=True, skip_group_check=True).then_inc(cum_pe, 1)
                        for n in range(12):
                            bk = pt[3 + n % 3]
                            if n >= 3:
                                pe.wait_ge(tr_taken, 1 + n - 2)
                            for a in range(4):
                                if n < 8:
                                    last = tr(bk[:, a * P:(a + 1) * P], cv[:, 4 * (n // 2) + a, (n % 2) * P:(n % 2 + 1) * P], ident[:])
                                elif n < 10:
                                    last = tr(bk[:, a * P:(a + 1) * P], cv[:, JX + a, (n - 8) * P:(n - 7) * P], ident[:])
                                else:
                                    last = tr(bk[0:DB, a * P:(a + 1) * P], cv[:, JX + NG * (n - 10) + a, SEQ:T], ident[:])
                            last.then_inc(tr_done, 1)
                        pe.wait_ge(da_ready, 1)
                        pe.wait_ge(ld_hsel, 16)
                        for j in range(JX):
                            last = mm(pt[6][:, j * (2 * DB + 1):(j + 1) * (2 * DB + 1)], hsel[:, j * P:(j + 1) * P], expin[:], start=True, stop=True)
                        last.then_inc(exp_pe, 1)
                        pe.wait_ge(cum_ready, 2)
                        pe.wait_ge(tr_taken, 13)

                        def cb(g):
                            if g == 0:
                                pe.wait_ge(ex_ready, 1)
                            if g >= 2:
                                pe.wait_ge(cb_ready, g - 1)
                            bk = pt[6 + g % 2]
                            mm(bk[:, 0:SEQ], cv[:, JX + g, 0:P], cv[:, JX + NG + g, 0:SEQ], start=True, stop=True)
                            mm(bk[:, SEQ:3 * P], cv[:, JX + g, P:SEQ], cv[:, JX + NG + g, P:SEQ], start=True, stop=True).then_inc(cb_done, 1)

                        def spread(h):
                            if h >= 3:
                                pe.wait_ge(seg_done, 2 * (h - 2))
                            mm(pt[h % 3][:, 0:SEQ], ident[0:NH, h:h + 1].to_broadcast([NH, P]), cumh[:], start=True, stop=True).then_inc(bc_done, 1)

                        cb(0)
                        spread(0)
                        spread(1)
                        for h in range(NH):
                            if h % 8 == 4 and h // 8 + 1 < NG:
                                cb(h // 8 + 1)
                            if h + 2 < NH:
                                spread(h + 2)
                            j, half = h // 2, 64 * (h % 2)
                            pe.wait_ge(w_done, h + 1)
                            if h % 2 == 0 and j >= 3:
                                pe.wait_ge(y_taken, j - 2)
                            yb = pt[3 + j % 3]
                            mm(yb[half:half + 64, 0:SEQ], xd[:, 0, h * HD:(h + 1) * HD], mm_[:, h % 2, 0:SEQ], start=True, stop=False, skip_group_check=True)
                            mm(yb[half:half + 64, P:SEQ], xd[:, 1, h * HD:(h + 1) * HD], mm_[:, h % 2, SEQ:3 * P], start=False, stop=True,
                               skip_group_check=True).then_inc(y_done, 1)
                        pe.wait_ge(xe_ready, 2)
                        pe.wait_ge(y_taken, JX)
                        for j in range(JX):
                            g = j // 4
                            for q in range(QT):
                                last = mm(pt[g][:, (j % 4) * NS:(j % 4 + 1) * NS], xd[:, q, j * P:(j + 1) * P],
                                          btok[:, q, g * NS:(g + 1) * NS], start=q == 0, stop=q == QT - 1)
                            if j % 4 == 3:
                                last.then_inc(st_done, 1)
                        for b in range(DB):
                            if b >= 2:
                                pe.wait_ge(dec_read, JX * (b - 1))
                            for c in range(2):
                                last = mm(pt[4 + 2 * (b % 2) + c][:], ident[0:DB, b:b + 1].to_broadcast([DB, P]), bcd[:, c, :], start=True, stop=True)
                            last.then_inc(bcb_done, 1)

                    @block.vector
                    def _(dve):
                        V = nc.vector
                        dve.wait_ge(sc_dt, 2)
                        V.tensor_scalar(na[:], na[:], -1.0, None, ALU.mult)
                        dve_step(dve, V.tensor_scalar(sp_t[:, 1, :], dtr[:], 0.0, None, ALU.max))
                        dve_step(dve, V.tensor_tensor(dt[:], sp_t[:, 0, :], sp_t[:, 1, :], ALU.add))
                        V.tensor_copy(expin[:, 0:DB], dt[:, SEQ:T])
                        V.tensor_copy(expin[:, 2 * DB:2 * DB + 1], heads[:, 2:3])
                        V.tensor_scalar(dta[:], dt[:], na[:, 0:1], None, ALU.mult).then_inc(dt_ready, 1)
                        dve.wait_ge(tr_done, 1)
                        V.tensor_copy(dtt[:], pt[0][:, 0:2 * NH].rearrange("p (q h) -> p q h", q=QT))
                        V.tensor_copy(dtat[:], pt[0][:, 2 * NH:4 * NH].rearrange("p (q h) -> p q h", q=QT)).then_inc(tr_taken, 1)
                        dve.wait_ge(tr_taken, 1)
                        dve.wait_ge(cum_pe, 1)
                        V.tensor_copy(cumt[:], pt[1][:, 0:2 * NH].rearrange("p (q h) -> p q h", q=QT)).then_inc(cum_ready, 1)
                        V.tensor_copy(cumh[:], pt[2][0:NH, 0:SEQ]).then_inc(cum_ready, 1)
                        dve.wait_ge(cum_ready, 2)
                        V.tensor_tensor(toend[:], pt[1][:, 2 * NH:3 * NH].unsqueeze(1).to_broadcast([P, QT, NH]), cumt[:], ALU.subtract).then_inc(cum_ready, 1)
                        for n in range(12):
                            dve.wait_ge(tr_done, n + 2)
                            bk = pt[3 + n % 3]
                            if n < 8:
                                g, q = n // 2, n % 2
                                V.tensor_tensor(xd[:, q, g * 512:(g + 1) * 512].rearrange("p (h d) -> p h d", d=HD), bk[:].rearrange("p (h d) -> p h d", d=HD),
                                                dtt[:, q, 8 * g:8 * g + 8].unsqueeze(2).to_broadcast([P, 8, HD]), ALU.mult).then_inc(tr_taken, 1)
                            elif n < 10:
                                V.tensor_copy(btok[:, n - 8, :], bk[:]).then_inc(tr_taken, 1)
                            else:
                                V.tensor_copy(bcd[:, n - 10, :], bk[0:DB, :]).then_inc(tr_taken, 1)
                        dve.wait_ge(exp_pe, 1)
                        V.tensor_copy(ex[:], pt[6][:, 0:JX * (2 * DB + 1)].rearrange("p (j c) -> p j c", j=JX)).then_inc(ex_ready, 1)
                        dve.wait_ge(ex_ready, 1)
                        def mask_cb(g):
                            dve.wait_ge(cb_done, g + 1)
                            V.tensor_tensor(cbm[:, g % 2, :], pt[6 + g % 2][:, 0:3 * P], m384[:], ALU.mult).then_inc(cb_ready, 1)
                        def segments(h):
                            dve.wait_ge(bc_done, h + 1)
                            if h >= 2:
                                dve.wait_ge(exp_done, h - 1)
                            V.tensor_scalar(seg[:, h % 2, 0:SEQ], pt[h % 3][:, 0:SEQ], cumt[:, 0, h:h + 1], 0.0, ALU.subtract, ALU.min).then_inc(seg_done, 1)
                            V.tensor_scalar(seg[:, h % 2, SEQ:3 * P], pt[h % 3][:, P:SEQ], cumt[:, 1, h:h + 1], 0.0, ALU.subtract, ALU.min).then_inc(seg_done, 1)
                        def y_out(j):
                            dve.wait_ge(y_done, 2 * j + 2)
                            dve_step(dve, V.scalar_tensor_tensor(cv[:, j, 0:SEQ], cv[:, j, 0:SEQ], ex[:, j, 2 * DB:2 * DB + 1], pt[3 + j % 3][:, 0:SEQ], ALU.mult, ALU.add))
                            V.tensor_tensor(cv[:, j, 0:SEQ], cv[:, j, 0:SEQ], zs[:, j, 0:SEQ], ALU.mult).then_inc(y_taken, 1)
                        mask_cb(0)
                        segments(0)
                        for h in range(NH):
                            if h % 8 == 7 and h // 8 + 1 < NG:
                                mask_cb(h // 8 + 1)
                            if h + 1 < NH:
                                segments(h + 1)
                            dve.wait_ge(exp_done, h + 1)
                            dve.wait_ge(cb_ready, h // 8 + 1)
                            if h >= 2:
                                dve.wait_ge(y_done, h - 1)
                            V.tensor_tensor(mm_[:, h % 2, :], dec[:, h % 2, :], cbm[:, (h // 8) % 2, :], ALU.mult).then_inc(w_done, 1)
                            if h % 2 == 1 and h >= 3:
                                y_out(h // 2 - 1)
                        y_out(JX - 1)
                        dve.wait_ge(cum_ready, 4)
                        for q in range(QT):
                            x3 = xd[:, q, :].rearrange("p (h d) -> p h d", d=HD)
                            V.tensor_tensor(x3, x3, toend[:, q, :].unsqueeze(2).to_broadcast([P, NH, HD]), ALU.mult).then_inc(xe_ready, 1)
                        V.tensor_tensor(yd[:], cv[:, 0:JX, SEQ:T], ex[:, :, 0:DB], ALU.mult).then_inc(dve_step.sem, 1)
                        dve_step.n += 1
                        dve.wait_ge(dve_step.sem, dve_step.n)
                        for b in range(DB):
                            dve.wait_ge(bcb_done, b + 1)
                            for j in range(JX):
                                g, s = j // 4, std[:, b % 2, j, :]
                                dve.wait_ge(sd_scaled, JX * b + j + 1)
                                V.scalar_tensor_tensor(s, pt[4 + 2 * (b % 2)][:, g * NS:(g + 1) * NS], yd[:, j, b:b + 1], s, ALU.mult, ALU.add).then_inc(new_state, 1)
                            for j in range(JX):
                                g, s = j // 4, std[:, b % 2, j, :]
                                dve.wait_ge(new_state, JX * b + j + 1)
                                if JX * b + j >= 4:
                                    dve.wait_ge(dec_read, JX * b + j - 3)
                                V.tensor_tensor_reduce(junk[:, j % 4, :], s, pt[5 + 2 * (b % 2)][:, g * NS:(g + 1) * NS], 1.0, 0.0, ALU.mult, ALU.add,
                                                       yd[:, j, b:b + 1]).then_inc(dec_read, 1)
                        dve.wait_ge(dec_read, JX * DB)
                        c3 = cv[:, 0:JX, SEQ:T]
                        dve_step(dve, V.tensor_tensor(c3, c3, ex[:, :, 2 * DB:2 * DB + 1].to_broadcast([P, JX, DB]), ALU.mult))
                        dve_step(dve, V.tensor_tensor(c3, c3, yd[:], ALU.add))
                        dve_step(dve, V.tensor_tensor(c3, c3, zs[:, :, SEQ:T], ALU.mult))

            with ExitStack() as st:
                rr = st.enter_context(nc.sbuf_tensor("rms", [P, NG, T], F32))
                bank = [st.enter_context(nc.psum_tensor(f"on{i}", [P, 512], F32)) for i in range(8)]
                sq_done, ms_done, sqrt_done, y_ready, o_done, o_taken = (sem("so_" + n) for n in ("sq", "ms", "sqrt", "y", "done", "taken"))
                base = [c * 16 for c in chunk_count]
                with nc.Block() as block:
                    @block.sync
                    def _(sp):
                        w = I["ssd_w_out"].rearrange("(k p) n -> p k n", p=P)
                        for c in range(4):
                            if c >= 2:
                                sp.wait_ge(o_done, 2 * (c - 1))
                            load_chunk(sp, c % 2, w[:, :, c * 256:(c + 1) * 256])

                    @block.scalar
                    def _(act):
                        for j in range(JX):
                            nc.scalar.activation(zs[:, j, :], cv[:, j, :], ACT.Square).then_inc(sq_done, 1)
                        for g in range(NG):
                            act.wait_ge(ms_done, g + 1)
                            nc.scalar.activation(rr[:, g, :], bank[g][:, 0:T], ACT.Sqrt, scale=1.0 / 512, bias=epst[:, 0:1]).then_inc(sqrt_done, 1)

                    @block.tensor
                    def _(pe):
                        for j in range(JX):
                            pe.wait_ge(sq_done, j + 1)
                            last = nc.tensor.matmul(bank[j // 4][:, 0:T], ones[:], zs[:, j, :], start=j % 4 == 0, stop=j % 4 == 3)
                            if j % 4 == 3:
                                last.then_inc(ms_done, 1)
                        pe.wait_ge(y_ready, JX)
                        for m in range(KD):
                            c = m // 2
                            if m % 2 == 0:
                                pe.wait_ge(ld_chunk[c % 2], base[c % 2] + 16 * (c // 2 + 1))
                            if m >= 4:
                                pe.wait_ge(o_taken, m - 3)
                            wc = chunk[c % 2].rearrange("p (k n) -> p k n", k=JX)
                            for k in range(JX):
                                last = nc.tensor.matmul(bank[4 + m % 4][:, 0:T], wc[:, k, (m % 2) * P:(m % 2 + 1) * P], cv[:, k, :],
                                                        start=k == 0, stop=k == JX - 1)
                            last.then_inc(o_done, 1)

                    @block.vector
                    def _(dve):
                        V = nc.vector
                        for g in range(NG):
                            dve.wait_ge(sqrt_done, g + 1)
                            dve_step(dve, V.reciprocal(rr[:, g, :], rr[:, g, :]))
                            for j in range(4 * g, 4 * g + 4):
                                V.scalar_tensor_tensor(cv[:, j, :], cv[:, j, :], normg[:, j:j + 1], rr[:, g, :], ALU.mult, ALU.mult).then_inc(y_ready, 1)
                        for m in range(KD):
                            dve.wait_ge(o_done, m + 1)
                            V.scalar_tensor_tensor(xT[:, m, :], xT[:, m, :], ALPHA, bank[4 + m % 4][:, 0:T], ALU.mult, ALU.add).then_inc(o_taken, 1)
                for c in range(2):
                    chunk_count[c] += 2

        ln_sems = [sem("ln_" + n) for n in ("mean", "cent", "sq", "var", "sqrt", "norm")]

        def layer_norm(L, which, src, dst, tag):
            use = 2 * L + which
            with ExitStack() as st:
                sq = st.enter_context(nc.sbuf_tensor("ln_sq_" + tag, [P, KD, T], F32))
                rs = st.enter_context(nc.sbuf_tensor("ln_rs_" + tag, [P, 2, T], F32))
                pm = st.enter_context(nc.psum_tensor("ln_m_" + tag, [P, 512], F32))
                pv = st.enter_context(nc.psum_tensor("ln_v_" + tag, [P, 512], F32))
                s_mean, s_cent, s_sq, s_var, s_sqrt, s_rs = ln_sems
                g, b = lnp[:, L, 2 * which, :], lnp[:, L, 2 * which + 1, :]
                with nc.Block() as block:
                    @block.tensor
                    def _(pe):
                        for k in range(KD):
                            last = nc.tensor.matmul(pm[:, 0:T], ones[:], src[:, k, :], start=k == 0, stop=k == KD - 1)
                        last.then_inc(s_mean, 1)
                        for k in range(KD):
                            pe.wait_ge(s_sq, KD * use + k + 1)
                            last = nc.tensor.matmul(pv[:, 0:T], ones[:], sq[:, k, :], start=k == 0, stop=k == KD - 1)
                        last.then_inc(s_var, 1)

                    @block.scalar
                    def _(act):
                        for k in range(KD):
                            act.wait_ge(s_cent, KD * use + k + 1)
                            nc.scalar.activation(sq[:, k, :], src[:, k, :], ACT.Square).then_inc(s_sq, 1)
                        act.wait_ge(s_var, use + 1)
                        nc.scalar.activation(rs[:, 1, :], pv[:, 0:T], ACT.Sqrt, scale=1.0 / D, bias=epst[:, 0:1]).then_inc(s_sqrt, 1)
                        for k in range(KD):
                            act.wait_ge(s_rs, KD * use + k + 1)
                            nc.scalar.activation(dst[:, k, :], src[:, k, :], ACT.Identity, scale=g[:, k:k + 1], bias=b[:, k:k + 1])

                    @block.vector
                    def _(dve):
                        V = nc.vector
                        dve.wait_ge(s_mean, use + 1)
                        dve_step(dve, V.tensor_scalar(rs[:, 0, :], pm[:, 0:T], 1.0 / D, None, ALU.mult))
                        for k in range(KD):
                            V.tensor_tensor(src[:, k, :], src[:, k, :], rs[:, 0, :], ALU.subtract).then_inc(s_cent, 1)
                        dve.wait_ge(s_sqrt, use + 1)
                        dve_step(dve, V.reciprocal(rs[:, 0, :], rs[:, 1, :]))
                        dve.wait_ge(s_sq, KD * use + KD)
                        for k in range(KD):
                            V.tensor_tensor(src[:, k, :], src[:, k, :], rs[:, 0, :], ALU.mult).then_inc(s_rs, 1)

        CAP = 64
        router_sems = [sem("r_" + n) for n in ("log", "init", "sig", "gate", "rank", "slots", "selg", "xtr", "xtok", "tr", "out", "got", "go")]
        ple_sems = [sem("e_" + n) for n in ("ld", "done", "sig", "out")]
        moe_sems = [sem("m_" + n) for n in ("gather", "packed", "gu", "silu", "hid", "turned", "ht", "down", "ys", "scatter", "acc")]

        def tail(L, out=None):
            layer_norm(L, 0, xT, xT, f"a{L}")
            with ExitStack() as outer:
                acc = outer.enter_context(nc.sbuf_tensor(f"acc{L}", [P, KD, T], F32))
                tile3 = [(0, P), (P, P), (SEQ, DB)]
                NF, NP2 = FF // P, NE // 2
                with ExitStack() as moe:
                    def sbm(name, shape, dt=F32):
                        return moe.enter_context(nc.sbuf_tensor(f"{name}{L}", shape, dt))
                    xtok = sbm("x_tok", [P, 3, D])
                    sel1 = sbm("slot_onehot", [P, 3, NE * CAP])
                    sgt = sbm("scatter_gates", [P, NP2, T])
                    gto = sbm("gates_over", [NE, T])
                    most = sbm("most_tokens", [1, 1], I32)
                    with ExitStack() as st:
                        def sb3(name, shape):
                            return st.enter_context(nc.sbuf_tensor(f"{name}{L}", shape, F32))
                        score, sel, cmp5, eq5, rank, insel, gs, best = (
                            sb3("score", [P, 3, NE]), sb3("sel", [P, 3, NE]), sb3("cmp", [P, 3, EG, EG, EG]), sb3("eq", [P, 3, EG, EG, EG]),
                            sb3("rank", [P, 3, NE]), sb3("insel", [P, 3, NE]), sb3("gs", [P, 3, EG]), sb3("best", [P, 3, EG]))
                        wsum, slot, gover, cmax = sb3("wsum", [P, 3]), sb3("slot", [P, 3, NE]), sb3("gover", [P, 3, NE]), sb3("cmax", [1, 1])
                        selg = sb3("slot_gate", [P, 3, NE * CAP])
                        pr = st.enter_context(nc.psum_tensor(f"pr{L}", [P, 512], F32))
                        prk = st.enter_context(nc.psum_tensor(f"prk{L}", [P, 512], F32))
                        pgo = st.enter_context(nc.psum_tensor(f"pgo{L}", [P, 512], F32))
                        pg = [st.enter_context(nc.psum_tensor(f"pg{L}{i}", [P, 512], F32)) for i in range(4)]
                        r_log, r_init, r_sig, r_gate, r_rank, r_slots, r_selg, r_xtr, r_xtok, r_tr, r_out, r_got, r_go = router_sems
                        with nc.Block() as block:
                            @block.sync
                            def _(sp):
                                load_expert(sp, NE * L + 1, 1)

                            @block.tensor
                            def _(pe):
                                tr, mm = nc.tensor.transpose, nc.tensor.matmul
                                for q, (t0, n) in enumerate(tile3):
                                    for k in range(KD):
                                        last = mm(pr[0:n, q * NE:(q + 1) * NE], xT[:, k, t0:t0 + n], rw[:, k, :], start=k == 0, stop=k == KD - 1)
                                last.then_inc(r_log, 1)
                                for c in range(6):
                                    t0, n = tile3[c // 2]
                                    if c >= 4:
                                        pe.wait_ge(r_xtok, 6 * L + c - 3)
                                    for a in range(4):
                                        last = tr(pg[c % 4][0:n, a * P:(a + 1) * P], xT[:, 4 * (c % 2) + a, t0:t0 + n], ident[:])
                                    last.then_inc(r_xtr, 1)
                                pe.wait_ge(r_gate, 2 * L + 1)
                                tri = m384[:, 0:P]
                                for q, (t0, n) in enumerate(tile3):
                                    for p in range(q):
                                        mm(prk[0:n, q * NE:(q + 1) * NE], ones[:, 0:n], insel[:, p, :], start=p == 0, stop=False)
                                    mm(prk[0:n, q * NE:(q + 1) * NE], tri[0:n, 0:n], insel[0:n, q, :], start=q == 0, stop=True)
                                for q, (t0, n) in enumerate(tile3):
                                    last = mm(prk[:, 3 * NE:4 * NE], ones[0:n, :], insel[0:n, q, :], start=q == 0, stop=q == 2)
                                last.then_inc(r_rank, 1)
                                pe.wait_ge(r_go, L + 1)
                                for q, (t0, n) in enumerate(tile3):
                                    last = tr(pgo[0:NE, t0:t0 + n], gover[0:n, q, :], ident[0:n, 0:n])
                                last.then_inc(r_got, 1)
                                pe.wait_ge(r_selg, 3 * (L + 1))
                                pe.wait_ge(r_xtok, 6 * (L + 1))
                                for i in range(NP2):
                                    if i >= 4:
                                        pe.wait_ge(r_out, NP2 * L + i - 3)
                                    for q, (t0, n) in enumerate(tile3):
                                        last = tr(pg[i % 4][:, t0:t0 + n], selg[0:n, q, i * P:(i + 1) * P], ident[0:n, 0:n])
                                    last.then_inc(r_tr, 1)

                            @block.scalar
                            def _(act):
                                act.wait_ge(r_log, L + 1)
                                act.wait_ge(r_init, L + 1)
                                nc.scalar.activation(score[:, 0:2, :], pr[:, 0:2 * NE].rearrange("p (q e) -> p q e", q=2), ACT.Sigmoid).then_inc(r_sig, 1)
                                nc.scalar.activation(score[0:DB, 2, :], pr[0:DB, 2 * NE:3 * NE], ACT.Sigmoid).then_inc(r_sig, 1)
                                for c in range(6):
                                    t0, n = tile3[c // 2]
                                    act.wait_ge(r_xtr, 6 * L + c + 1)
                                    nc.scalar.activation(xtok[0:n, c // 2, (c % 2) * 512:(c % 2 + 1) * 512], pg[c % 4][0:n, :], ACT.Copy).then_inc(r_xtok, 1)
                                act.wait_ge(r_got, L + 1)
                                nc.scalar.activation(gto[:], pgo[0:NE, 0:T], ACT.Copy)
                                for i in range(NP2):
                                    act.wait_ge(r_tr, NP2 * L + i + 1)
                                    nc.scalar.activation(sgt[:, i, :], pg[i % 4][:, 0:T], ACT.Copy).then_inc(r_out, 1)

                            @block.gpsimd
                            def _(pool):
                                pool.wait_ge(r_gate, 2 * L + 2)
                                for q, (t0, n) in enumerate(tile3):
                                    pool.wait_ge(r_slots, 3 * L + q + 1)
                                    c3 = lambda t: t[0:n, q, :].rearrange("p (e c) -> p e c", c=CAP)
                                    nc.gpsimd.tensor_tensor(c3(selg), c3(sel1), rank[0:n, q, :].unsqueeze(2).to_broadcast([n, NE, CAP]), ALU.mult).then_inc(r_selg, 1)

                            @block.vector
                            def _(dve):
                                V = nc.vector
                                V.memset(score[:], 0.5).then_inc(r_init, 1)
                                dve.wait_ge(r_sig, 2 * L + 2)
                                dve_step(dve, V.tensor_tensor(sel[:], score[:], rbias[:].unsqueeze(1).to_broadcast([P, 3, NE]), ALU.add))
                                low = lower4[:].unsqueeze(1).to_broadcast([P, 3 * EG, EG, EG])
                                c4, e4 = (t[:].rearrange("p q g j i -> p (q g) j i") for t in (cmp5, eq5))
                                s3 = sel[:].rearrange("p q (g j) -> p (q g) j", j=EG)
                                si, sj = s3.unsqueeze(2).to_broadcast([P, 3 * EG, EG, EG]), s3.unsqueeze(3).to_broadcast([P, 3 * EG, EG, EG])
                                V.tensor_tensor(c4, si, sj, ALU.is_gt)
                                dve_step(dve, V.tensor_tensor(e4, si, sj, ALU.is_equal))
                                dve_step(dve, V.tensor_tensor(e4, e4, low, ALU.mult))
                                dve_step(dve, V.tensor_tensor(c4, c4, e4, ALU.add))
                                dve_step(dve, V.tensor_reduce(rank[:].rearrange("p q (g j) -> p (q g) j", j=EG), c4, AX.X, ALU.add))
                                dve_step(dve, V.tensor_scalar(insel[:], rank[:], 1.5, None, ALU.is_lt))
                                dve_step(dve, V.tensor_tensor(rank[:], sel[:], insel[:], ALU.mult))
                                dve_step(dve, V.tensor_reduce(gs[:].rearrange("p q g -> p (q g)"), rank[:].rearrange("p q (g j) -> p (q g) j", j=EG), AX.X, ALU.add))
                                gi, gj = gs[:].unsqueeze(2).to_broadcast([P, 3, EG, EG]), gs[:].unsqueeze(3).to_broadcast([P, 3, EG, EG])
                                cg, eg = cmp5[:, :, 0, :, :], eq5[:, :, 0, :, :]
                                V.tensor_tensor(cg, gi, gj, ALU.is_gt)
                                dve_step(dve, V.tensor_tensor(eg, gi, gj, ALU.is_equal))
                                dve_step(dve, V.tensor_tensor(eg, eg, lower4[:].unsqueeze(1).to_broadcast([P, 3, EG, EG]), ALU.mult))
                                dve_step(dve, V.tensor_tensor(cg, cg, eg, ALU.add))
                                dve_step(dve, V.tensor_reduce(best[:], cg, AX.X, ALU.add))
                                dve_step(dve, V.tensor_scalar(best[:], best[:], 0.5, None, ALU.is_lt))
                                i3 = insel[:].rearrange("p q (g j) -> p (q g) j", j=EG)
                                V.tensor_tensor(i3, i3, best[:].rearrange("p q g -> p (q g)").unsqueeze(2).to_broadcast([P, 3 * EG, EG]), ALU.mult).then_inc(r_gate, 1)
                                dve.wait_ge(r_gate, 2 * L + 1)
                                dve_step(dve, V.tensor_tensor(rank[:], insel[:], score[:], ALU.mult))
                                dve_step(dve, V.tensor_reduce(wsum[:], rank[:], AX.X, ALU.add))
                                dve_step(dve, V.reciprocal(wsum[:], wsum[:]))
                                V.tensor_tensor(rank[:], rank[:], wsum[:].unsqueeze(2).to_broadcast([P, 3, NE]), ALU.mult).then_inc(r_gate, 1)
                                dve.wait_ge(r_rank, L + 1)
                                for q0, q1, n in ((0, 2, P), (2, 3, DB)):
                                    v = lambda t: t[0:n, q0:q1, :]
                                    pk = prk[0:n, q0 * NE:q1 * NE].rearrange("p (q e) -> p q e", e=NE)
                                    V.tensor_tensor(v(slot), pk, v(insel), ALU.mult)
                                    i1 = V.tensor_scalar(v(gover), pk, CAP + 0.5, None, ALU.is_gt)
                                dve_step(dve, i1)
                                for q, (t0, n) in enumerate(tile3):
                                    V.tensor_tensor(sel1[0:n, q, :].rearrange("p (e c) -> p e c", c=CAP), slot[0:n, q, :].unsqueeze(2).to_broadcast([n, NE, CAP]),
                                                    iota64[0:n, :].unsqueeze(1).to_broadcast([n, NE, CAP]), ALU.is_equal).then_inc(r_slots, 1)
                                dve.wait_ge(r_gate, 2 * L + 2)
                                V.tensor_tensor(gover[:, 0:2, :], gover[:, 0:2, :], rank[:, 0:2, :], ALU.mult)
                                V.tensor_tensor(gover[0:DB, 2, :], gover[0:DB, 2, :], rank[0:DB, 2, :], ALU.mult).then_inc(r_go, 1)
                                dve_step(dve, V.tensor_reduce(cmax[:], prk[0:1, 3 * NE:4 * NE], AX.X, ALU.max))
                                V.tensor_copy(most[:], cmax[:])
                                V.tensor_scalar(acc[:], xT[:], ALPHA, None, ALU.mult)
                    xg = sbm("x_packed", [P, KD, 2 * CAP])
                    sg = sbm("silu_gate", [P, FF])
                    hid = sbm("hid", [P, FF])
                    ht = sbm("hid_T", [P, NF, 2 * CAP])
                    ys = sbm("y_slots", [P, D])
                    gb = [moe.enter_context(nc.psum_tensor(f"mg{L}{n}", [P, 512], F32)) for n in range(2)]
                    hb = [moe.enter_context(nc.psum_tensor(f"mh{L}{n}", [P, 512], F32)) for n in range(2)]
                    ob = [moe.enter_context(nc.psum_tensor(f"mo{L}{n}", [P, 512], F32)) for n in range(4)]
                    gathered, packed, gu_done, silu_ok, hid_ok, turned, ht_ok, down_done, ys_ok, sc_done, acc_ok = moe_sems
                    n1, n2, n8 = NP2 * L, 2 * NP2 * L, 8 * NP2 * L
                    ld0 = 16 * NP2 * L

                    with nc.Block() as block:
                        @block.sync
                        def _(sp):
                            def body(i, last=False):
                                slots = [s for s in range(2) if not (last and (s == 1 or L == 1))]
                                src = lambda w, s: w[bass.ds(NE * L + 2 + 2 * i + s, 1)].rearrange("a (k p) n -> p (a k) n", p=P)
                                for s in slots:
                                    sp.wait_ge(gu_done, 2 * i + s + 1 + n2)
                                    sp.dma_start(ring[:, s, 0:CH].rearrange("p (k n) -> p k n", k=KD), src(I["moe_w_gate"], s)).then_inc(ld_wg[s], 16)
                                    sp.dma_start(ring[:, s, CH:2 * CH].rearrange("p (k n) -> p k n", k=KD), src(I["moe_w_up"], s)).then_inc(ld_wu[s], 16)
                                for s in slots:
                                    sp.wait_ge(down_done, 2 * i + s + 1 + n2)
                                    sp.dma_start(ring[:, s, 2 * CH:3 * CH].rearrange("p (k n) -> p k n", k=NF), src(I["moe_w_down"], s)).then_inc(ld_wd[s], 16)
                            with sp.Fori(0, NP2 - 1) as i:
                                body(i)
                            body(NP2 - 1, True)

                        @block.tensor
                        def _(pe):
                            mm = nc.tensor.matmul

                            def gather(i, first=False):
                                for a in range(2):
                                    if not first:
                                        pe.wait_ge(packed, 2 * i + a - 1 + n2)
                                    for k in range(4):
                                        for q, (t0, n) in enumerate(tile3):
                                            last = mm(gb[a][:, k * P:(k + 1) * P], xtok[0:n, q, (4 * a + k) * P:(4 * a + k + 1) * P],
                                                      sel1[0:n, q, bass.ds(i * 2 * CAP, 2 * CAP)], start=q == 0, stop=q == 2)
                                    last.then_inc(gathered, 1)

                            def gate_up(i, first=False):
                                pe.wait_ge(packed, 2 * i + 2 + n2)
                                if not first:
                                    pe.wait_ge(hid_ok, i + n1)
                                for s in range(2):
                                    for w, ld in enumerate((ld_wg, ld_wu)):
                                        pe.wait_ge(ld[s], 16 * i + 16 + ld0)
                                        wt = ring[:, s, w * CH:(w + 1) * CH].rearrange("p (k n) -> p k n", k=KD)
                                        for k in range(KD):
                                            last = mm(hb[w][s * CAP:(s + 1) * CAP, :], xg[:, k, s * CAP:(s + 1) * CAP], wt[:, k, :],
                                                      start=k == 0, stop=k == KD - 1)
                                    last.then_inc(gu_done, 1)

                            def turn(i, first=False):
                                pe.wait_ge(hid_ok, i + 1 + n1)
                                if not first:
                                    pe.wait_ge(acc_ok, 8 * i - 1 + n8)
                                for f in range(NF):
                                    last = nc.tensor.transpose(ob[0][:, f * P:(f + 1) * P], hid[:, f * P:(f + 1) * P], ident[:])
                                last.then_inc(turned, 1)

                            def down(i, first=False):
                                pe.wait_ge(ht_ok, i + 1 + n1)
                                if not first:
                                    pe.wait_ge(ys_ok, 2 * i + n2)
                                for s in range(2):
                                    pe.wait_ge(ld_wd[s], 16 * i + 16 + ld0)
                                    wt = ring[:, s, 2 * CH:3 * CH].rearrange("p (k n) -> p k n", k=NF)
                                    for a in range(2):
                                        for k in range(NF):
                                            last = mm(ob[2 + a][s * CAP:(s + 1) * CAP, :], ht[:, k, s * CAP:(s + 1) * CAP], wt[:, k, a * 512:(a + 1) * 512],
                                                      start=k == 0, stop=k == NF - 1)
                                    last.then_inc(down_done, 1)

                            def scatter(i, first=False):
                                pe.wait_ge(ys_ok, 2 * i + 2 + n2)
                                for d in range(KD):
                                    if not (first and d < 2):
                                        pe.wait_ge(acc_ok, 8 * i + d - 1 + n8)
                                    mm(ob[d % 2][:, 0:T], ys[:, d * P:(d + 1) * P], sgt[:, bass.ds(i, 1), :].rearrange("p a t -> p (a t)"),
                                       start=True, stop=True).then_inc(sc_done, 1)

                            def body(i):
                                gate_up(i)
                                scatter(i - 1)
                                turn(i)
                                gather(i + 1)
                                down(i)

                            gather(0, True)
                            gate_up(0, True)
                            turn(0, True)
                            gather(1)
                            down(0, True)
                            gate_up(1)
                            scatter(0, True)
                            turn(1)
                            gather(2)
                            down(1)
                            with pe.Fori(2, NP2 - 1) as i:
                                body(i)
                            gate_up(NP2 - 1)
                            scatter(NP2 - 2)
                            turn(NP2 - 1)
                            down(NP2 - 1)
                            scatter(NP2 - 1)

                        @block.scalar
                        def _(act):
                            A_ = nc.scalar.activation

                            def pack(i, first=False):
                                for a in range(2):
                                    act.wait_ge(gathered, 2 * i + a + 1 + n2)
                                    if not first:
                                        act.wait_ge(gu_done, 2 * i + n2)
                                    A_(xg[:, 4 * a:4 * a + 4, :].rearrange("p k c -> p (k c)"), gb[a][:], ACT.Copy).then_inc(packed, 1)

                            def body(i, first=False, last=False):
                                act.wait_ge(gu_done, 2 * i + 2 + n2)
                                if not first:
                                    act.wait_ge(hid_ok, i + n1)
                                A_(sg[:], hb[0][:], ACT.Silu).then_inc(silu_ok, 1)
                                act.wait_ge(turned, i + 1 + n1)
                                if not first:
                                    act.wait_ge(down_done, 2 * i + n2)
                                A_(ht[:].rearrange("p f c -> p (f c)"), ob[0][:], ACT.Copy).then_inc(ht_ok, 1)
                                if not last:
                                    pack(i + 1)
                                act.wait_ge(down_done, 2 * i + 2 + n2)
                                if not first:
                                    act.wait_ge(sc_done, 8 * i + n8)
                                for a in range(2):
                                    A_(ys[:, a * 512:(a + 1) * 512], ob[2 + a][:], ACT.Copy).then_inc(ys_ok, 1)

                            pack(0, True)
                            body(0, True)
                            with act.Fori(1, NP2 - 1) as i:
                                body(i)
                            body(NP2 - 1, last=True)

                        @block.vector
                        def _(dve):
                            V = nc.vector

                            def body(i, first=False):
                                dve.wait_ge(silu_ok, i + 1 + n1)
                                if not first:
                                    dve.wait_ge(turned, i + n1)
                                V.tensor_tensor(hid[:], hb[1][:], sg[:], ALU.mult).then_inc(hid_ok, 1)
                                if not first:
                                    add(i - 1)

                            def add(i):
                                for d in range(KD):
                                    dve.wait_ge(sc_done, 8 * i + d + 1 + n8)
                                    V.tensor_tensor(acc[:, d, :], acc[:, d, :], ob[d % 2][:, 0:T], ALU.add).then_inc(acc_ok, 1)

                            body(0, True)
                            with dve.Fori(1, NP2) as i:
                                body(i)
                            add(NP2 - 1)

                    o_ld, o_dve, o_pe, o_act = (sem(f"over{L}_{n}") for n in ("ld", "dve", "pe", "act"))
                    gox = sbm("gate_row", [NE, T])
                    osg, ohu, ohid = sbm("over_silu", [P, T]), sbm("over_up", [P, T]), sbm("over_hid", [P, NF, T])
                    NPE, NDV = 1 + NF + KD, 1 + 2 * NF + KD

                    def rounds(eng, body, before=None):
                        n = eng.value_load(most[0:1, 0:1], min_val=0, max_val=T)
                        with eng.If(n > CAP):
                            if before is not None:
                                before()
                            with eng.Fori(0, NE) as e:
                                body(e)

                    with nc.Block() as block:
                        @block.sync
                        def _(sp):
                            def body(e):
                                sp.wait_ge(o_dve, NDV * e + 1)
                                for w, (name, k) in enumerate((("moe_w_gate", KD), ("moe_w_up", KD), ("moe_w_down", NF))):
                                    src = I[name][bass.ds(NE * L + e, 1)].rearrange("a (k p) n -> p (a k) n", p=P)
                                    sp.dma_start(ring[:, 1, w * CH:(w + 1) * CH].rearrange("p (k n) -> p k n", k=k), src).then_inc(o_ld, 16)
                            rounds(sp, body)

                        @block.tensor
                        def _(pe):
                            def body(e):
                                pe.wait_ge(o_dve, NDV * e + 2)
                                nc.tensor.matmul(gb[0][:, 0:T], ones[0:NE, :], gox[:], start=True, stop=True).then_inc(o_pe, 1)
                                pe.wait_ge(o_ld, 48 * e + 48)
                                for f in range(NF):
                                    if f >= 1:
                                        pe.wait_ge(o_dve, NDV * e + 2 + 2 * f)
                                    for w in range(2):
                                        wt = ring[:, 1, w * CH:(w + 1) * CH].rearrange("p (k n) -> p k n", k=KD)
                                        for k in range(KD):
                                            last = nc.tensor.matmul(hb[w][:, 0:T], wt[:, k, f * P:(f + 1) * P], xT[:, k, :], start=k == 0, stop=k == KD - 1)
                                    last.then_inc(o_pe, 1)
                                wt = ring[:, 1, 2 * CH:3 * CH].rearrange("p (k n) -> p k n", k=NF)
                                for d in range(KD):
                                    pe.wait_ge(o_dve, NDV * e + 2 + 2 * NF + d)
                                    for k in range(NF):
                                        last = nc.tensor.matmul(ob[0][:, 0:T], wt[:, k, d * P:(d + 1) * P], ohid[:, k, :], start=k == 0, stop=k == NF - 1)
                                    last.then_inc(o_pe, 1)
                            rounds(pe, body)

                        @block.scalar
                        def _(act):
                            def body(e):
                                for f in range(NF):
                                    act.wait_ge(o_pe, NPE * e + f + 2)
                                    nc.scalar.activation(osg[:], hb[0][:, 0:T], ACT.Silu).then_inc(o_act, 1)
                            rounds(act, body)

                        @block.vector
                        def _(dve):
                            V = nc.vector

                            def before():
                                V.memset(gox[:], 0.0).then_inc(o_dve, 1)

                            def body(e):
                                dve.wait_ge(o_dve, NDV * e + 1)
                                V.tensor_scalar(gox[:], gto[:], ident[0:NE, bass.ds(e, 1)], None, ALU.mult).then_inc(o_dve, 1)
                                for f in range(NF):
                                    dve.wait_ge(o_act, NF * e + f + 1)
                                    V.tensor_tensor(ohu[:], hb[1][:, 0:T], osg[:], ALU.mult).then_inc(o_dve, 1)
                                    dve.wait_ge(o_dve, NDV * e + 3 + 2 * f)
                                    V.tensor_tensor(ohid[:, f, :], gb[0][:, 0:T], ohu[:], ALU.mult).then_inc(o_dve, 1)
                                for d in range(KD):
                                    dve.wait_ge(o_pe, NPE * e + NF + d + 2)
                                    V.tensor_tensor(acc[:, d, :], acc[:, d, :], ob[0][:, 0:T], ALU.add).then_inc(o_dve, 1)
                            rounds(dve, body, before)

                layer_norm(L, 1, acc, acc, f"b{L}")
                with ExitStack() as st:
                    pT = st.enter_context(nc.sbuf_tensor(f"pT{L}", [P, 2, T], F32))
                    sgm = st.enter_context(nc.sbuf_tensor(f"sgm{L}", [P, 2, T], F32))
                    pa = [st.enter_context(nc.psum_tensor(f"pa{L}{i}", [P, 512], F32)) for i in range(2)]
                    pb = [st.enter_context(nc.psum_tensor(f"pb{L}{i}", [P, 512], F32)) for i in range(2)]
                    ld_p, e_done, e_sig, e_out = ple_sems
                    cnt = [16 * c for c in chunk_count]
                    with nc.Block() as block:
                        @block.sync
                        def _(sp):
                            sp.dma_start(pT[:], I["pT"][L].rearrange("(k p) t -> p k t", p=P)).then_inc(ld_p, 16)
                            load_chunk(sp, 2, I["ple_proj"][L].rearrange("(k p) n -> p k n", p=P))
                            w = I["ple_gate"][L].rearrange("(k p) n -> p k n", p=P)
                            for c in range(2):
                                load_chunk(sp, c, w[:, :, 512 * c:512 * c + 512])
                            if out is not None:
                                sp.wait_ge(e_out, KD * L + KD)
                                store(sp, out, xT[:])

                        @block.tensor
                        def _(pe):
                            pe.wait_ge(ld_p, 16 * L + 16)
                            pe.wait_ge(ld_chunk[2], cnt[2] + 16)
                            wp = chunk[2][:, 0:2 * D].rearrange("p (k n) -> p k n", k=2)
                            for m in range(KD):
                                if m % 4 == 0:
                                    pe.wait_ge(ld_chunk[m // 4], cnt[m // 4] + 16)
                                if m >= 2:
                                    pe.wait_ge(e_out, KD * L + m - 1)
                                wc = chunk[m // 4].rearrange("p (k n) -> p k n", k=KD)
                                for k in range(KD):
                                    nc.tensor.matmul(pa[m % 2][:, 0:T], wc[:, k, (m % 4) * P:(m % 4 + 1) * P], acc[:, k, :], start=k == 0, stop=k == KD - 1)
                                for k in range(2):
                                    last = nc.tensor.matmul(pb[m % 2][:, 0:T], wp[:, k, m * P:(m + 1) * P], pT[:, k, :], start=k == 0, stop=k == 1)
                                last.then_inc(e_done, 1)

                        @block.scalar
                        def _(act):
                            for m in range(KD):
                                act.wait_ge(e_done, KD * L + m + 1)
                                if m >= 2:
                                    act.wait_ge(e_out, KD * L + m - 1)
                                nc.scalar.activation(sgm[:, m % 2, :], pa[m % 2][:, 0:T], ACT.Sigmoid).then_inc(e_sig, 1)

                        @block.vector
                        def _(dve):
                            for m in range(KD):
                                dve.wait_ge(e_sig, KD * L + m + 1)
                                dve_step(dve, nc.vector.tensor_tensor(sgm[:, m % 2, :], sgm[:, m % 2, :], pb[m % 2][:, 0:T], ALU.mult))
                                nc.vector.tensor_tensor(xT[:, m, :], sgm[:, m % 2, :], acc[:, m, :], ALU.add).then_inc(e_out, 1)
                    for c in range(3):
                        chunk_count[c] += 1

        tail(0)
        with ExitStack() as nsa:
            def sb(name, shape, dt=F32):
                return nsa.enter_context(nc.sbuf_tensor(name, shape, dt))

            qT = sb("q_T", [P, KD, T])
            kvT = sb("kv_T", [P, KVT, T])
            oT = sb("o_T", [P, KD, T])
            gT_ = sb("gates_T", [3 * AH, T])
            vtok = sb("v_tok", [P, QT, 512])
            vnew = sb("v_new", [DB, 512])
            gtok = sb("gates_tok", [P, QT, 3 * AH])
            wb = sb("pos_softmax", [P, 4, BLK])
            kcd = sb("cmp_dec", [P, 4, DB, NBP])
            vcd = sb("vc_dec", [NBP, DB, 256])
            ptab = sb("page_table", [1, DB * NPG], I32)
            K_CMP, V_CMP, K_SEL, V_SEL, K_WIN, V_WIN = range(0, KVT, 2)
            ld_ptab, n_base = sem("ld_ptab"), [16 * c for c in chunk_count]

            with ExitStack() as st:
                bank = [st.enter_context(nc.psum_tensor(f"np{i}", [P, 512], F32)) for i in range(8)]
                tile_done, tile_taken = sem("n_tile_done"), sem("n_tile_taken")
                NT = KD + KVT + 1
                nchunk = (NT + 3) // 4
                with nc.Block() as block:
                    @block.sync
                    def _(sp):
                        w = I["nsa_w_in"].rearrange("(k p) n -> p k n", p=P)
                        for c in range(nchunk):
                            if c >= 2:
                                sp.wait_ge(tile_done, 4 * (c - 1))
                            load_chunk(sp, c % 2, w[:, :, c * 512:min(c * 512 + 512, w.shape[2])])
                        sp.dma_start(wb[:], I["pos_w"]).then_inc(ld_ptab, 16)
                        sp.dma_start(ptab[:], I["page_table"]).then_inc(ld_ptab, 16)
                        store(sp, O["win_old"], I["cache_win"][:, 1:, :])

                    @block.tensor
                    def _(pe):
                        for m in range(NT):
                            c, s = m // 4, (m // 4) % 2
                            if m % 4 == 0:
                                pe.wait_ge(ld_chunk[s], n_base[s] + 16 * (c // 2 + 1))
                            if m >= 8:
                                pe.wait_ge(tile_taken, m - 7)
                            M = P if m < NT - 1 else 3 * AH
                            wc = chunk[s][:, 0:KD * (512 if m < NT - 1 else M)].rearrange("p (k n) -> p k n", k=KD)
                            for k in range(KD):
                                last = nc.tensor.matmul(bank[m % 8][0:M, 0:T], wc[:, k, (m % 4) * P:(m % 4) * P + M],
                                                        xT[:, k, :], start=k == 0, stop=k == KD - 1)
                            last.then_inc(tile_done, 1)

                    @block.scalar
                    def _(act):
                        for m in range(NT):
                            act.wait_ge(tile_done, m + 1)
                            if m < KD:
                                nc.scalar.activation(qT[:, m, :], bank[m % 8][:, 0:T], ACT.Copy, scale=QS).then_inc(tile_taken, 1)
                            elif m < NT - 1:
                                nc.scalar.activation(kvT[:, m - KD, :], bank[m % 8][:, 0:T], ACT.Copy).then_inc(tile_taken, 1)
                            else:
                                nc.scalar.activation(gT_[:], bank[m % 8][0:3 * AH, 0:T], ACT.Sigmoid).then_inc(tile_taken, 1)
                chunk_count[0] += (nchunk + 1) // 2
                chunk_count[1] += nchunk // 2

            with ExitStack() as st:
                def sb2(name, shape, dt=F32):
                    return st.enter_context(nc.sbuf_tensor(name, shape, dt))

                dm = sb2("dist_masked", [P, 3 * P])
                cbias, cmask = sb2("cmp_bias", [P, QT, AH, 4]), sb2("cmp_mask", [P, QT, AH, 4])
                wst = sb2("pos_stat", [P, 4])
                ctmp = sb2("cmp_tmp", [P, 4, SEQ])
                kc = sb2("cmp_prompt", [P, 4, 4])
                vx = sb2("vc_spread", [P, 580])
                vci = sb2("vc_blockdiag", [4 * AH, KD, P])
                pc = sb2("cmp_probs", [P, QT, AH, 4])
                pst = sb2("cmp_stat", [P, QT, AH])
                pct = sb2("cmp_probs_T", [4 * AH, SEQ])
                sbuf = sb2("scores", [P, 3, 3 * P])
                nm, sm, wgt = sb2("neg_max", [P, 3, 2]), sb2("row_sum", [P, 3, 2]), sb2("row_scale", [P, 3, 2])
                pts = sb2("probs_T", [P, 2, 3 * P])
                pt = [st.enter_context(nc.psum_tensor(f"at{i}", [P, 512], F32)) for i in range(8)]
                ld_ac, pos_d, pos_a, kc_ok, pre_tr, pre_tk, csc, cexp_in, cexp, pc_ok, pc_tr, pct_ok = (
                    sem("h_" + n) for n in ("ld", "pos_d", "pos_a", "kc", "pre_tr", "pre_tk", "csc", "cexp_in", "cexp", "pc", "pc_tr", "pct"))
                score_done, soft_done, ex_done, wgt_ok, scaled, tr_ok, pts_ok, pv_ok, ot_ok = (
                    sem("u_" + n) for n in ("score", "soft", "exp", "wgt", "scaled", "tr", "pts", "pv", "ot"))
                NU = 4 * KD

                def unit(u):
                    i, half, v = u // 4, (u // 2) % 2, u % 2
                    return i, 64 * half, v, 8 * (i // 4) + i % 4 + 4 * half, 2 * (i // 4) + half

                with nc.Block() as block:
                    @block.sync
                    def _(sp):
                        for dst, n in ((dm, "dist_masked"), (cbias, "cmp_bias"), (cmask, "cmp_mask")):
                            sp.dma_start(dst[:], I[n]).then_inc(ld_ac, 16)
                        store(sp, O["kv"], kvT[:])
                        w = I["nsa_w_out"].rearrange("(k p) n -> p k n", p=P)
                        for c in range(2):
                            load_chunk(sp, c, w[:, :, c * 512:(c + 1) * 512])

                    @block.gpsimd
                    def _(pool):
                        for u in range(NU):
                            pool.wait_ge(wgt_ok, u + 1)
                            s = sbuf[:, u % 3, :]
                            nc.gpsimd.tensor_scalar(s[:, 0:P], s[:, 0:P], wgt[:, u % 3, 0:1], None, ALU.mult).then_inc(scaled, 1)
                            nc.gpsimd.tensor_scalar(s[:, P:3 * P], s[:, P:3 * P], wgt[:, u % 3, 1:2], None, ALU.mult).then_inc(scaled, 1)

                    @block.tensor
                    def _(pe):
                        tr, mm = nc.tensor.transpose, nc.tensor.matmul
                        vt = (V_SEL, V_SEL + 1, V_WIN, V_WIN + 1)
                        for q in range(QT):
                            for a, t in enumerate(vt):
                                last = tr(pt[q][:, a * P:(a + 1) * P], kvT[:, t, q * P:(q + 1) * P], ident[:])
                            last.then_inc(pre_tr, 1)
                        for a, t in enumerate(vt):
                            last = tr(pt[2][0:DB, a * P:(a + 1) * P], kvT[:, t, SEQ:T], ident[:])
                        last.then_inc(pre_tr, 1)
                        for q in range(QT):
                            last = tr(pt[3][:, q * 48:(q + 1) * 48], gT_[:, q * P:(q + 1) * P], ident[0:48, 0:48])
                        last.then_inc(pre_tr, 1)
                        pe.wait_ge(kc_ok, 1)
                        for i in range(KD):
                            for half in range(2):
                                r, h = slice(64 * half, 64 * half + 64), 8 * (i // 4) + i % 4 + 4 * half
                                for q in range(QT):
                                    last = mm(pt[4 + half][:, (q * AH + h) * 4:(q * AH + h) * 4 + 4], qT[r, i, q * P:(q + 1) * P], kc[r, i // 4, :], start=True, stop=True)
                        last.then_inc(csc, 1)
                        pe.wait_ge(kc_ok, 2)
                        pe.wait_ge(pre_tk, 1)
                        for i in range(KD):
                            last = tr(pt[6 * (i // 4)][0:64, (i % 4) * P:(i % 4 + 1) * P], vx[:, i * 64:(i + 1) * 64], ident[:])
                        last.then_inc(pre_tr, 1)
                        pe.wait_ge(pc_ok, 1)
                        for q in range(QT):
                            last = tr(pt[7][0:64, q * P:(q + 1) * P], pc[:, q].rearrange("p h n -> p (h n)"), ident[:])
                        last.then_inc(pc_tr, 1)
                        pe.wait_ge(pct_ok, 1)
                        pe.wait_ge(pre_tk, 5)

                        def score(u):
                            i, lo, v, h, kv = unit(u)
                            if u >= 2:
                                pe.wait_ge(soft_done, 2 * (u - 1))
                            r, kt = slice(lo, lo + 64), (K_WIN if v else K_SEL) + i // 4
                            mm(pt[u % 2][:, 0:P], qT[r, i, 0:P], kvT[r, kt, 0:P], start=True, stop=True)
                            mm(pt[u % 2][:, P:3 * P], qT[r, i, P:SEQ], kvT[r, kt, 0:SEQ], start=True, stop=True).then_inc(score_done, 1)

                        def turn(u):
                            pe.wait_ge(scaled, 2 * u + 2)
                            if u >= 2:
                                pe.wait_ge(pts_ok, u - 1)
                            for a in range(3):
                                last = tr(pt[2 + u % 2][:, a * P:(a + 1) * P], sbuf[:, u % 3, a * P:(a + 1) * P], ident[:])
                            last.then_inc(tr_ok, 1)

                        def values(u):
                            i, lo, v, h, kv = unit(u)
                            ob = pt[4 + i % 2]
                            if u % 4 == 0:
                                if i >= 2:
                                    pe.wait_ge(ot_ok, i - 1)
                                mm(ob[:, 0:SEQ], vci[:, i, :], pct[:], start=True, stop=False, skip_group_check=True)
                            pe.wait_ge(pts_ok, u + 1)
                            vw = slice(v * 256 + kv * 64, v * 256 + kv * 64 + 64)
                            mm(ob[lo:lo + 64, 0:SEQ], vtok[:, 0, vw], pts[:, u % 2, 0:SEQ], start=False, stop=False, skip_group_check=True)
                            mm(ob[lo:lo + 64, P:SEQ], vtok[:, 1, vw], pts[:, u % 2, SEQ:3 * P], start=False, stop=u % 4 >= 1, skip_group_check=True).then_inc(pv_ok, 1)

                        score(0)
                        score(1)
                        for u in range(NU):
                            turn(u)
                            if u + 2 < NU:
                                score(u + 2)
                            if u >= 1:
                                values(u - 1)
                        values(NU - 1)

                    @block.scalar
                    def _(act):
                        A_ = nc.scalar.activation
                        act.wait_ge(pos_d, 1)
                        A_(wb[:], wb[:], ACT.Exp).then_inc(pos_a, 1)
                        act.wait_ge(cexp_in, 1)
                        A_(pc[:], pc[:], ACT.Exp).then_inc(cexp, 1)

                        def exps(u):
                            act.wait_ge(soft_done, 2 * u + 2)
                            if u >= 3:
                                act.wait_ge(wgt_ok, u - 2)
                            s = sbuf[:, u % 3, :]
                            A_(s[:, 0:P], s[:, 0:P], ACT.Exp, bias=nm[:, u % 3, 0:1], accum_out=sm[:, u % 3, 0:1]).then_inc(ex_done, 1)
                            A_(s[:, P:3 * P], s[:, P:3 * P], ACT.Exp, bias=nm[:, u % 3, 1:2], accum_out=sm[:, u % 3, 1:2]).then_inc(ex_done, 1)

                        exps(0)
                        for u in range(NU):
                            if u + 1 < NU:
                                exps(u + 1)
                            act.wait_ge(tr_ok, u + 1)
                            if u >= 2:
                                act.wait_ge(pv_ok, u - 1)
                            A_(pts[:, u % 2, :], pt[2 + u % 2][:, 0:3 * P], ACT.Copy).then_inc(pts_ok, 1)

                    @block.vector
                    def _(dve):
                        V = nc.vector
                        dve.wait_ge(ld_ptab, 32)
                        dve_step(dve, V.tensor_reduce(wst[:], wb[:], AX.X, ALU.max))
                        V.tensor_tensor(wb[:], wb[:], wst[:].unsqueeze(2).to_broadcast([P, 4, BLK]), ALU.subtract).then_inc(pos_d, 1)
                        dve.wait_ge(pos_a, 1)
                        dve_step(dve, V.tensor_reduce(wst[:], wb[:], AX.X, ALU.add))
                        dve_step(dve, V.reciprocal(wst[:], wst[:]))
                        dve_step(dve, V.tensor_tensor(wb[:], wb[:], wst[:].unsqueeze(2).to_broadcast([P, 4, BLK]), ALU.mult))
                        for a in range(4):
                            i1 = V.tensor_tensor(ctmp[:, a, :].rearrange("p (n l) -> p n l", l=BLK), kvT[:, a, 0:SEQ].rearrange("p (n l) -> p n l", l=BLK),
                                                 wb[:, a:a + 1, :].to_broadcast([P, 4, BLK]), ALU.mult)
                        dve_step(dve, i1)
                        V.tensor_reduce(kc[:].rearrange("p a n -> p (a n)"), ctmp[:].rearrange("p a (n l) -> p (a n) l", l=BLK), AX.X, ALU.add).then_inc(kc_ok, 1)
                        dve_step(dve, V.memset(vx[:], 0.0))
                        dve.wait_ge(kc_ok, 1)
                        for p in range(2):
                            for half in range(2):
                                r, base = slice(64 * half, 64 * half + 64), 288 * p + 16 * half
                                i1 = V.tensor_copy(vx[r, base:base + 272].rearrange("q (r c) -> q r c", c=68)[:, :, 0:4],
                                                   kc[r, 2 + p:3 + p, :].to_broadcast([64, 4, 4]))
                        i1.then_inc(kc_ok, 1)
                        for q in range(QT):
                            dve.wait_ge(pre_tr, q + 1)
                            V.tensor_copy(vtok[:, q, :], pt[q][:]).then_inc(pre_tk, 1)
                        dve.wait_ge(pre_tr, 3)
                        V.tensor_copy(vnew[:], pt[2][0:DB, :]).then_inc(pre_tk, 1)
                        dve.wait_ge(pre_tr, 4)
                        dve_step(dve, V.tensor_copy(gtok[:], pt[3][:, 0:96].rearrange("p (q c) -> p q c", q=QT)))
                        dve.wait_ge(csc, 1)
                        dve.wait_ge(ld_ac, 48)
                        f = lambda t: t[:].rearrange("p q h n -> p (q h) n")
                        g = lambda t: t[:].rearrange("p q h -> p (q h)")
                        bc = g(pst).unsqueeze(2).to_broadcast([P, QT * AH, 4])
                        e = lambda t, half: t.rearrange("p (a f c) -> p a f c", f=2, c=16)[:, :, half, :]
                        w = lambda t: t[:].rearrange("p q h n -> p (q h n)")
                        V.tensor_tensor(e(w(pc), 0), e(pt[4][:, 0:QT * AH * 4], 0), e(w(cbias), 0), ALU.add)
                        dve_step(dve, V.tensor_tensor(e(w(pc), 1), e(pt[5][:, 0:QT * AH * 4], 1), e(w(cbias), 1), ALU.add))
                        dve_step(dve, V.tensor_reduce(g(pst), f(pc), AX.X, ALU.max))
                        V.tensor_tensor(f(pc), f(pc), bc, ALU.subtract).then_inc(cexp_in, 1)
                        dve.wait_ge(cexp, 1)
                        dve_step(dve, V.tensor_tensor(f(pc), f(pc), f(cmask), ALU.mult))
                        dve_step(dve, V.tensor_reduce(g(pst), f(pc), AX.X, ALU.add))
                        dve_step(dve, V.tensor_scalar(g(pst), g(pst), 1e-30, None, ALU.max))
                        dve_step(dve, V.reciprocal(g(pst), g(pst)))
                        g3 = gtok[:].rearrange("p q (h c) -> p q h c", c=3)
                        dve_step(dve, V.tensor_tensor(pst[:], pst[:], g3[:, :, :, 0], ALU.mult))
                        V.tensor_tensor(f(pc), f(pc), bc, ALU.mult).then_inc(pc_ok, 1)
                        dve.wait_ge(pre_tr, 5)
                        for a in range(2):
                            i1 = V.tensor_copy(vci[:, 4 * a:4 * a + 4, :], pt[6 * a][0:64, :].rearrange("p (i m) -> p i m", i=4))
                        i1.then_inc(pre_tk, 1)
                        dve.wait_ge(pc_tr, 1)
                        V.tensor_copy(pct[:], pt[7][0:64, 0:SEQ]).then_inc(pre_tk, 1)
                        dve.wait_ge(pre_tk, 5)
                        dve_step(dve, V.memset(wgt[:], 0.0))
                        V.tensor_copy(nm[:], wgt[:]).then_inc(pct_ok, 1)
                        dve.wait_ge(pct_ok, 1)

                        def soft(u):
                            i, lo, v, h, kv = unit(u)
                            dve.wait_ge(score_done, u + 1)
                            if u >= 3:
                                dve.wait_ge(tr_ok, u - 2)
                            s = sbuf[:, u % 3, :]
                            dve_step(dve, V.scalar_tensor_tensor(s, dm[:], -2.0 ** (-8.0 * (h + 1) / AH), pt[u % 2][:, 0:3 * P], ALU.mult, ALU.add))
                            V.tensor_reduce(nm[:, u % 3, 0:1], s[:, 0:P], AX.X, ALU.max, negate=True).then_inc(soft_done, 1)
                            V.tensor_reduce(nm[:, u % 3, 1:2], s[:, P:3 * P], AX.X, ALU.max, negate=True).then_inc(soft_done, 1)

                        def scale(u):
                            i, lo, v, h, kv = unit(u)
                            dve.wait_ge(ex_done, 2 * u + 2)
                            if u >= 3:
                                dve.wait_ge(scaled, 2 * (u - 2))
                            dve_step(dve, V.reciprocal(wgt[:, u % 3, :], sm[:, u % 3, :]))
                            V.tensor_tensor(wgt[:, u % 3, :], wgt[:, u % 3, :], g3[:, :, h, 1 + v], ALU.mult).then_inc(wgt_ok, 1)

                        def out_tile(i):
                            dve.wait_ge(pv_ok, 4 * i + 4)
                            V.tensor_copy(oT[:, i, 0:SEQ], pt[4 + i % 2][:, 0:SEQ]).then_inc(ot_ok, 1)

                        soft(0)
                        for u in range(NU):
                            if u + 1 < NU:
                                soft(u + 1)
                            scale(u)
                            if u >= 5 and (u - 5) % 4 == 0:
                                out_tile((u - 5) // 4)
                        out_tile(KD - 1)

            with ExitStack() as st:
                cpg = st.enter_context(nc.sbuf_tensor("cmp_pages", [P, 2, NPG, 4, PAGE], F32))
                pv = [st.enter_context(nc.psum_tensor(f"vc{i}", [P, 512], F32)) for i in range(4)]
                ld_c, c_used, c_tr = [sem("c_ld0"), sem("c_ld1")], sem("c_used"), sem("c_tr")
                with nc.Block() as block:
                    @block.sync
                    def _(sp):
                        sp.wait_ge(ld_ptab, 32)
                        for b in range(DB):
                            if b >= 2:
                                sp.wait_ge(c_used, b - 1)
                            for n in range(NPG):
                                page = sp.value_load(ptab[0:1, b * NPG + n:b * NPG + n + 1], min_val=0, max_val=I["cmp_pages"].shape[0] - 1)
                                sp.dma_start(cpg[:, b % 2, n], I["cmp_pages"][bass.ds(page, 1)].rearrange("a p c t -> (a p) c t")).then_inc(ld_c[b % 2], 16)

                    @block.vector
                    def _(dve):
                        V = nc.vector
                        for b in range(DB):
                            dve.wait_ge(ld_c[b % 2], 16 * NPG * (b // 2 + 1))
                            for a in range(4):
                                x = cpg[:, b % 2, :, a, :].rearrange("p n (c l) -> p n c l", l=BLK)
                                i1 = V.tensor_tensor(x, x, wb[:, a:a + 1, :].unsqueeze(1).to_broadcast([P, NPG, 2, BLK]), ALU.mult)
                            dve_step(dve, i1)
                            for a in range(4):
                                x = cpg[:, b % 2, :, a, :].rearrange("p n (c l) -> p n c l", l=BLK)
                                i1 = V.tensor_reduce(kcd[:, a, b, :].rearrange("p (n c) -> p n c", c=2), x, AX.X, ALU.add)
                            i1.then_inc(c_used, 1)
                        dve.wait_ge(c_tr, 1)
                        for n in range(4):
                            V.tensor_copy(vcd[:, 2 * n:2 * n + 2, :].rearrange("p b d -> p (b d)"), pv[n][0:NBP, :])

                    @block.tensor
                    def _(pe):
                        pe.wait_ge(c_used, DB)
                        for b in range(DB):
                            for p in range(2):
                                last = nc.tensor.transpose(pv[b // 2][0:NBP, ((b % 2) * 2 + p) * P:((b % 2) * 2 + p + 1) * P], kcd[:, 2 + p, b, :], ident[:])
                        last.then_inc(c_tr, 1)

            with ExitStack() as st:
                def sb2(name, shape, dt=F32):
                    return st.enter_context(nc.sbuf_tensor(name, shape, dt))

                qbd = ring[:, 1, 2 * CH:2 * CH + 2 * DB * 144].rearrange("p (a c) -> p a c", a=2)
                kvb = sb2("kv_ring", [P, 2, 3072])
                biasd, biasw, cbd, g4, idx, mb = (sb2(n, s) for n, s in (("bias_dec", [P, PAST]), ("bias_win", [P, WIN]), ("bias_cmp", [P, NBP]),
                                                                       ("same_group", [P, P]), ("block_idx", [P, NBP]), ("batch_mask", [P, DB])))
                gmask, gsel = sb2("gate_mask", [48, AH]), sb2("gate_sel", [48, 3])
                gl = sb2("gate_spread", [48, DB, AH])
                gd = sb2("gate_dec", [P, 3])
                ss, sw = sb2("s_sel", [P, PAST + 1]), sb2("s_win", [P, WIN + 1])
                sc, pcn, nb, tmp = sb2("s_cmp", [P, NBP]), sb2("p_cmp", [P, NBP]), sb2("block_bias", [P, NBP]), sb2("imp_tmp", [P, NBP])
                nmx, sums, rcp, ex_ = sb2("d_negmax", [P, 3]), sb2("d_sum", [P, 3]), sb2("d_rcp", [P, 3]), sb2("excluded", [P, 2])
                pnd = sb2("p_new_diag", [P, 2, DB])
                ptd = sb2("d_probs_T", [P, 12, P])
                pcd, pnt = sb2("d_pcmp_T", [NBP, P]), sb2("d_pnew_T", [DB, 2, P])
                pt = [st.enter_context(nc.psum_tensor(f"dt{i}", [P, 512], F32)) for i in range(8)]
                ld_dc, kv_used, q_zero, q_ok, gl_ok, s_all, imp_in, imp_ok, to_exp, exped, p_ok, t_ok, t_taken = (
                    sem("d_" + n) for n in ("ldc", "kv_used", "q_zero", "q_ok", "gl", "s_all", "imp_in", "imp", "to_exp", "exped", "p", "t", "tk"))
                ld_kv = [sem("d_ldkv0"), sem("d_ldkv1")]

                with nc.Block() as block:
                    @block.sync
                    def _(sp):
                        cl = (("bias_dec", biasd), ("bias_win", biasw), ("bias_cmp", cbd), ("same_group", g4), ("block_idx", idx), ("batch_mask", mb),
                              ("gate_mask", gmask), ("gate_sel", gsel))
                        for n, (name, dst) in enumerate(cl):
                            sp.dma_start(dst[:], I[name]).then_inc(ld_dc, 16)
                        for n in range(2 * DB):
                            b, s = n % DB, n % 2
                            if n >= 2:
                                sp.wait_ge(kv_used, n - 1)
                            for g in range(NPG):
                                page = sp.value_load(ptab[0:1, b * NPG + g:b * NPG + g + 1], min_val=0, max_val=I["cmp_pages"].shape[0] - 1)
                                src = I["ksel_pages" if n < DB else "vsel_pages"][bass.ds(page, 1)].rearrange("a p c -> (a p) c")
                                sp.dma_start(kvb[:, s, g * 256:(g + 1) * 256], src).then_inc(ld_kv[s], 16)
                            src = I["kwin"][b] if n < DB else I["vwin"][b]
                            sp.dma_start(kvb[:, s, 2048:3072].rearrange("p (a c) -> p a c", a=src.shape[1]), src).then_inc(ld_kv[s], 16)

                    @block.gpsimd
                    def _(pool):
                        nc.gpsimd.memset(qbd, 0.0).then_inc(q_zero, 1)

                    @block.tensor
                    def _(pe):
                        tr, mm = nc.tensor.transpose, nc.tensor.matmul
                        pe.wait_ge(q_ok, 1)
                        for b in range(DB):
                            pe.wait_ge(ld_kv[b % 2], 16 * (NPG + 1) * (b // 2 + 1))
                            k3 = kvb[:, b % 2, 0:2048].rearrange("p (g c t) -> p g c t", g=NPG, c=2)
                            kw = kvb[:, b % 2, 2048:3072].rearrange("p (c t) -> p c t", c=2)
                            for p in range(2):
                                q = qbd[:, p, b * P:(b + 1) * P]
                                st_, sp_ = b == 0 and p == 0, b == DB - 1 and p == 1
                                for a in range(2):
                                    mm(pt[a][:], q, k3[:, 4 * a:4 * a + 4, p, :], start=st_, stop=sp_)
                                last = mm(pt[2][:], q, kw[:, p, :], start=st_, stop=sp_)
                            last.then_inc(kv_used, 1)
                        for col, n, key in ((0, 1, lambda b, p: kvT[:, K_SEL + p, SEQ + b:SEQ + b + 1]), (1, 1, lambda b, p: kvT[:, K_WIN + p, SEQ + b:SEQ + b + 1]),
                                            (2, NBP, lambda b, p: kcd[:, p, b, :])):
                            for b in range(DB):
                                for p in range(2):
                                    mm(pt[3][:, col:col + n], qbd[:, p, b * P:(b + 1) * P], key(b, p), start=b == 0 and p == 0, stop=b == DB - 1 and p == 1)
                        pe.wait_ge(gl_ok, 1)
                        mm(pt[3][:, 18:21], gl[:].rearrange("k b h -> k (b h)"), gsel[:], start=True, stop=True).then_inc(s_all, 1)
                        pe.wait_ge(imp_in, 1)
                        mm(pt[4][:, 0:NBP], g4[:], pcn[:], start=True, stop=True).then_inc(imp_ok, 1)
                        pe.wait_ge(p_ok, 3)
                        for a in range(8):
                            last = tr(pt[5 * (a // 4)][:, (a % 4) * P:(a % 4 + 1) * P], ss[:, a * P:(a + 1) * P], ident[:])
                        for a in range(4):
                            last = tr(pt[1][:, a * P:(a + 1) * P], sw[:, a * P:(a + 1) * P], ident[:])
                        tr(pt[2][0:NBP, 0:P], sc[:], ident[:])
                        tr(pt[2][0:DB, P:2 * P], pnd[:, 0, :], ident[:])
                        tr(pt[2][0:DB, 2 * P:3 * P], pnd[:, 1, :], ident[:]).then_inc(t_ok, 1)
                        pe.wait_ge(t_taken, 1)
                        for p in range(2):
                            for v in range(2):
                                mm(pt[6 + p][:, 0:P], vnew[:, v * 256 + p * P:v * 256 + (p + 1) * P], pnt[:, v, :], start=v == 0, stop=False, skip_group_check=True)
                        for b in range(DB):
                            n = DB + b
                            pe.wait_ge(ld_kv[n % 2], 16 * (NPG + 1) * (n // 2 + 1))
                            v3 = kvb[:, n % 2, :].rearrange("p (g c) -> p g c", c=256)
                            for p in range(2):
                                cols = slice(b * AH + 8 * p, b * AH + 8 * p + 8)
                                mm(pt[6 + p][:, cols], vcd[:, b, p * P:(p + 1) * P], pcd[:, cols], start=False, stop=False, skip_group_check=True)
                                for g in range(12):
                                    last = mm(pt[6 + p][:, cols], v3[:, g, p * P:(p + 1) * P], ptd[:, g, cols], start=False, stop=g == 11, skip_group_check=True)
                            last.then_inc(kv_used, 1)

                    @block.scalar
                    def _(act):
                        A_ = nc.scalar.activation
                        act.wait_ge(to_exp, 1)
                        A_(sc[:], sc[:], ACT.Exp, bias=nmx[:, 0:1], accum_out=sums[:, 0:1]).then_inc(exped, 1)
                        act.wait_ge(to_exp, 2)
                        A_(sw[:], sw[:], ACT.Exp, bias=nmx[:, 2:3], accum_out=sums[:, 2:3]).then_inc(exped, 1)
                        act.wait_ge(to_exp, 3)
                        A_(ss[:], ss[:], ACT.Exp, bias=nmx[:, 1:2], accum_out=sums[:, 1:2]).then_inc(exped, 1)

                    @block.vector
                    def _(dve):
                        V = nc.vector
                        dve.wait_ge(q_zero, 1)
                        for p in range(2):
                            for half in range(2):
                                r = slice(64 * half, 64 * half + 64)
                                i1 = V.tensor_copy(qbd[r, p, :].rearrange("q (b c) -> q b c", c=144)[:, :, 8 * p + 4 * half:8 * p + 4 * half + 4],
                                                   qT[r, 4 * p:4 * p + 4, SEQ:T].rearrange("q r b -> q b r"))
                        i1.then_inc(q_ok, 1)
                        dve.wait_ge(ld_dc, 16 * 8)
                        V.tensor_tensor(gl[:], gT_[:, SEQ:T].unsqueeze(2).to_broadcast([48, DB, AH]), gmask[:].unsqueeze(1).to_broadcast([48, DB, AH]), ALU.mult).then_inc(gl_ok, 1)
                        dve.wait_ge(s_all, 1)
                        V.tensor_copy(gd[:], pt[3][:, 18:21])
                        dve_step(dve, V.tensor_tensor(sc[:], pt[3][:, 2:2 + NBP], cbd[:], ALU.add))
                        V.tensor_reduce(nmx[:, 0:1], sc[:], AX.X, ALU.max, negate=True).then_inc(to_exp, 1)
                        V.tensor_tensor(sw[:, 0:WIN], pt[2][:], biasw[:], ALU.add)
                        dve_step(dve, V.tensor_copy(sw[:, WIN:WIN + 1], pt[3][:, 1:2]))
                        V.tensor_reduce(nmx[:, 2:3], sw[:], AX.X, ALU.max, negate=True).then_inc(to_exp, 1)
                        V.tensor_copy(ss[:, PAST:PAST + 1], pt[3][:, 0:1])
                        V.tensor_tensor(ss[:, 0:512], pt[0][:], biasd[:, 0:512], ALU.add)
                        dve_step(dve, V.tensor_tensor(ss[:, 512:PAST], pt[1][:], biasd[:, 512:PAST], ALU.add))
                        dve.wait_ge(exped, 1)
                        dve_step(dve, V.reciprocal(rcp[:, 0:1], sums[:, 0:1]))
                        V.tensor_scalar(pcn[:], sc[:], rcp[:, 0:1], None, ALU.mult).then_inc(imp_in, 1)
                        dve.wait_ge(imp_in, 1)
                        V.tensor_scalar(sc[:], pcn[:], gd[:, 0:1], None, ALU.mult).then_inc(p_ok, 1)
                        dve.wait_ge(imp_ok, 1)
                        dve_step(dve, V.tensor_copy(tmp[:], pt[4][:, 0:NBP]))
                        dve_step(dve, V.tensor_reduce(ex_[:, 0:1], tmp[:, 1:NBP], AX.X, ALU.min))
                        dve_step(dve, V.tensor_scalar(nb[:], tmp[:], ex_[:, 0:1], None, ALU.is_equal))
                        dve_step(dve, V.tensor_tensor(nb[:], nb[:], idx[:], ALU.mult))
                        dve_step(dve, V.tensor_reduce(ex_[:, 1:2], nb[:, 1:NBP], AX.X, ALU.max))
                        dve_step(dve, V.tensor_scalar(nb[:], idx[:], ex_[:, 1:2], NEG, ALU.is_equal, ALU.mult))
                        s3 = ss[:, 0:PAST].rearrange("p (n l) -> p n l", l=BLK)
                        dve_step(dve, V.tensor_tensor(s3, s3, nb[:].unsqueeze(2).to_broadcast([P, NBP, BLK]), ALU.add))
                        V.tensor_reduce(nmx[:, 1:2], ss[:], AX.X, ALU.max, negate=True).then_inc(to_exp, 1)
                        for n, (x, v) in enumerate(((sw, 2), (ss, 1))):
                            dve.wait_ge(exped, 2 + n)
                            dve_step(dve, V.reciprocal(rcp[:, v:v + 1], sums[:, v:v + 1]))
                            dve_step(dve, V.tensor_tensor(rcp[:, v:v + 1], rcp[:, v:v + 1], gd[:, v:v + 1], ALU.mult))
                            dve_step(dve, V.tensor_scalar(x[:], x[:], rcp[:, v:v + 1], None, ALU.mult))
                            V.tensor_scalar(pnd[:, v - 1, :], mb[:], x[:, x.shape[1] - 1:x.shape[1]], None, ALU.mult).then_inc(p_ok, 1)
                        dve.wait_ge(t_ok, 1)
                        V.tensor_copy(ptd[:, 0:4, :], pt[0][:].rearrange("p (a c) -> p a c", a=4))
                        V.tensor_copy(ptd[:, 4:8, :], pt[5][:].rearrange("p (a c) -> p a c", a=4))
                        V.tensor_copy(ptd[:, 8:12, :], pt[1][:].rearrange("p (a c) -> p a c", a=4))
                        V.tensor_copy(pcd[:], pt[2][0:NBP, 0:P])
                        V.tensor_copy(pnt[:], pt[2][0:DB, P:3 * P].rearrange("p (a c) -> p a c", a=2)).then_inc(t_taken, 1)
                        dve.wait_ge(kv_used, 2 * DB)
                        for p in range(2):
                            for half in range(2):
                                r = slice(64 * half, 64 * half + 64)
                                V.tensor_copy(oT[r, 4 * p:4 * p + 4, SEQ:T],
                                              pt[6 + p][r, 0:P].rearrange("q (b c) -> q b c", c=AH)[:, :, 8 * p + 4 * half:8 * p + 4 * half + 4].rearrange("q b r -> q r b"))

            with ExitStack() as st:
                bank = [st.enter_context(nc.psum_tensor(f"no{i}", [P, 512], F32)) for i in range(4)]
                o_done, o_taken = sem("no_done"), sem("no_taken")
                base = [16 * c for c in chunk_count]
                with nc.Block() as block:
                    @block.tensor
                    def _(pe):
                        for m in range(KD):
                            if m % 4 == 0:
                                pe.wait_ge(ld_chunk[m // 4], base[m // 4] + 16)
                            if m >= 4:
                                pe.wait_ge(o_taken, m - 3)
                            wc = chunk[m // 4].rearrange("p (k n) -> p k n", k=KD)
                            for k in range(KD):
                                last = nc.tensor.matmul(bank[m % 4][:, 0:T], wc[:, k, (m % 4) * P:(m % 4 + 1) * P], oT[:, k, :], start=k == 0, stop=k == KD - 1)
                            last.then_inc(o_done, 1)

                    @block.vector
                    def _(dve):
                        for m in range(KD):
                            dve.wait_ge(o_done, m + 1)
                            nc.vector.scalar_tensor_tensor(xT[:, m, :], xT[:, m, :], ALPHA, bank[m % 4][:, 0:T], ALU.mult, ALU.add).then_inc(o_taken, 1)

                    @block.sync
                    def _(sp):
                        sp.wait_ge(stored, n_stored[0])
                for c in range(2):
                    chunk_count[c] += 1

        tail(1, out=O["y"])
        with nc.Block() as block:
            @block.sync
            def _(sp):
                sp.wait_ge(stored, n_stored[0])


def consts():
    c = {}
    r = np.arange(P)
    c["ident"] = np.eye(P, dtype=np.float32)
    c["ones"] = np.ones((P, P), np.float32)
    tri = (r[:, None] <= r[None, :]).astype(np.float32)
    c["m384"] = np.concatenate([tri, c["ones"], tri], 1)
    c["eps"] = np.full((P, 1), EPS, np.float32)
    c["slot_numbers"] = np.ascontiguousarray(np.broadcast_to(np.arange(1, 65, dtype=np.float32), (P, 64)))
    i4 = np.arange(EG)
    c["lower4"] = np.ascontiguousarray(np.broadcast_to((i4[None, :] < i4[:, None]).astype(np.float32), (P, EG, EG)))
    c["hsel"] = np.repeat(np.eye(NH, dtype=np.float32), HD, axis=1)
    slope = 2.0 ** (-8.0 * np.arange(1, AH + 1) / AH)
    f32 = lambda a: np.ascontiguousarray(a, np.float32)
    far = lambda d: np.where(d >= 0, d, 1e33)
    c["dist_masked"] = f32(np.concatenate([far(r[:, None] - r[None, :]), far(P + r[:, None] - np.arange(SEQ)[None, :])], 1))
    d = (np.arange(QT)[None, :, None] * P + r[:, None, None] - ((np.arange(4) + 1) * BLK - 1)).astype(float)[:, :, None, :]
    c["cmp_mask"] = f32(np.broadcast_to(d >= 0, (P, QT, AH, 4)))
    c["cmp_bias"] = f32(np.where(d >= 0, -slope[None, None, :, None] * d, NEG))
    sl = slope[r % AH][:, None]
    pos = np.arange(PAST)[None, :]
    c["bias_dec"] = f32(-sl * (PAST - pos))
    c["bias_win"] = f32(np.where(np.arange(WIN) >= 1, -sl * (WIN - np.arange(WIN)), NEG))
    c["bias_cmp"] = f32(-sl * (PAST - ((np.arange(NBP) + 1) * BLK - 1)))
    c["same_group"] = f32(r[:, None] // REP == r[None, :] // REP)
    c["block_idx"] = f32(np.broadcast_to(np.arange(NBP), (P, NBP)))
    c["batch_mask"] = f32(r[:, None] // AH == np.arange(DB))
    k = np.arange(3 * AH)[:, None]
    c["gate_mask"], c["gate_sel"] = f32(k // 3 == np.arange(AH)), f32(k % 3 == np.arange(3))
    return c


def kernel(x_prompt, x_sample, state_ssm, state_conv, cache_kv, cache_win, page_table, p_prompt, p_sample,
           ssd_w_in, ssd_conv_w, ssd_conv_b, ssd_dt_bias, ssd_a_log, ssd_d, ssd_norm_g, ssd_w_out,
           nsa_w_in, nsa_pos_w, nsa_w_out, ln1_g, ln1_b, ln2_g, ln2_b, router_w, router_bias,
           moe_w_gate, moe_w_up, moe_w_down, ple_proj, ple_gate):
    import concourse.bacc as bacc
    from concourse.bass_utils import run_bass_kernel_spmd

    A = lambda a: np.asarray(a)
    tiles = lambda a: np.moveaxis(A(a).reshape(-1, P, *A(a).shape[1:]), 0, 1)
    cc = np.ascontiguousarray
    ins = consts()
    ins["xT"] = cc(np.concatenate([A(x_prompt)[0], A(x_sample)[:, 0]], 0).T)
    ins["pT"] = cc(np.concatenate([A(p_prompt)[:, 0], A(p_sample)[:, :, 0]], 1).transpose(0, 2, 1))
    ins["state_ssm"] = A(state_ssm)[0].reshape(DB, DI, NS)
    ins["conv_state"] = cc(tiles(A(state_conv)[0].transpose(2, 1, 0)))
    ins["conv_params"] = cc(tiles(np.concatenate([A(ssd_conv_w)[0], A(ssd_conv_b)], 0).T))
    ins["heads"] = cc(np.stack([A(ssd_dt_bias)[0], A(ssd_a_log)[0], A(ssd_d)[0]], 1))
    ins["norm_g"] = cc(tiles(A(ssd_norm_g)[0]))
    ins["lnp"] = cc(np.stack([A(ln1_g), A(ln1_b), A(ln2_g), A(ln2_b)], 1).reshape(2, 4, KD, P).transpose(3, 0, 1, 2))
    ins["router_w"] = cc(tiles(router_w))
    ins["router_bias"] = cc(np.broadcast_to(A(router_bias), (P, NE)))
    ins["ssd_w_in"], ins["ssd_w_out"] = A(ssd_w_in)[0], A(ssd_w_out)[0]
    for n, w in (("moe_w_gate", moe_w_gate), ("moe_w_up", moe_w_up), ("moe_w_down", moe_w_down)):
        ins[n] = A(w).reshape(2 * NE, *w.shape[2:])
    ins["ple_proj"], ins["ple_gate"] = A(ple_proj), A(ple_gate)
    order = [8 * (i // 4) + i % 4 + 4 * half for i in range(KD) for half in range(2)]
    cols = np.concatenate([np.arange(h * 64, h * 64 + 64) for h in order])
    w = A(nsa_w_in)[0]
    ins["nsa_w_in"] = np.concatenate([w[:, cols], w[:, D:]], 1)
    ins["nsa_w_out"] = A(nsa_w_out)[0][cols]
    pw = A(nsa_pos_w)[0].transpose(0, 2, 1).reshape(4, 2, BLK)
    ins["pos_w"] = cc(np.repeat(pw.transpose(1, 0, 2), 64, axis=0))
    ins["page_table"] = A(page_table).reshape(1, -1)
    kv = A(cache_kv)[0].reshape(-1, PAGE, 4, 256)
    ins["cmp_pages"] = cc(kv[:, :, 0:2].reshape(-1, PAGE, 4, P).transpose(0, 3, 2, 1))
    ins["ksel_pages"] = cc(kv[:, :, 2].reshape(-1, PAGE, 2, P).transpose(0, 3, 2, 1)).reshape(-1, P, 256)
    ins["vsel_pages"] = cc(kv[:, :, 3])
    cw = A(cache_win)[0].reshape(DB, WIN, 2, 256)
    ins["kwin"] = cc(cw[:, :, 0].reshape(DB, WIN, 2, P).transpose(0, 3, 2, 1))
    ins["vwin"] = cc(cw[:, :, 1].reshape(DB, 4, P, 256).transpose(0, 2, 1, 3))
    ins["cache_win"] = cw.reshape(DB, WIN, 512)

    outs = {"conv_prompt": (P, JC, 3), "conv_sample": (P, JC, 3, DB), "ssm_prompt": (DI, NS), "ssm_sample": (DB, DI, NS), "y": (P, KD, T)}
    outs |= {"kv": (P, KVT, T), "win_old": (DB, WIN - 1, 512)}
    nc = bacc.Bacc("TRN2", target_bir_lowering=False, num_devices=1)
    I = {n: nc.dram_tensor("in_" + n, a.shape, mybir.dt.from_np(a.dtype), kind="ExternalInput").ap() for n, a in ins.items()}
    O = {n: nc.dram_tensor("out_" + n, s, F32, kind="ExternalOutput").ap() for n, s in outs.items()}
    trunk(nc, I, O)
    r = run_bass_kernel_spmd(nc, [{"in_" + n: a for n, a in ins.items()}], core_ids=[0]).results[0]
    o = {n: A(r["out_" + n]) for n in outs}
    feat = lambda a: np.moveaxis(a, 1, 0).reshape(-1, *a.shape[2:])
    y = feat(o["y"]).T
    conv_p = feat(o["conv_prompt"]).T[None, None]
    conv_s = feat(o["conv_sample"]).transpose(2, 1, 0)[None]
    ssm_p = o["ssm_prompt"].reshape(1, 1, NH, HD, NS)
    ssm_s = o["ssm_sample"].reshape(1, DB, NH, HD, NS)
    kvo = feat(o["kv"]).T.reshape(T, 6, AKV, 64)
    win_s = np.concatenate([o["win_old"].reshape(DB, WIN - 1, 2, AKV, 64), kvo[SEQ:, None, 4:6]], 1)
    return (y[None, :SEQ], y[SEQ:, None], ssm_p, conv_p, kvo[None, None, :SEQ, 0:4], kvo[None, None, :SEQ, 4:6],
            ssm_s, conv_s, kvo[None, SEQ:, None, 0:4], win_s[None])
```

```python
from contextlib import ExitStack

import numpy as np

import concourse.bass as bass
from concourse import mybir

F32 = mybir.dt.float32
I32 = mybir.dt.int32
ALU = mybir.AluOpType
ACT = mybir.ActivationFunctionType
AX = mybir.AxisListType

P = 128
D = 1024
KD = D // P
SEQ = 256
DB = 8
T = SEQ + DB
QT = SEQ // P
DI, HD, NH, NG, NS, NCONV = 2048, 64, 32, 4, 128, 4
CD = DI + 2 * NG * NS
JX = DI // P
JC = CD // P
AH, AKV, REP, BLK, WIN, PAST, PAGE = 16, 4, 4, 64, 512, 1024, 128
NPG = PAST // PAGE
NBP = PAST // BLK
QS = 64 ** -0.5
KVT = 6 * AKV * 64 // P
NE, FF, EG = 16, 512, 4
CH = 4096
ALPHA = 4.0 ** 0.25
EPS = 1e-5
NEG = -1e30


class Chain:

    def __init__(self, sem):
        self.sem, self.n = sem, 0

    def __call__(self, eng, ins):
        self.n += 1
        ins.then_inc(self.sem, 1)
        eng.wait_ge(self.sem, self.n)


def trunk(nc, I, O):
    root = ExitStack()
    with root:
        def sem(name):
            return root.enter_context(nc.semaphore(name))

        def keep(name, shape, dt=F32):
            return root.enter_context(nc.sbuf_tensor(name, shape, dt))

        ring = keep("expert_ring", [P, 2, 3 * CH])
        xT = keep("xT", [P, KD, T])
        ident = keep("ident", [P, P])
        ones = keep("ones", [P, P])
        m384 = keep("m384", [P, 3 * P])
        lnp = keep("lnp", [P, 2, 4, KD])
        rw = keep("router_w", [P, KD, NE])
        rbias = keep("router_bias", [P, NE])
        epst = keep("eps", [P, 1])
        lower4 = keep("lower4", [P, EG, EG])
        iota64 = keep("slot_numbers", [P, 64])
        wb = keep("pos_softmax", [P, 4, BLK])
        wst = keep("pos_stat", [P, 4])
        kcd = keep("cmp_dec", [P, 4, DB, NBP])
        ptab = keep("page_table", [1, DB * NPG], I32)
        dve_step, act_step, pool_step = (Chain(sem(n)) for n in ("dve_step", "act_step", "pool_step"))
        ld_const, ld_wg, ld_wu, ld_wd = sem("ld_const"), [sem("ld_wg0"), sem("ld_wg1")], \
            [sem("ld_wu0"), sem("ld_wu1")], [sem("ld_wd0"), sem("ld_wd1")]
        ld_chunk = [sem("ld_chunk0"), sem("ld_chunk1"), sem("ld_chunk2")]
        chunk_count = [0, 0, 0]
        stored = sem("stored")
        n_stored = [0]

        chunk = [ring[:, 1, c * CH:(c + 1) * CH] for c in range(3)]

        def load_chunk(sp, c, src):
            n = 1
            for v in src.shape[1:]:
                n *= v
            sp.dma_start(chunk[c][0:src.shape[0], 0:n].rearrange("p (a b) -> p a b", b=src.shape[2]), src)\
              .then_inc(ld_chunk[c], 16)

        def store(eng, dst, src):
            n_stored[0] += 16
            eng.dma_start(dst, src).then_inc(stored, 16)

        def load_expert(sp, e, s):
            g = lambda w, k: w[bass.ds(e, 1)].rearrange("a (k p) n -> p (a k) n", p=P)
            sp.dma_start(ring[:, s, 0:CH].rearrange("p (k n) -> p k n", k=KD), g(I["moe_w_gate"], KD)).then_inc(ld_wg[s], 16)
            sp.dma_start(ring[:, s, CH:2 * CH].rearrange("p (k n) -> p k n", k=KD), g(I["moe_w_up"], KD)).then_inc(ld_wu[s], 16)
            sp.dma_start(ring[:, s, 2 * CH:3 * CH].rearrange("p (k n) -> p k n", k=FF // P), g(I["moe_w_down"], 4)).then_inc(ld_wd[s], 16)

        with ExitStack() as ssd:
            def sb(name, shape, dt=F32):
                return ssd.enter_context(nc.sbuf_tensor(name, shape, dt))

            zs = sb("z", [P, JX, T])
            cv = sb("conv_out", [P, JC, T])
            dtr = sb("dt_raw", [NH, T])
            heads = sb("head_params", [NH, 3])
            normg = sb("norm_g", [P, JX])

            zw = [ring[:, 0, c * CH:(c + 1) * CH].rearrange("p (k n) -> p k n", k=KD) for c in range(3)]
            ld_z = [sem(f"ld_z{c}") for c in range(3)]
            w_in = I["ssd_w_in"].rearrange("(k p) n -> p k n", p=P)
            with ExitStack() as st:
                raw = st.enter_context(nc.sbuf_tensor("xbc_raw", [P, 2, SEQ + 3], F32))
                taps = st.enter_context(nc.sbuf_tensor("taps", [P, JC, NCONV, DB], F32))
                cacc = st.enter_context(nc.sbuf_tensor("conv_acc", [P, 2, T], F32))
                lastp = st.enter_context(nc.sbuf_tensor("last_prompt", [P, JC, 3], F32))
                convp = st.enter_context(nc.sbuf_tensor("conv_params", [P, JC, NCONV + 1], F32))
                bank = [st.enter_context(nc.psum_tensor(f"pj{i}", [P, 512], F32)) for i in range(8)]
                tile_done, tile_taken, conv_done, silu_done, pads, ld_x, ld_pos, pos_d, pos_a = (
                    sem(n) for n in ("s_tile_done", "s_tile_taken", "s_conv_done", "s_silu_done", "s_pads", "s_ld_x", "s_ld_pos", "s_pos_d", "s_pos_a"))
                NT = JC + 1
                taken = lambda m: 2 * (m + 1)
                nchunk = (NT + 3) // 4

                with nc.Block() as block:
                    @block.sync
                    def _(sp):
                        sp.dma_start(xT[:], I["xT"].rearrange("(k p) t -> p k t", p=P)).then_inc(ld_x, 16)
                        for c in range(nchunk):
                            lo, hi = DI + c * 512, min(DI + c * 512 + 512, w_in.shape[2])
                            if c >= 2:
                                sp.wait_ge(tile_done, 4 * (c - 1))
                            load_chunk(sp, c % 2, w_in[:, :, lo:hi])
                            if c == 0:
                                for dst, name in ((convp[:], "conv_params"), (taps[:, :, 0:3, :], "conv_state"),
                                                  (ident[:], "ident"), (ones[:], "ones"), (m384[:], "m384"), (lnp[:], "lnp"),
                                                  (rw[:], "router_w"), (rbias[:], "router_bias"),
                                                  (epst[:], "eps"), (iota64[:], "slot_numbers"), (lower4[:], "lower4"), (heads[:], "heads"), (normg[:], "norm_g")):
                                    sp.dma_start(dst, I[name]).then_inc(ld_const, 16)
                                sp.dma_start(wb[:], I["pos_w"]).then_inc(ld_pos, 16)
                                sp.dma_start(ptab[:], I["page_table"]).then_inc(ld_pos, 16)
                        for c in range(3):
                            sp.dma_start(zw[c], w_in[:, :, c * 512:(c + 1) * 512]).then_inc(ld_z[c], 16)
                        sp.wait_ge(conv_done, JC)
                        store(sp, O["conv_prompt"], lastp[:])
                        store(sp, O["conv_sample"], taps[:, :, 1:4, :])
                        sp.wait_ge(stored, n_stored[0])

                    @block.tensor
                    def _(pe):
                        pe.wait_ge(ld_x, 16)
                        for m in range(NT):
                            c, s = m // 4, (m // 4) % 2
                            if m % 4 == 0:
                                pe.wait_ge(ld_chunk[s], 16 * (c // 2 + 1))
                            if m >= 8:
                                pe.wait_ge(tile_taken, taken(m - 8))
                            M = P if m < NT - 1 else NH
                            wc = chunk[s][:, 0:KD * (512 if m < NT - 1 else NH)].rearrange("p (k n) -> p k n", k=KD)
                            for k in range(KD):
                                last = nc.tensor.matmul(bank[m % 8][0:M, 0:T], wc[:, k, (m % 4) * P:(m % 4) * P + M],
                                                        xT[:, k, :], start=k == 0, stop=k == KD - 1)
                            last.then_inc(tile_done, 1)

                    @block.scalar
                    def _(act):
                        def silu(j):
                            act.wait_ge(conv_done, j + 1)
                            nc.scalar.activation(cv[:, j, :], cacc[:, j % 2, :], ACT.Silu).then_inc(silu_done, 1)
                        act.wait_ge(pos_d, 1)
                        nc.scalar.activation(wb[:], wb[:], ACT.Exp).then_inc(pos_a, 1)
                        act.wait_ge(ld_const, 16 * 13)
                        act.wait_ge(pads, 1)
                        for m in range(NT):
                            act.wait_ge(tile_done, m + 1)
                            j = m
                            if j < JC:
                                if j >= 2:
                                    act.wait_ge(conv_done, j - 1)
                                nc.scalar.activation(raw[:, j % 2, 3:SEQ + 3], bank[m % 8][:, 0:SEQ], ACT.Copy).then_inc(tile_taken, 1)
                                nc.scalar.activation(taps[:, j, 3, :], bank[m % 8][:, SEQ:T], ACT.Copy).then_inc(tile_taken, 1)
                                if j >= 1:
                                    silu(j - 1)
                            else:
                                nc.scalar.activation(dtr[:], bank[m % 8][0:NH, 0:T], ACT.Identity, bias=heads[:, 0:1]).then_inc(tile_taken, 1)
                                silu(JC - 1)

                    @block.vector
                    def _(dve):
                        V = nc.vector
                        V.memset(raw[:, :, 0:3], 0.0).then_inc(pads, 1)
                        dve.wait_ge(ld_pos, 32)
                        dve_step(dve, V.tensor_reduce(wst[:], wb[:], AX.X, ALU.max))
                        V.tensor_tensor(wb[:], wb[:], wst[:].unsqueeze(2).to_broadcast([P, 4, BLK]), ALU.subtract).then_inc(pos_d, 1)
                        dve.wait_ge(pos_a, 1)
                        dve_step(dve, V.tensor_reduce(wst[:], wb[:], AX.X, ALU.add))
                        dve_step(dve, V.reciprocal(wst[:], wst[:]))
                        V.tensor_tensor(wb[:], wb[:], wst[:].unsqueeze(2).to_broadcast([P, 4, BLK]), ALU.mult)
                        dve.wait_ge(ld_const, 16 * 13)
                        for j in range(JC):
                            dve.wait_ge(tile_taken, taken(j))
                            if j >= 2:
                                dve.wait_ge(silu_done, j - 1)
                            r, a = raw[:, j % 2, :], cacc[:, j % 2, :]
                            nc.vector.tensor_copy(lastp[:, j, :], r[:, SEQ:SEQ + 3])
                            nc.vector.tensor_scalar(a[:, 0:SEQ], r[:, 0:SEQ], convp[:, j, 0:1], convp[:, j, 4:5], ALU.mult, ALU.add)
                            dve_step(dve, nc.vector.tensor_scalar(a[:, SEQ:T], taps[:, j, 0, :], convp[:, j, 0:1], convp[:, j, 4:5], ALU.mult, ALU.add))
                            for k in range(1, NCONV):
                                nc.vector.scalar_tensor_tensor(a[:, 0:SEQ], r[:, k:k + SEQ], convp[:, j, k:k + 1], a[:, 0:SEQ], ALU.mult, ALU.add)
                                i2 = nc.vector.scalar_tensor_tensor(a[:, SEQ:T], taps[:, j, k, :], convp[:, j, k:k + 1], a[:, SEQ:T], ALU.mult, ALU.add)
                                if k < NCONV - 1:
                                    dve_step(dve, i2)
                            i2.then_inc(conv_done, 1)
                chunk_count[0] = (nchunk + 1) // 2
                chunk_count[1] = nchunk // 2

            with ExitStack() as st:
                def sb2(name, shape, dt=F32):
                    return st.enter_context(nc.sbuf_tensor(name, shape, dt))

                hsel = ring[0:NH, 1, 0:DI]
                sp_t = sb2("softplus_tmp", [NH, 2, T])
                dt = sb2("dt", [NH, T])
                dta = sb2("dta", [NH, T])
                na = sb2("neg_a", [NH, 1])
                expin = sb2("expand_in", [NH, 2 * DB + 1])
                ex = sb2("expanded", [P, JX, 2 * DB + 1])
                dtt = sb2("dt_tok", [P, QT, NH])
                dtat = sb2("dta_tok", [P, QT, NH])
                cumt = sb2("cum_tok", [P, QT, NH])
                cumh = sb2("cum_head", [NH, SEQ])
                toend = sb2("to_end", [P, QT, NH])
                xd = ring[:, 1, CH:2 * CH].rearrange("p (q f) -> p q f", q=QT)
                btok = sb2("b_tok", [P, QT, NG * NS])
                bcd = sb2("bc_dec", [DB, 2, NG * NS])
                cbm = sb2("cb_masked", [P, 2, 3 * P])
                seg = sb2("seg", [P, 2, 3 * P])
                dec = sb2("decay", [P, 2, 3 * P])
                mm_ = sb2("weights_sbm", [P, 2, 3 * P])
                stp = ring[:, 1, 2 * CH:2 * CH + JX * NS].rearrange("p (j n) -> p j n", j=JX)
                std2 = sb2("state_dec", [P, 2, JX, NS])
                std = [std2[:, 0], std2[:, 1]] + [ring[:, 1, o + 2048:o + 2048 + JX * NS].rearrange("p (j n) -> p j n", j=JX) for o in (0, 2 * CH)]
                yd = sb2("y_dec", [P, JX, DB])
                junk = sb2("junk", [P, 4, NS])
                pt = [st.enter_context(nc.psum_tensor(f"ss{i}", [P, 512], F32)) for i in range(8)]
                (ld_hsel, sc_dt, dt_ready, da_ready, tr_done, tr_taken, cum_pe, cum_ready, cb_done, cb_ready, bc_done, seg_done,
                 exp_done, w_done, y_done, y_taken, exp_pe, ex_ready, xe_ready, st_done, st_taken, bcb_done, dec_read, new_state, sd_scaled, z_done, z_taken, z_silu, y_gated) = (
                    sem("ss_" + n) for n in (
                        "ld_hsel", "sc_dt", "dt_ready", "da_ready", "tr_done", "tr_taken", "cum_pe", "cum_ready", "cb_done", "cb_ready",
                        "bc_done", "seg_done", "exp_done", "w_done", "y_done", "y_taken", "exp_pe", "ex_ready", "xe_ready", "st_done", "st_taken",
                        "bcb_done", "dec_read", "new_state", "sd_scaled", "z_done", "z_taken", "z_silu", "y_gated"))
                st_out = [sem(f"ss_out{n}") for n in range(4)]
                ld_sd = [sem(f"ss_ld_sd{n}") for n in range(4)]
                z_bank = lambda j: pt[7 if j == 0 else 2 if j < JX // 2 else j % 4]

                with nc.Block() as block:
                    @block.sync
                    def _(sp):
                        sp.dma_start(hsel, I["hsel"]).then_inc(ld_hsel, 16)

                        def load_state(b):
                            sp.dma_start(std[b % 4], I["state_ssm"][b].rearrange("(j p) n -> p j n", p=P)).then_inc(ld_sd[b % 4], 16)
                        for b in range(3):
                            load_state(b)
                        store(sp, O["win_old"], I["cache_win"][:, 1:, :])
                        sp.wait_ge(z_done, 4)
                        sp.dma_start(zw[0], w_in[:, :, 3 * 512:4 * 512]).then_inc(ld_z[0], 16)
                        sp.wait_ge(st_taken, 4)
                        store(sp, O["ssm_prompt"].rearrange("(j p) n -> p j n", p=P), stp)
                        for b in range(DB):
                            sp.wait_ge(new_state, JX * (b + 1))
                            sp.dma_start(O["ssm_sample"][b].rearrange("(j p) n -> p j n", p=P), std[b % 4]).then_inc(st_out[b % 4], 16)
                            if b + 3 < DB:
                                if b >= 1:
                                    sp.wait_ge(dec_read, JX * b)
                                    sp.wait_ge(st_out[(b - 1) % 4], 16 * ((b - 1) // 4 + 1))
                                load_state(b + 3)
                        for n in range(4):
                            sp.wait_ge(st_out[n], 16 * (DB // 4))
                        sp.wait_ge(stored, n_stored[0])

                    @block.gpsimd
                    def _(pool):
                        for g in range(NG):
                            pool.wait_ge(y_taken, 4 * g + 4)
                            pool.wait_ge(z_silu, g + 1)
                            y4 = cv[:, 4 * g:4 * g + 4, 0:SEQ]
                            nc.gpsimd.tensor_tensor(y4, y4, zs[:, 4 * g:4 * g + 4, 0:SEQ], ALU.mult).then_inc(y_gated, 1)

                    @block.scalar
                    def _(act):
                        act_step(act, nc.scalar.activation(sp_t[:, 0, :], dtr[:], ACT.Abs))
                        act_step(act, nc.scalar.activation(sp_t[:, 1, :], sp_t[:, 0, :], ACT.Exp, scale=-1.0))
                        nc.scalar.activation(sp_t[:, 0, :], sp_t[:, 1, :], ACT.Ln, bias=ones[0:NH, 0:1]).then_inc(sc_dt, 1)
                        nc.scalar.activation(na[:], heads[:, 1:2], ACT.Exp).then_inc(sc_dt, 1)
                        act.wait_ge(dt_ready, 1)
                        nc.scalar.activation(expin[:, DB:2 * DB], dta[:, SEQ:T], ACT.Exp).then_inc(da_ready, 1)
                        act.wait_ge(cum_ready, 3)
                        nc.scalar.activation(toend[:], toend[:], ACT.Exp).then_inc(cum_ready, 1)
                        def take_z(j):
                            act.wait_ge(z_done, j + 1)
                            nc.scalar.activation(zs[:, j, :], z_bank(j)[:, 0:T], ACT.Copy).then_inc(z_taken, 1)
                        take_z(0)
                        for h in range(NH):
                            act.wait_ge(seg_done, 2 * h + 2)
                            if h >= 2:
                                act.wait_ge(w_done, h - 1)
                            nc.scalar.activation(dec[:, h % 2, :], seg[:, h % 2, :], ACT.Exp).then_inc(exp_done, 1)
                            if h >= 4 and h % 4 == 0:
                                take_z(h // 4)

                        def silu_z(g):
                            act.wait_ge(z_taken, 4 * g + 4)
                            z4 = zs[:, 4 * g:4 * g + 4, :]
                            nc.scalar.activation(z4, z4, ACT.Silu).then_inc(z_silu, 1)
                        for g in range(4):
                            act.wait_ge(st_done, g + 1)
                            nc.scalar.activation(stp[:, 4 * g:4 * g + 4, :], pt[g][:].rearrange("p (j n) -> p j n", j=4), ACT.Copy).then_inc(st_taken, 1)
                        act.wait_ge(ex_ready, 1)
                        for b in range(DB):
                            act.wait_ge(ld_sd[b % 4], 16 * (b // 4 + 1))
                            for j in range(JX):
                                nc.scalar.activation(std[b % 4][:, j, :], std[b % 4][:, j, :], ACT.Copy, scale=ex[:, j, DB + b:DB + b + 1]).then_inc(sd_scaled, 1)
                            take_z(JX // 2 + b)
                            if b == 4:
                                for g in range(NG - 1):
                                    silu_z(g)
                        silu_z(NG - 1)

                    @block.tensor
                    def _(pe):
                        tr = nc.tensor.transpose

                        def z_tile(j, ks):
                            if j % 4 == 0 and ks[0] == 0:
                                pe.wait_ge(ld_z[(j // 4) % 3], 16 * (j // 12 + 1))
                            if ks[0] == 0:
                                if JX // 2 <= j < JX // 2 + 4:
                                    pe.wait_ge(st_taken, j % 4 + 1)
                                elif j >= 2:
                                    pe.wait_ge(z_taken, j if j < JX // 2 else j - 3)
                            for k in ks:
                                last = nc.tensor.matmul(z_bank(j)[:, 0:T], zw[(j // 4) % 3][:, k, (j % 4) * P:(j % 4 + 1) * P], xT[:, k, :],
                                                        start=k == 0, stop=k == KD - 1)
                            if ks[-1] == KD - 1:
                                last.then_inc(z_done, 1)

                        z_tile(0, range(KD))
                        pe.wait_ge(dt_ready, 1)
                        for q in range(QT):
                            tr(pt[0][:, q * NH:(q + 1) * NH], dt[:, q * P:(q + 1) * P], ident[0:NH, 0:NH])
                            last = tr(pt[0][:, (2 + q) * NH:(3 + q) * NH], dta[:, q * P:(q + 1) * P], ident[0:NH, 0:NH])
                        last.then_inc(tr_done, 1)
                        pe.wait_ge(tr_taken, 1)
                        tri = m384[:, 0:P]
                        mm = nc.tensor.matmul
                        mm(pt[1][:, 0:NH], tri, dtat[:, 0, :], start=True, stop=True)
                        mm(pt[1][:, NH:2 * NH], tri, dtat[:, 1, :], start=True, stop=False)
                        mm(pt[1][:, NH:2 * NH], ones[:], dtat[:, 0, :], start=False, stop=True)
                        mm(pt[1][:, 2 * NH:3 * NH], ones[:], dtat[:, 0, :], start=True, stop=False)
                        mm(pt[1][:, 2 * NH:3 * NH], ones[:], dtat[:, 1, :], start=False, stop=True)
                        mm(pt[2][0:NH, 0:SEQ], dtat[:, 0, :], m384[:, 0:SEQ], start=True, stop=False, skip_group_check=True)
                        mm(pt[2][0:NH, P:SEQ], dtat[:, 1, :], tri, start=False, stop=True, skip_group_check=True).then_inc(cum_pe, 1)
                        for n in range(12):
                            bk = pt[3 + n % 3]
                            if n >= 3:
                                pe.wait_ge(tr_taken, 1 + n - 2)
                            for a in range(4):
                                if n < 8:
                                    last = tr(bk[:, a * P:(a + 1) * P], cv[:, 4 * (n // 2) + a, (n % 2) * P:(n % 2 + 1) * P], ident[:])
                                elif n < 10:
                                    last = tr(bk[:, a * P:(a + 1) * P], cv[:, JX + a, (n - 8) * P:(n - 7) * P], ident[:])
                                else:
                                    last = tr(bk[0:DB, a * P:(a + 1) * P], cv[:, JX + NG * (n - 10) + a, SEQ:T], ident[:])
                            last.then_inc(tr_done, 1)
                        pe.wait_ge(da_ready, 1)
                        pe.wait_ge(ld_hsel, 16)
                        for j in range(JX):
                            last = mm(pt[6][:, j * (2 * DB + 1):(j + 1) * (2 * DB + 1)], hsel[:, j * P:(j + 1) * P], expin[:], start=True, stop=True)
                        last.then_inc(exp_pe, 1)
                        pe.wait_ge(cum_ready, 2)
                        pe.wait_ge(tr_taken, 13)

                        def cb(g):
                            if g == 0:
                                pe.wait_ge(ex_ready, 1)
                            if g >= 2:
                                pe.wait_ge(cb_ready, g - 1)
                            if g == 1:
                                pe.wait_ge(z_taken, 1)
                            bk = pt[6 + g % 2]
                            mm(bk[:, 0:SEQ], cv[:, JX + g, 0:P], cv[:, JX + NG + g, 0:SEQ], start=True, stop=True)
                            mm(bk[:, SEQ:3 * P], cv[:, JX + g, P:SEQ], cv[:, JX + NG + g, P:SEQ], start=True, stop=True).then_inc(cb_done, 1)

                        def spread(h):
                            if h >= 2:
                                pe.wait_ge(seg_done, 2 * (h - 1))
                            mm(pt[h % 2][:, 0:SEQ], ident[0:NH, h:h + 1].to_broadcast([NH, P]), cumh[:], start=True, stop=True).then_inc(bc_done, 1)

                        cb(0)
                        spread(0)
                        spread(1)
                        for h in range(NH):
                            if h % 8 == 4 and h // 8 + 1 < NG:
                                cb(h // 8 + 1)
                            if h + 2 < NH:
                                spread(h + 2)
                            j, half = h // 2, 64 * (h % 2)
                            pe.wait_ge(w_done, h + 1)
                            if h % 2 == 0 and j >= 3:
                                pe.wait_ge(y_taken, j - 2)
                            yb = pt[3 + j % 3]
                            mm(yb[half:half + 64, 0:SEQ], xd[:, 0, h * HD:(h + 1) * HD], mm_[:, h % 2, 0:SEQ], start=True, stop=False, skip_group_check=True)
                            mm(yb[half:half + 64, P:SEQ], xd[:, 1, h * HD:(h + 1) * HD], mm_[:, h % 2, SEQ:3 * P], start=False, stop=True,
                               skip_group_check=True).then_inc(y_done, 1)
                            if h // 4 + 1 < JX // 2:
                                z_tile(h // 4 + 1, range(2 * (h % 4), 2 * (h % 4) + 2))
                        pe.wait_ge(xe_ready, 2)
                        pe.wait_ge(y_taken, JX)
                        pe.wait_ge(z_taken, JX // 2)
                        for j in range(JX):
                            g = j // 4
                            for q in range(QT):
                                last = mm(pt[g][:, (j % 4) * NS:(j % 4 + 1) * NS], xd[:, q, j * P:(j + 1) * P],
                                          btok[:, q, g * NS:(g + 1) * NS], start=q == 0, stop=q == QT - 1)
                            if j % 4 == 3:
                                last.then_inc(st_done, 1)
                        for b in range(DB):
                            if b >= 2:
                                pe.wait_ge(dec_read, JX * (b - 1))
                            for c in range(2):
                                last = mm(pt[4 + 2 * (b % 2) + c][:], ident[0:DB, b:b + 1].to_broadcast([DB, P]), bcd[:, c, :], start=True, stop=True)
                            last.then_inc(bcb_done, 1)
                            z_tile(JX // 2 + b, range(KD))

                    @block.vector
                    def _(dve):
                        V = nc.vector
                        dve.wait_ge(sc_dt, 2)
                        V.tensor_scalar(na[:], na[:], -1.0, None, ALU.mult)
                        dve_step(dve, V.tensor_scalar(sp_t[:, 1, :], dtr[:], 0.0, None, ALU.max))
                        dve_step(dve, V.tensor_tensor(dt[:], sp_t[:, 0, :], sp_t[:, 1, :], ALU.add))
                        V.tensor_copy(expin[:, 0:DB], dt[:, SEQ:T])
                        V.tensor_copy(expin[:, 2 * DB:2 * DB + 1], heads[:, 2:3])
                        V.tensor_scalar(dta[:], dt[:], na[:, 0:1], None, ALU.mult).then_inc(dt_ready, 1)
                        dve.wait_ge(tr_done, 1)
                        V.tensor_copy(dtt[:], pt[0][:, 0:2 * NH].rearrange("p (q h) -> p q h", q=QT))
                        V.tensor_copy(dtat[:], pt[0][:, 2 * NH:4 * NH].rearrange("p (q h) -> p q h", q=QT)).then_inc(tr_taken, 1)
                        dve.wait_ge(tr_taken, 1)
                        dve.wait_ge(cum_pe, 1)
                        V.tensor_copy(cumt[:], pt[1][:, 0:2 * NH].rearrange("p (q h) -> p q h", q=QT)).then_inc(cum_ready, 1)
                        V.tensor_copy(cumh[:], pt[2][0:NH, 0:SEQ]).then_inc(cum_ready, 1)
                        dve.wait_ge(cum_ready, 2)
                        V.tensor_tensor(toend[:], pt[1][:, 2 * NH:3 * NH].unsqueeze(1).to_broadcast([P, QT, NH]), cumt[:], ALU.subtract).then_inc(cum_ready, 1)
                        for n in range(12):
                            dve.wait_ge(tr_done, n + 2)
                            bk = pt[3 + n % 3]
                            if n < 8:
                                g, q = n // 2, n % 2
                                V.tensor_tensor(xd[:, q, g * 512:(g + 1) * 512].rearrange("p (h d) -> p h d", d=HD), bk[:].rearrange("p (h d) -> p h d", d=HD),
                                                dtt[:, q, 8 * g:8 * g + 8].unsqueeze(2).to_broadcast([P, 8, HD]), ALU.mult).then_inc(tr_taken, 1)
                            elif n < 10:
                                V.tensor_copy(btok[:, n - 8, :], bk[:]).then_inc(tr_taken, 1)
                            else:
                                V.tensor_copy(bcd[:, n - 10, :], bk[0:DB, :]).then_inc(tr_taken, 1)
                        dve.wait_ge(exp_pe, 1)
                        V.tensor_copy(ex[:], pt[6][:, 0:JX * (2 * DB + 1)].rearrange("p (j c) -> p j c", j=JX)).then_inc(ex_ready, 1)
                        dve.wait_ge(ex_ready, 1)
                        def mask_cb(g):
                            dve.wait_ge(cb_done, g + 1)
                            V.tensor_tensor(cbm[:, g % 2, :], pt[6 + g % 2][:, 0:3 * P], m384[:], ALU.mult).then_inc(cb_ready, 1)
                        def segments(h):
                            dve.wait_ge(bc_done, h + 1)
                            if h >= 2:
                                dve.wait_ge(exp_done, h - 1)
                            V.tensor_scalar(seg[:, h % 2, 0:SEQ], pt[h % 2][:, 0:SEQ], cumt[:, 0, h:h + 1], 0.0, ALU.subtract, ALU.min).then_inc(seg_done, 1)
                            V.tensor_scalar(seg[:, h % 2, SEQ:3 * P], pt[h % 2][:, P:SEQ], cumt[:, 1, h:h + 1], 0.0, ALU.subtract, ALU.min).then_inc(seg_done, 1)
                        def y_out(j):
                            dve.wait_ge(y_done, 2 * j + 2)
                            V.scalar_tensor_tensor(cv[:, j, 0:SEQ], cv[:, j, 0:SEQ], ex[:, j, 2 * DB:2 * DB + 1], pt[3 + j % 3][:, 0:SEQ], ALU.mult, ALU.add).then_inc(y_taken, 1)
                        mask_cb(0)
                        segments(0)
                        for h in range(NH):
                            if h % 8 == 7 and h // 8 + 1 < NG:
                                mask_cb(h // 8 + 1)
                            if h + 1 < NH:
                                segments(h + 1)
                            dve.wait_ge(exp_done, h + 1)
                            dve.wait_ge(cb_ready, h // 8 + 1)
                            if h >= 2:
                                dve.wait_ge(y_done, h - 1)
                            V.tensor_tensor(mm_[:, h % 2, :], dec[:, h % 2, :], cbm[:, (h // 8) % 2, :], ALU.mult).then_inc(w_done, 1)
                            if h % 2 == 1 and h >= 3:
                                y_out(h // 2 - 1)
                        y_out(JX - 1)
                        dve.wait_ge(cum_ready, 4)
                        for q in range(QT):
                            x3 = xd[:, q, :].rearrange("p (h d) -> p h d", d=HD)
                            V.tensor_tensor(x3, x3, toend[:, q, :].unsqueeze(2).to_broadcast([P, NH, HD]), ALU.mult).then_inc(xe_ready, 1)
                        V.tensor_tensor(yd[:], cv[:, 0:JX, SEQ:T], ex[:, :, 0:DB], ALU.mult).then_inc(dve_step.sem, 1)
                        dve_step.n += 1
                        dve.wait_ge(dve_step.sem, dve_step.n)
                        for b in range(DB):
                            dve.wait_ge(bcb_done, b + 1)
                            for j in range(JX):
                                g, s = j // 4, std[b % 4][:, j, :]
                                dve.wait_ge(sd_scaled, JX * b + j + 1)
                                V.scalar_tensor_tensor(s, pt[4 + 2 * (b % 2)][:, g * NS:(g + 1) * NS], yd[:, j, b:b + 1], s, ALU.mult, ALU.add).then_inc(new_state, 1)
                            for j in range(JX):
                                g, s = j // 4, std[b % 4][:, j, :]
                                dve.wait_ge(new_state, JX * b + j + 1)
                                if JX * b + j >= 4:
                                    dve.wait_ge(dec_read, JX * b + j - 3)
                                V.tensor_tensor_reduce(junk[:, j % 4, :], s, pt[5 + 2 * (b % 2)][:, g * NS:(g + 1) * NS], 1.0, 0.0, ALU.mult, ALU.add,
                                                       yd[:, j, b:b + 1]).then_inc(dec_read, 1)
                        dve.wait_ge(dec_read, JX * DB)
                        c3 = cv[:, 0:JX, SEQ:T]
                        dve_step(dve, V.tensor_tensor(c3, c3, ex[:, :, 2 * DB:2 * DB + 1].to_broadcast([P, JX, DB]), ALU.mult))
                        dve_step(dve, V.tensor_tensor(c3, c3, yd[:], ALU.add))
                        dve.wait_ge(z_silu, NG)
                        dve_step(dve, V.tensor_tensor(c3, c3, zs[:, :, SEQ:T], ALU.mult))

            with ExitStack() as st:
                rr = st.enter_context(nc.sbuf_tensor("rms", [P, NG, T], F32))
                bank = [st.enter_context(nc.psum_tensor(f"on{i}", [P, 512], F32)) for i in range(8)]
                sq_done, ms_done, sqrt_done, y_ready, o_done, o_taken = (sem("so_" + n) for n in ("sq", "ms", "sqrt", "y", "done", "taken"))
                base = [c * 16 for c in chunk_count]
                with nc.Block() as block:
                    @block.sync
                    def _(sp):
                        w = I["ssd_w_out"].rearrange("(k p) n -> p k n", p=P)
                        for c in range(4):
                            if c >= 2:
                                sp.wait_ge(o_done, 2 * (c - 1))
                            load_chunk(sp, c % 2, w[:, :, c * 256:(c + 1) * 256])
                        load_expert(sp, 0, 0)

                    @block.scalar
                    def _(act):
                        for j in range(JX):
                            nc.scalar.activation(zs[:, j, :], cv[:, j, :], ACT.Square).then_inc(sq_done, 1)
                        for g in range(NG):
                            act.wait_ge(ms_done, g + 1)
                            nc.scalar.activation(rr[:, g, :], bank[g][:, 0:T], ACT.Sqrt, scale=1.0 / 512, bias=epst[:, 0:1]).then_inc(sqrt_done, 1)

                    @block.tensor
                    def _(pe):
                        for j in range(JX):
                            pe.wait_ge(sq_done, j + 1)
                            last = nc.tensor.matmul(bank[j // 4][:, 0:T], ones[:], zs[:, j, :], start=j % 4 == 0, stop=j % 4 == 3)
                            if j % 4 == 3:
                                last.then_inc(ms_done, 1)
                        pe.wait_ge(y_ready, JX)
                        for m in range(KD):
                            c = m // 2
                            if m % 2 == 0:
                                pe.wait_ge(ld_chunk[c % 2], base[c % 2] + 16 * (c // 2 + 1))
                            if m >= 4:
                                pe.wait_ge(o_taken, m - 3)
                            wc = chunk[c % 2].rearrange("p (k n) -> p k n", k=JX)
                            for k in range(JX):
                                last = nc.tensor.matmul(bank[4 + m % 4][:, 0:T], wc[:, k, (m % 2) * P:(m % 2 + 1) * P], cv[:, k, :],
                                                        start=k == 0, stop=k == JX - 1)
                            last.then_inc(o_done, 1)

                    @block.vector
                    def _(dve):
                        V = nc.vector
                        for g in range(NG):
                            dve.wait_ge(sqrt_done, g + 1)
                            dve_step(dve, V.reciprocal(rr[:, g, :], rr[:, g, :]))
                            for j in range(4 * g, 4 * g + 4):
                                V.scalar_tensor_tensor(cv[:, j, :], cv[:, j, :], normg[:, j:j + 1], rr[:, g, :], ALU.mult, ALU.mult).then_inc(y_ready, 1)
                        for m in range(KD):
                            dve.wait_ge(o_done, m + 1)
                            V.scalar_tensor_tensor(xT[:, m, :], xT[:, m, :], ALPHA, bank[4 + m % 4][:, 0:T], ALU.mult, ALU.add).then_inc(o_taken, 1)
                for c in range(2):
                    chunk_count[c] += 2

        ln_sems = [sem("ln_" + n) for n in ("mean", "cent", "sq", "var", "sqrt", "norm")]

        def layer_norm(L, which, src, dst, tag, prefetch=None):
            use = 2 * L + which
            with ExitStack() as st:
                sq = st.enter_context(nc.sbuf_tensor("ln_sq_" + tag, [P, KD, T], F32))
                rs = st.enter_context(nc.sbuf_tensor("ln_rs_" + tag, [P, 2, T], F32))
                pm = st.enter_context(nc.psum_tensor("ln_m_" + tag, [P, 512], F32))
                pv = st.enter_context(nc.psum_tensor("ln_v_" + tag, [P, 512], F32))
                s_mean, s_cent, s_sq, s_var, s_sqrt, s_rs = ln_sems
                g, b = lnp[:, L, 2 * which, :], lnp[:, L, 2 * which + 1, :]
                with nc.Block() as block:
                    @block.sync
                    def _(sp):
                        if prefetch is not None:
                            prefetch(sp)

                    @block.tensor
                    def _(pe):
                        for k in range(KD):
                            last = nc.tensor.matmul(pm[:, 0:T], ones[:], src[:, k, :], start=k == 0, stop=k == KD - 1)
                        last.then_inc(s_mean, 1)
                        for k in range(KD):
                            pe.wait_ge(s_sq, KD * use + k + 1)
                            last = nc.tensor.matmul(pv[:, 0:T], ones[:], sq[:, k, :], start=k == 0, stop=k == KD - 1)
                        last.then_inc(s_var, 1)

                    @block.scalar
                    def _(act):
                        for k in range(KD):
                            act.wait_ge(s_cent, KD * use + k + 1)
                            nc.scalar.activation(sq[:, k, :], src[:, k, :], ACT.Square).then_inc(s_sq, 1)
                        act.wait_ge(s_var, use + 1)
                        nc.scalar.activation(rs[:, 1, :], pv[:, 0:T], ACT.Sqrt, scale=1.0 / D, bias=epst[:, 0:1]).then_inc(s_sqrt, 1)
                        for k in range(KD):
                            act.wait_ge(s_rs, KD * use + k + 1)
                            nc.scalar.activation(dst[:, k, :], src[:, k, :], ACT.Identity, scale=g[:, k:k + 1], bias=b[:, k:k + 1])

                    @block.vector
                    def _(dve):
                        V = nc.vector
                        dve.wait_ge(s_mean, use + 1)
                        dve_step(dve, V.tensor_scalar(rs[:, 0, :], pm[:, 0:T], 1.0 / D, None, ALU.mult))
                        for k in range(KD):
                            V.tensor_tensor(src[:, k, :], src[:, k, :], rs[:, 0, :], ALU.subtract).then_inc(s_cent, 1)
                        dve.wait_ge(s_sqrt, use + 1)
                        dve_step(dve, V.reciprocal(rs[:, 0, :], rs[:, 1, :]))
                        dve.wait_ge(s_sq, KD * use + KD)
                        for k in range(KD):
                            V.tensor_tensor(src[:, k, :], src[:, k, :], rs[:, 0, :], ALU.mult).then_inc(s_rs, 1)

        CAP = 64
        router_sems = [sem("r_" + n) for n in ("log", "init", "sig", "gate", "rank", "slots", "selg", "xtr", "xtok", "tr", "out", "got", "go")]
        ple_sems = [sem("e_" + n) for n in ("ld", "done", "sig", "out")]
        moe_sems = [sem("m_" + n) for n in ("gather", "packed", "gu", "silu", "hid", "turned", "ht", "down", "ys", "scatter", "acc")]

        def tail(L, out=None):
            layer_norm(L, 0, xT, xT, f"a{L}")
            with ExitStack() as outer:
                acc = outer.enter_context(nc.sbuf_tensor(f"acc{L}", [P, KD, T], F32))
                tile3 = [(0, P), (P, P), (SEQ, DB)]
                NF, NP2 = FF // P, NE // 2
                with ExitStack() as moe:
                    def sbm(name, shape, dt=F32):
                        return moe.enter_context(nc.sbuf_tensor(f"{name}{L}", shape, dt))
                    xtok = sbm("x_tok", [P, 3, D])
                    sel1 = sbm("slot_onehot", [P, 3, NE * CAP])
                    sgt = sbm("scatter_gates", [P, NP2, T])
                    gto = sbm("gates_over", [NE, T])
                    most = sbm("most_tokens", [1, 1], I32)
                    with ExitStack() as st:
                        def sb3(name, shape):
                            return st.enter_context(nc.sbuf_tensor(f"{name}{L}", shape, F32))
                        score, sel, cmp5, eq5, rank, insel, gs, best = (
                            sb3("score", [P, 3, NE]), sb3("sel", [P, 3, NE]), sb3("cmp", [P, 3, EG, EG, EG]), sb3("eq", [P, 3, EG, EG, EG]),
                            sb3("rank", [P, 3, NE]), sb3("insel", [P, 3, NE]), sb3("gs", [P, 3, EG]), sb3("best", [P, 3, EG]))
                        wsum, slot, gover, cmax = sb3("wsum", [P, 3]), sb3("slot", [P, 3, NE]), sb3("gover", [P, 3, NE]), sb3("cmax", [1, 1])
                        selg = sb3("slot_gate", [P, 3, NE * CAP])
                        pr = st.enter_context(nc.psum_tensor(f"pr{L}", [P, 512], F32))
                        prk = st.enter_context(nc.psum_tensor(f"prk{L}", [P, 512], F32))
                        pgo = st.enter_context(nc.psum_tensor(f"pgo{L}", [P, 512], F32))
                        pg = [st.enter_context(nc.psum_tensor(f"pg{L}{i}", [P, 512], F32)) for i in range(4)]
                        r_log, r_init, r_sig, r_gate, r_rank, r_slots, r_selg, r_xtr, r_xtok, r_tr, r_out, r_got, r_go = router_sems
                        with nc.Block() as block:
                            @block.sync
                            def _(sp):
                                load_expert(sp, NE * L + 1, 1)

                            @block.tensor
                            def _(pe):
                                tr, mm = nc.tensor.transpose, nc.tensor.matmul
                                for q, (t0, n) in enumerate(tile3):
                                    for k in range(KD):
                                        last = mm(pr[0:n, q * NE:(q + 1) * NE], xT[:, k, t0:t0 + n], rw[:, k, :], start=k == 0, stop=k == KD - 1)
                                last.then_inc(r_log, 1)
                                for c in range(6):
                                    t0, n = tile3[c // 2]
                                    if c >= 4:
                                        pe.wait_ge(r_xtok, 6 * L + c - 3)
                                    for a in range(4):
                                        last = tr(pg[c % 4][0:n, a * P:(a + 1) * P], xT[:, 4 * (c % 2) + a, t0:t0 + n], ident[:])
                                    last.then_inc(r_xtr, 1)
                                pe.wait_ge(r_gate, 2 * L + 1)
                                tri = m384[:, 0:P]
                                for q, (t0, n) in enumerate(tile3):
                                    for p in range(q):
                                        mm(prk[0:n, q * NE:(q + 1) * NE], ones[:, 0:n], insel[:, p, :], start=p == 0, stop=False)
                                    mm(prk[0:n, q * NE:(q + 1) * NE], tri[0:n, 0:n], insel[0:n, q, :], start=q == 0, stop=True)
                                for q, (t0, n) in enumerate(tile3):
                                    last = mm(prk[:, 3 * NE:4 * NE], ones[0:n, :], insel[0:n, q, :], start=q == 0, stop=q == 2)
                                last.then_inc(r_rank, 1)
                                pe.wait_ge(r_go, L + 1)
                                for q, (t0, n) in enumerate(tile3):
                                    last = tr(pgo[0:NE, t0:t0 + n], gover[0:n, q, :], ident[0:n, 0:n])
                                last.then_inc(r_got, 1)
                                pe.wait_ge(r_selg, 3 * (L + 1))
                                pe.wait_ge(r_xtok, 6 * (L + 1))
                                for i in range(NP2):
                                    if i >= 4:
                                        pe.wait_ge(r_out, NP2 * L + i - 3)
                                    for q, (t0, n) in enumerate(tile3):
                                        last = tr(pg[i % 4][:, t0:t0 + n], selg[0:n, q, i * P:(i + 1) * P], ident[0:n, 0:n])
                                    last.then_inc(r_tr, 1)

                            @block.scalar
                            def _(act):
                                act.wait_ge(r_log, L + 1)
                                act.wait_ge(r_init, L + 1)
                                nc.scalar.activation(score[:, 0:2, :], pr[:, 0:2 * NE].rearrange("p (q e) -> p q e", q=2), ACT.Sigmoid).then_inc(r_sig, 1)
                                nc.scalar.activation(score[0:DB, 2, :], pr[0:DB, 2 * NE:3 * NE], ACT.Sigmoid).then_inc(r_sig, 1)
                                for c in range(6):
                                    t0, n = tile3[c // 2]
                                    act.wait_ge(r_xtr, 6 * L + c + 1)
                                    nc.scalar.activation(xtok[0:n, c // 2, (c % 2) * 512:(c % 2 + 1) * 512], pg[c % 4][0:n, :], ACT.Copy).then_inc(r_xtok, 1)
                                act.wait_ge(r_got, L + 1)
                                nc.scalar.activation(gto[:], pgo[0:NE, 0:T], ACT.Copy)
                                for i in range(NP2):
                                    act.wait_ge(r_tr, NP2 * L + i + 1)
                                    nc.scalar.activation(sgt[:, i, :], pg[i % 4][:, 0:T], ACT.Copy).then_inc(r_out, 1)

                            @block.gpsimd
                            def _(pool):
                                pool.wait_ge(r_gate, 2 * L + 2)
                                for q, (t0, n) in enumerate(tile3):
                                    pool.wait_ge(r_slots, 3 * L + q + 1)
                                    c3 = lambda t: t[0:n, q, :].rearrange("p (e c) -> p e c", c=CAP)
                                    nc.gpsimd.tensor_tensor(c3(selg), c3(sel1), rank[0:n, q, :].unsqueeze(2).to_broadcast([n, NE, CAP]), ALU.mult).then_inc(r_selg, 1)

                            @block.vector
                            def _(dve):
                                V = nc.vector
                                V.memset(score[:], 0.5).then_inc(r_init, 1)
                                dve.wait_ge(r_sig, 2 * L + 2)
                                dve_step(dve, V.tensor_tensor(sel[:], score[:], rbias[:].unsqueeze(1).to_broadcast([P, 3, NE]), ALU.add))
                                low = lower4[:].unsqueeze(1).to_broadcast([P, 3 * EG, EG, EG])
                                c4, e4 = (t[:].rearrange("p q g j i -> p (q g) j i") for t in (cmp5, eq5))
                                s3 = sel[:].rearrange("p q (g j) -> p (q g) j", j=EG)
                                si, sj = s3.unsqueeze(2).to_broadcast([P, 3 * EG, EG, EG]), s3.unsqueeze(3).to_broadcast([P, 3 * EG, EG, EG])
                                V.tensor_tensor(c4, si, sj, ALU.is_gt)
                                dve_step(dve, V.tensor_tensor(e4, si, sj, ALU.is_equal))
                                dve_step(dve, V.tensor_tensor(e4, e4, low, ALU.mult))
                                dve_step(dve, V.tensor_tensor(c4, c4, e4, ALU.add))
                                dve_step(dve, V.tensor_reduce(rank[:].rearrange("p q (g j) -> p (q g) j", j=EG), c4, AX.X, ALU.add))
                                dve_step(dve, V.tensor_scalar(insel[:], rank[:], 1.5, None, ALU.is_lt))
                                dve_step(dve, V.tensor_tensor(rank[:], sel[:], insel[:], ALU.mult))
                                dve_step(dve, V.tensor_reduce(gs[:].rearrange("p q g -> p (q g)"), rank[:].rearrange("p q (g j) -> p (q g) j", j=EG), AX.X, ALU.add))
                                gi, gj = gs[:].unsqueeze(2).to_broadcast([P, 3, EG, EG]), gs[:].unsqueeze(3).to_broadcast([P, 3, EG, EG])
                                cg, eg = cmp5[:, :, 0, :, :], eq5[:, :, 0, :, :]
                                V.tensor_tensor(cg, gi, gj, ALU.is_gt)
                                dve_step(dve, V.tensor_tensor(eg, gi, gj, ALU.is_equal))
                                dve_step(dve, V.tensor_tensor(eg, eg, lower4[:].unsqueeze(1).to_broadcast([P, 3, EG, EG]), ALU.mult))
                                dve_step(dve, V.tensor_tensor(cg, cg, eg, ALU.add))
                                dve_step(dve, V.tensor_reduce(best[:], cg, AX.X, ALU.add))
                                dve_step(dve, V.tensor_scalar(best[:], best[:], 0.5, None, ALU.is_lt))
                                i3 = insel[:].rearrange("p q (g j) -> p (q g) j", j=EG)
                                V.tensor_tensor(i3, i3, best[:].rearrange("p q g -> p (q g)").unsqueeze(2).to_broadcast([P, 3 * EG, EG]), ALU.mult).then_inc(r_gate, 1)
                                dve.wait_ge(r_gate, 2 * L + 1)
                                dve_step(dve, V.tensor_tensor(rank[:], insel[:], score[:], ALU.mult))
                                dve_step(dve, V.tensor_reduce(wsum[:], rank[:], AX.X, ALU.add))
                                dve_step(dve, V.reciprocal(wsum[:], wsum[:]))
                                V.tensor_tensor(rank[:], rank[:], wsum[:].unsqueeze(2).to_broadcast([P, 3, NE]), ALU.mult).then_inc(r_gate, 1)
                                dve.wait_ge(r_rank, L + 1)
                                for q0, q1, n in ((0, 2, P), (2, 3, DB)):
                                    v = lambda t: t[0:n, q0:q1, :]
                                    pk = prk[0:n, q0 * NE:q1 * NE].rearrange("p (q e) -> p q e", e=NE)
                                    V.tensor_tensor(v(slot), pk, v(insel), ALU.mult)
                                    i1 = V.tensor_scalar(v(gover), pk, CAP + 0.5, None, ALU.is_gt)
                                dve_step(dve, i1)
                                for q, (t0, n) in enumerate(tile3):
                                    V.tensor_tensor(sel1[0:n, q, :].rearrange("p (e c) -> p e c", c=CAP), slot[0:n, q, :].unsqueeze(2).to_broadcast([n, NE, CAP]),
                                                    iota64[0:n, :].unsqueeze(1).to_broadcast([n, NE, CAP]), ALU.is_equal).then_inc(r_slots, 1)
                                dve.wait_ge(r_gate, 2 * L + 2)
                                V.tensor_tensor(gover[:, 0:2, :], gover[:, 0:2, :], rank[:, 0:2, :], ALU.mult)
                                V.tensor_tensor(gover[0:DB, 2, :], gover[0:DB, 2, :], rank[0:DB, 2, :], ALU.mult).then_inc(r_go, 1)
                                dve_step(dve, V.tensor_reduce(cmax[:], prk[0:1, 3 * NE:4 * NE], AX.X, ALU.max))
                                V.tensor_copy(most[:], cmax[:])
                                V.tensor_scalar(acc[:], xT[:], ALPHA, None, ALU.mult)
                    xg = sbm("x_packed", [P, KD, 2 * CAP])
                    sg = sbm("silu_gate", [P, FF])
                    hid = sbm("hid", [P, FF])
                    ht = sbm("hid_T", [P, NF, 2 * CAP])
                    ys = sbm("y_slots", [P, D])
                    gb = [moe.enter_context(nc.psum_tensor(f"mg{L}{n}", [P, 512], F32)) for n in range(2)]
                    hb = [moe.enter_context(nc.psum_tensor(f"mh{L}{n}", [P, 512], F32)) for n in range(2)]
                    ob = [moe.enter_context(nc.psum_tensor(f"mo{L}{n}", [P, 512], F32)) for n in range(4)]
                    gathered, packed, gu_done, silu_ok, hid_ok, turned, ht_ok, down_done, ys_ok, sc_done, acc_ok = moe_sems
                    n1, n2, n8 = NP2 * L, 2 * NP2 * L, 8 * NP2 * L
                    ld0 = 16 * NP2 * L

                    with nc.Block() as block:
                        @block.sync
                        def _(sp):
                            def body(i, last=False):
                                slots = [s for s in range(2) if not (last and (s == 1 or L == 1))]
                                src = lambda w, s: w[bass.ds(NE * L + 2 + 2 * i + s, 1)].rearrange("a (k p) n -> p (a k) n", p=P)
                                for s in slots:
                                    sp.wait_ge(gu_done, 2 * i + s + 1 + n2)
                                    sp.dma_start(ring[:, s, 0:CH].rearrange("p (k n) -> p k n", k=KD), src(I["moe_w_gate"], s)).then_inc(ld_wg[s], 16)
                                    sp.dma_start(ring[:, s, CH:2 * CH].rearrange("p (k n) -> p k n", k=KD), src(I["moe_w_up"], s)).then_inc(ld_wu[s], 16)
                                for s in slots:
                                    sp.wait_ge(down_done, 2 * i + s + 1 + n2)
                                    sp.dma_start(ring[:, s, 2 * CH:3 * CH].rearrange("p (k n) -> p k n", k=NF), src(I["moe_w_down"], s)).then_inc(ld_wd[s], 16)
                            with sp.Fori(0, NP2 - 1) as i:
                                body(i)
                            body(NP2 - 1, True)

                        @block.tensor
                        def _(pe):
                            mm = nc.tensor.matmul

                            def gather(i, first=False):
                                for a in range(2):
                                    if not first:
                                        pe.wait_ge(packed, 2 * i + a - 1 + n2)
                                    for k in range(4):
                                        for q, (t0, n) in enumerate(tile3):
                                            last = mm(gb[a][:, k * P:(k + 1) * P], xtok[0:n, q, (4 * a + k) * P:(4 * a + k + 1) * P],
                                                      sel1[0:n, q, bass.ds(i * 2 * CAP, 2 * CAP)], start=q == 0, stop=q == 2)
                                    last.then_inc(gathered, 1)

                            def gate_up(i, first=False):
                                pe.wait_ge(packed, 2 * i + 2 + n2)
                                if not first:
                                    pe.wait_ge(hid_ok, i + n1)
                                for s in range(2):
                                    for w, ld in enumerate((ld_wg, ld_wu)):
                                        pe.wait_ge(ld[s], 16 * i + 16 + ld0)
                                        wt = ring[:, s, w * CH:(w + 1) * CH].rearrange("p (k n) -> p k n", k=KD)
                                        for k in range(KD):
                                            last = mm(hb[w][s * CAP:(s + 1) * CAP, :], xg[:, k, s * CAP:(s + 1) * CAP], wt[:, k, :],
                                                      start=k == 0, stop=k == KD - 1)
                                    last.then_inc(gu_done, 1)

                            def turn(i, first=False):
                                pe.wait_ge(hid_ok, i + 1 + n1)
                                if not first:
                                    pe.wait_ge(acc_ok, 8 * i - 1 + n8)
                                for f in range(NF):
                                    last = nc.tensor.transpose(ob[0][:, f * P:(f + 1) * P], hid[:, f * P:(f + 1) * P], ident[:])
                                last.then_inc(turned, 1)

                            def down(i, first=False):
                                pe.wait_ge(ht_ok, i + 1 + n1)
                                if not first:
                                    pe.wait_ge(ys_ok, 2 * i + n2)
                                for s in range(2):
                                    pe.wait_ge(ld_wd[s], 16 * i + 16 + ld0)
                                    wt = ring[:, s, 2 * CH:3 * CH].rearrange("p (k n) -> p k n", k=NF)
                                    for a in range(2):
                                        for k in range(NF):
                                            last = mm(ob[2 + a][s * CAP:(s + 1) * CAP, :], ht[:, k, s * CAP:(s + 1) * CAP], wt[:, k, a * 512:(a + 1) * 512],
                                                      start=k == 0, stop=k == NF - 1)
                                    last.then_inc(down_done, 1)

                            def scatter(i, first=False):
                                pe.wait_ge(ys_ok, 2 * i + 2 + n2)
                                for d in range(KD):
                                    if not (first and d < 2):
                                        pe.wait_ge(acc_ok, 8 * i + d - 1 + n8)
                                    mm(ob[d % 2][:, 0:T], ys[:, d * P:(d + 1) * P], sgt[:, bass.ds(i, 1), :].rearrange("p a t -> p (a t)"),
                                       start=True, stop=True).then_inc(sc_done, 1)

                            def body(i):
                                gate_up(i)
                                scatter(i - 1)
                                turn(i)
                                gather(i + 1)
                                down(i)

                            gather(0, True)
                            gate_up(0, True)
                            turn(0, True)
                            gather(1)
                            down(0, True)
                            gate_up(1)
                            scatter(0, True)
                            turn(1)
                            gather(2)
                            down(1)
                            with pe.Fori(2, NP2 - 1) as i:
                                body(i)
                            gate_up(NP2 - 1)
                            scatter(NP2 - 2)
                            turn(NP2 - 1)
                            down(NP2 - 1)
                            scatter(NP2 - 1)

                        @block.scalar
                        def _(act):
                            A_ = nc.scalar.activation

                            def pack(i, first=False):
                                for a in range(2):
                                    act.wait_ge(gathered, 2 * i + a + 1 + n2)
                                    if not first:
                                        act.wait_ge(gu_done, 2 * i + n2)
                                    A_(xg[:, 4 * a:4 * a + 4, :].rearrange("p k c -> p (k c)"), gb[a][:], ACT.Copy).then_inc(packed, 1)

                            def body(i, first=False, last=False):
                                act.wait_ge(gu_done, 2 * i + 2 + n2)
                                if not first:
                                    act.wait_ge(hid_ok, i + n1)
                                A_(sg[:], hb[0][:], ACT.Silu).then_inc(silu_ok, 1)
                                act.wait_ge(turned, i + 1 + n1)
                                if not first:
                                    act.wait_ge(down_done, 2 * i + n2)
                                A_(ht[:].rearrange("p f c -> p (f c)"), ob[0][:], ACT.Copy).then_inc(ht_ok, 1)
                                if not last:
                                    pack(i + 1)
                                act.wait_ge(down_done, 2 * i + 2 + n2)
                                if not first:
                                    act.wait_ge(sc_done, 8 * i + n8)
                                for a in range(2):
                                    A_(ys[:, a * 512:(a + 1) * 512], ob[2 + a][:], ACT.Copy).then_inc(ys_ok, 1)

                            pack(0, True)
                            body(0, True)
                            with act.Fori(1, NP2 - 1) as i:
                                body(i)
                            body(NP2 - 1, last=True)

                        @block.vector
                        def _(dve):
                            V = nc.vector

                            def body(i, first=False):
                                dve.wait_ge(silu_ok, i + 1 + n1)
                                if not first:
                                    dve.wait_ge(turned, i + n1)
                                V.tensor_tensor(hid[:], hb[1][:], sg[:], ALU.mult).then_inc(hid_ok, 1)
                                if not first:
                                    add(i - 1)

                            def add(i):
                                for d in range(KD):
                                    dve.wait_ge(sc_done, 8 * i + d + 1 + n8)
                                    V.tensor_tensor(acc[:, d, :], acc[:, d, :], ob[d % 2][:, 0:T], ALU.add).then_inc(acc_ok, 1)

                            body(0, True)
                            with dve.Fori(1, NP2) as i:
                                body(i)
                            add(NP2 - 1)

                    o_ld, o_dve, o_pe, o_act = (sem(f"over{L}_{n}") for n in ("ld", "dve", "pe", "act"))
                    gox = sbm("gate_row", [NE, T])
                    osg, ohu, ohid = sbm("over_silu", [P, T]), sbm("over_up", [P, T]), sbm("over_hid", [P, NF, T])
                    NPE, NDV = 1 + NF + KD, 1 + 2 * NF + KD

                    def rounds(eng, body, before=None):
                        n = eng.value_load(most[0:1, 0:1], min_val=0, max_val=T)
                        with eng.If(n > CAP):
                            if before is not None:
                                before()
                            with eng.Fori(0, NE) as e:
                                body(e)

                    with nc.Block() as block:
                        @block.sync
                        def _(sp):
                            def body(e):
                                sp.wait_ge(o_dve, NDV * e + 1)
                                for w, (name, k) in enumerate((("moe_w_gate", KD), ("moe_w_up", KD), ("moe_w_down", NF))):
                                    src = I[name][bass.ds(NE * L + e, 1)].rearrange("a (k p) n -> p (a k) n", p=P)
                                    sp.dma_start(ring[:, 1, w * CH:(w + 1) * CH].rearrange("p (k n) -> p k n", k=k), src).then_inc(o_ld, 16)
                            rounds(sp, body)

                        @block.tensor
                        def _(pe):
                            def body(e):
                                pe.wait_ge(o_dve, NDV * e + 2)
                                nc.tensor.matmul(gb[0][:, 0:T], ones[0:NE, :], gox[:], start=True, stop=True).then_inc(o_pe, 1)
                                pe.wait_ge(o_ld, 48 * e + 48)
                                for f in range(NF):
                                    if f >= 1:
                                        pe.wait_ge(o_dve, NDV * e + 2 + 2 * f)
                                    for w in range(2):
                                        wt = ring[:, 1, w * CH:(w + 1) * CH].rearrange("p (k n) -> p k n", k=KD)
                                        for k in range(KD):
                                            last = nc.tensor.matmul(hb[w][:, 0:T], wt[:, k, f * P:(f + 1) * P], xT[:, k, :], start=k == 0, stop=k == KD - 1)
                                    last.then_inc(o_pe, 1)
                                wt = ring[:, 1, 2 * CH:3 * CH].rearrange("p (k n) -> p k n", k=NF)
                                for d in range(KD):
                                    pe.wait_ge(o_dve, NDV * e + 2 + 2 * NF + d)
                                    for k in range(NF):
                                        last = nc.tensor.matmul(ob[0][:, 0:T], wt[:, k, d * P:(d + 1) * P], ohid[:, k, :], start=k == 0, stop=k == NF - 1)
                                    last.then_inc(o_pe, 1)
                            rounds(pe, body)

                        @block.scalar
                        def _(act):
                            def body(e):
                                for f in range(NF):
                                    act.wait_ge(o_pe, NPE * e + f + 2)
                                    nc.scalar.activation(osg[:], hb[0][:, 0:T], ACT.Silu).then_inc(o_act, 1)
                            rounds(act, body)

                        @block.vector
                        def _(dve):
                            V = nc.vector

                            def before():
                                V.memset(gox[:], 0.0).then_inc(o_dve, 1)

                            def body(e):
                                dve.wait_ge(o_dve, NDV * e + 1)
                                V.tensor_scalar(gox[:], gto[:], ident[0:NE, bass.ds(e, 1)], None, ALU.mult).then_inc(o_dve, 1)
                                for f in range(NF):
                                    dve.wait_ge(o_act, NF * e + f + 1)
                                    V.tensor_tensor(ohu[:], hb[1][:, 0:T], osg[:], ALU.mult).then_inc(o_dve, 1)
                                    dve.wait_ge(o_dve, NDV * e + 3 + 2 * f)
                                    V.tensor_tensor(ohid[:, f, :], gb[0][:, 0:T], ohu[:], ALU.mult).then_inc(o_dve, 1)
                                for d in range(KD):
                                    dve.wait_ge(o_pe, NPE * e + NF + d + 2)
                                    V.tensor_tensor(acc[:, d, :], acc[:, d, :], ob[0][:, 0:T], ALU.add).then_inc(o_dve, 1)
                            rounds(dve, body, before)

                def gate_weights(sp):
                    w = I["ple_gate"][L].rearrange("(k p) n -> p k n", p=P)
                    load_chunk(sp, 0, w[:, :, 0:512])
                    load_chunk(sp, 2, I["ple_proj"][L].rearrange("(k p) n -> p k n", p=P))
                    load_chunk(sp, 1, w[:, :, 512:1024])

                layer_norm(L, 1, acc, acc, f"b{L}", gate_weights)
                with ExitStack() as st:
                    pT = st.enter_context(nc.sbuf_tensor(f"pT{L}", [P, 2, T], F32))
                    sgm = st.enter_context(nc.sbuf_tensor(f"sgm{L}", [P, 2, T], F32))
                    pa = [st.enter_context(nc.psum_tensor(f"pa{L}{i}", [P, 512], F32)) for i in range(2)]
                    pb = [st.enter_context(nc.psum_tensor(f"pb{L}{i}", [P, 512], F32)) for i in range(2)]
                    ld_p, e_done, e_sig, e_out = ple_sems
                    cnt = [16 * c for c in chunk_count]
                    with nc.Block() as block:
                        @block.sync
                        def _(sp):
                            sp.dma_start(pT[:], I["pT"][L].rearrange("(k p) t -> p k t", p=P)).then_inc(ld_p, 16)
                            if L == 0:
                                for c in range(2):
                                    sp.wait_ge(e_done, 4 * c + 4)
                                    load_chunk(sp, c, I["nsa_w_in"].rearrange("(k p) n -> p k n", p=P)[:, :, 512 * c:512 * c + 512])
                            if out is not None:
                                sp.wait_ge(e_out, KD * L + KD)
                                store(sp, out, xT[:])

                        @block.tensor
                        def _(pe):
                            wp = chunk[2][:, 0:2 * D].rearrange("p (k n) -> p k n", k=2)
                            for m in range(KD):
                                if m % 4 == 0:
                                    pe.wait_ge(ld_chunk[m // 4], cnt[m // 4] + 16)
                                if m >= 2:
                                    pe.wait_ge(e_out, KD * L + m - 1)
                                wc = chunk[m // 4].rearrange("p (k n) -> p k n", k=KD)
                                for k in range(KD):
                                    nc.tensor.matmul(pa[m % 2][:, 0:T], wc[:, k, (m % 4) * P:(m % 4 + 1) * P], acc[:, k, :], start=k == 0, stop=k == KD - 1)
                                if m == 0:
                                    pe.wait_ge(ld_p, 16 * L + 16)
                                    pe.wait_ge(ld_chunk[2], cnt[2] + 16)
                                for k in range(2):
                                    last = nc.tensor.matmul(pb[m % 2][:, 0:T], wp[:, k, m * P:(m + 1) * P], pT[:, k, :], start=k == 0, stop=k == 1)
                                last.then_inc(e_done, 1)

                        @block.scalar
                        def _(act):
                            for m in range(KD):
                                act.wait_ge(e_done, KD * L + m + 1)
                                if m >= 2:
                                    act.wait_ge(e_out, KD * L + m - 1)
                                nc.scalar.activation(sgm[:, m % 2, :], pa[m % 2][:, 0:T], ACT.Sigmoid).then_inc(e_sig, 1)

                        @block.vector
                        def _(dve):
                            for m in range(KD):
                                dve.wait_ge(e_sig, KD * L + m + 1)
                                dve_step(dve, nc.vector.tensor_tensor(sgm[:, m % 2, :], sgm[:, m % 2, :], pb[m % 2][:, 0:T], ALU.mult))
                                nc.vector.tensor_tensor(xT[:, m, :], sgm[:, m % 2, :], acc[:, m, :], ALU.add).then_inc(e_out, 1)
                    for c in range(3):
                        chunk_count[c] += 1

        tail(0)
        with ExitStack() as nsa:
            def sb(name, shape, dt=F32):
                return nsa.enter_context(nc.sbuf_tensor(name, shape, dt))

            qT = sb("q_T", [P, KD, T])
            kvT = sb("kv_T", [P, KVT, T])
            oT = sb("o_T", [P, KD, T])
            gT_ = sb("gates_T", [3 * AH, T])
            vtok = sb("v_tok", [P, QT, 512])
            vnew = sb("v_new", [DB, 512])
            gtok = sb("gates_tok", [P, QT, 3 * AH])
            vcd = sb("vc_dec", [NBP, DB, 256])
            K_CMP, V_CMP, K_SEL, V_SEL, K_WIN, V_WIN = range(0, KVT, 2)
            qbd = ring[:, 1, 2 * CH:2 * CH + 2 * DB * 144].rearrange("p (a c) -> p a c", a=2)
            ld_kv, kv_used, q_zero, q_ok = [sem("d_ldkv0"), sem("d_ldkv1")], sem("d_kv_used"), sem("d_q_zero"), sem("d_q_ok")
            R_WIN, R_VAL = DB, DB + DB // 2
            kv_dmas = lambda n: NPG if n < R_WIN else 2 if n < R_VAL else NPG + 1
            kv_loaded = lambda n: sum(16 * kv_dmas(m) for m in range(n % 2, n + 1, 2))

            def load_kv(sp, n):
                s = n % 2
                if n >= 2:
                    sp.wait_ge(kv_used, n - 1)
                if R_WIN <= n < R_VAL:
                    for a in range(2):
                        sp.dma_start(kvb[:, s, a * 1024:(a + 1) * 1024].rearrange("p (c t) -> p c t", c=2), I["kwin"][2 * (n - R_WIN) + a]).then_inc(ld_kv[s], 16)
                    return
                b = n if n < R_WIN else n - R_VAL
                for g in range(NPG):
                    page = sp.value_load(ptab[0:1, b * NPG + g:b * NPG + g + 1], min_val=0, max_val=I["cmp_pages"].shape[0] - 1)
                    src = I["ksel_pages" if n < R_WIN else "vsel_pages"][bass.ds(page, 1)].rearrange("a p c -> (a p) c")
                    sp.dma_start(kvb[:, s, g * 256:(g + 1) * 256], src).then_inc(ld_kv[s], 16)
                if n >= R_VAL:
                    sp.dma_start(kvb[:, s, 2048:3072].rearrange("p (a c) -> p a c", a=4), I["vwin"][b]).then_inc(ld_kv[s], 16)

            sel_sc = [nsa.enter_context(nc.psum_tensor(f"sel_scores{n}", [P, 512], F32)) for n in range(2)]
            n_base = [16 * c for c in chunk_count]

            with ExitStack() as st:
                bank = [st.enter_context(nc.psum_tensor(f"np{i}", [P, 512], F32)) for i in range(6)] + sel_sc
                cpg = st.enter_context(nc.sbuf_tensor("cmp_pages", [P, 2, NPG, 4, PAGE], F32))
                tile_done, tile_taken = sem("n_tile_done"), sem("n_tile_taken")
                ld_c, c_used = [sem("c_ld0"), sem("c_ld1")], sem("c_used")
                NT = KD + KVT + 1
                nchunk = (NT + 3) // 4
                with nc.Block() as block:
                    @block.sync
                    def _(sp):
                        for b in range(DB):
                            if b >= 2:
                                sp.wait_ge(c_used, b - 1)
                            for n in range(NPG):
                                page = sp.value_load(ptab[0:1, b * NPG + n:b * NPG + n + 1], min_val=0, max_val=I["cmp_pages"].shape[0] - 1)
                                sp.dma_start(cpg[:, b % 2, n], I["cmp_pages"][bass.ds(page, 1)].rearrange("a p c t -> (a p) c t")).then_inc(ld_c[b % 2], 16)

                    @block.vector
                    def _(dve):
                        V = nc.vector
                        for b in range(DB):
                            dve.wait_ge(ld_c[b % 2], 16 * NPG * (b // 2 + 1))
                            for a in range(4):
                                x = cpg[:, b % 2, :, a, :].rearrange("p n (c l) -> p n c l", l=BLK)
                                i1 = V.tensor_tensor(x, x, wb[:, a:a + 1, :].unsqueeze(1).to_broadcast([P, NPG, 2, BLK]), ALU.mult)
                            dve_step(dve, i1)
                            for a in range(4):
                                x = cpg[:, b % 2, :, a, :].rearrange("p n (c l) -> p n c l", l=BLK)
                                i1 = V.tensor_reduce(kcd[:, a, b, :].rearrange("p (n c) -> p n c", c=2), x, AX.X, ALU.add)
                            i1.then_inc(c_used, 1)

                    @block.tensor
                    def _(pe):
                        for m in range(NT):
                            c, s = m // 4, (m // 4) % 2
                            if m % 4 == 0:
                                pe.wait_ge(ld_chunk[s], n_base[s] + 16 * (c // 2 + 1))
                            if m >= 8:
                                pe.wait_ge(tile_taken, m - 7)
                            M = P if m < NT - 1 else 3 * AH
                            wc = chunk[s][:, 0:KD * (512 if m < NT - 1 else M)].rearrange("p (k n) -> p k n", k=KD)
                            for k in range(KD):
                                last = nc.tensor.matmul(bank[m % 8][0:M, 0:T], wc[:, k, (m % 4) * P:(m % 4) * P + M],
                                                        xT[:, k, :], start=k == 0, stop=k == KD - 1)
                            last.then_inc(tile_done, 1)

                    @block.scalar
                    def _(act):
                        w = I["nsa_w_in"].rearrange("(k p) n -> p k n", p=P)
                        for m in range(NT):
                            act.wait_ge(tile_done, m + 1)
                            if m < KD:
                                nc.scalar.activation(qT[:, m, :], bank[m % 8][:, 0:T], ACT.Copy, scale=QS).then_inc(tile_taken, 1)
                            elif m < NT - 1:
                                nc.scalar.activation(kvT[:, m - KD, :], bank[m % 8][:, 0:T], ACT.Copy).then_inc(tile_taken, 1)
                            else:
                                nc.scalar.activation(gT_[:], bank[m % 8][0:3 * AH, 0:T], ACT.Sigmoid).then_inc(tile_taken, 1)
                            c = (m + 1) // 4 + 1
                            if (m + 1) % 4 == 0 and 2 <= c < nchunk:
                                load_chunk(act, c % 2, w[:, :, c * 512:min(c * 512 + 512, w.shape[2])])
                chunk_count[0] += (nchunk + 1) // 2
                chunk_count[1] += nchunk // 2

            kvb = sb("kv_ring", [P, 2, 3072])

            with ExitStack() as st:
                def sb2(name, shape, dt=F32):
                    return st.enter_context(nc.sbuf_tensor(name, shape, dt))

                dm = sb2("dist_masked", [P, 3 * P])
                cbias, cmask = sb2("cmp_bias", [P, QT, AH, 4]), sb2("cmp_mask", [P, QT, AH, 4])
                ctmp = sb2("cmp_tmp", [P, 4, SEQ])
                kc = sb2("cmp_prompt", [P, 4, 4])
                vx = sb2("vc_spread", [P, 580])
                vci = sb2("vc_blockdiag", [4 * AH, KD, P])
                pc = sb2("cmp_probs", [P, QT, AH, 4])
                pst = sb2("cmp_stat", [P, QT, AH])
                pct = sb2("cmp_probs_T", [4 * AH, SEQ])
                sbuf = sb2("scores", [P, 4, 3 * P])
                nm, sm, wgt = sb2("neg_max", [P, 4, 2]), sb2("row_sum", [P, 4, 2]), sb2("row_scale", [P, 4, 2])
                pts = sb2("probs_T", [P, 2, 3 * P])
                pt = [st.enter_context(nc.psum_tensor(f"at{i}", [P, 512], F32)) for i in range(6)] + sel_sc
                ld_ac, vc_tr, vc_taken, kc_ok, pre_tr, pre_tk, csc, cexp_in, cexp, pc_ok, pc_tr, pct_ok = (
                    sem("h_" + n) for n in ("ld", "vc_tr", "vc_taken", "kc", "pre_tr", "pre_tk", "csc", "cexp_in", "cexp", "pc", "pc_tr", "pct"))
                score_done, soft_done, ex_done, wgt_ok, scaled, tr_ok, pts_ok, pv_ok, ot_ok = (
                    sem("u_" + n) for n in ("score", "soft", "exp", "wgt", "scaled", "tr", "pts", "pv", "ot"))
                NU = 4 * KD

                def unit(u):
                    i, half, v = u // 4, (u // 2) % 2, u % 2
                    return i, 64 * half, v, 8 * (i // 4) + i % 4 + 4 * half, 2 * (i // 4) + half

                with nc.Block() as block:
                    @block.sync
                    def _(sp):
                        for dst, n in ((dm, "dist_masked"), (cbias, "cmp_bias"), (cmask, "cmp_mask")):
                            sp.dma_start(dst[:], I[n]).then_inc(ld_ac, 16)
                        store(sp, O["kv"], kvT[:])
                        for n in range(2):
                            load_kv(sp, n)
                        w = I["nsa_w_out"].rearrange("(k p) n -> p k n", p=P)
                        for c in range(2):
                            load_chunk(sp, c, w[:, :, c * 512:(c + 1) * 512])
                        for n in range(2, R_WIN + 2):
                            load_kv(sp, n)

                    @block.gpsimd
                    def _(pool):
                        nc.gpsimd.memset(qbd, 0.0).then_inc(q_zero, 1)
                        for u in range(NU):
                            pool.wait_ge(wgt_ok, u + 1)
                            s = sbuf[:, u % 4, :]
                            nc.gpsimd.tensor_scalar(s[:, 0:P], s[:, 0:P], wgt[:, u % 4, 0:1], None, ALU.mult).then_inc(scaled, 1)
                            nc.gpsimd.tensor_scalar(s[:, P:3 * P], s[:, P:3 * P], wgt[:, u % 4, 1:2], None, ALU.mult).then_inc(scaled, 1)

                    @block.tensor
                    def _(pe):
                        tr, mm = nc.tensor.transpose, nc.tensor.matmul
                        for b in range(DB):
                            for p in range(2):
                                last = tr(pt[4 + b // 2][0:NBP, ((b % 2) * 2 + p) * P:((b % 2) * 2 + p + 1) * P], kcd[:, 2 + p, b, :], ident[:])
                        last.then_inc(vc_tr, 1)
                        vt = (V_SEL, V_SEL + 1, V_WIN, V_WIN + 1)
                        for q in range(QT):
                            for a, t in enumerate(vt):
                                last = tr(pt[q][:, a * P:(a + 1) * P], kvT[:, t, q * P:(q + 1) * P], ident[:])
                            last.then_inc(pre_tr, 1)
                        for a, t in enumerate(vt):
                            last = tr(pt[2][0:DB, a * P:(a + 1) * P], kvT[:, t, SEQ:T], ident[:])
                        last.then_inc(pre_tr, 1)
                        for q in range(QT):
                            last = tr(pt[3][:, q * 48:(q + 1) * 48], gT_[:, q * P:(q + 1) * P], ident[0:48, 0:48])
                        last.then_inc(pre_tr, 1)
                        pe.wait_ge(kc_ok, 1)
                        pe.wait_ge(vc_taken, 1)
                        for i in range(KD):
                            for half in range(2):
                                r, h = slice(64 * half, 64 * half + 64), 8 * (i // 4) + i % 4 + 4 * half
                                for q in range(QT):
                                    last = mm(pt[4 + half][:, (q * AH + h) * 4:(q * AH + h) * 4 + 4], qT[r, i, q * P:(q + 1) * P], kc[r, i // 4, :], start=True, stop=True)
                        last.then_inc(csc, 1)
                        pe.wait_ge(kc_ok, 2)
                        pe.wait_ge(pre_tk, 2)
                        for i in range(KD):
                            last = tr(pt[i // 4][0:64, (i % 4) * P:(i % 4 + 1) * P], vx[:, i * 64:(i + 1) * 64], ident[:])
                        last.then_inc(pre_tr, 1)
                        pe.wait_ge(pc_ok, 1)
                        for q in range(QT):
                            last = tr(pt[2][0:64, q * P:(q + 1) * P], pc[:, q].rearrange("p h n -> p (h n)"), ident[:])
                        last.then_inc(pc_tr, 1)
                        pe.wait_ge(pct_ok, 1)
                        pe.wait_ge(pre_tk, 5)

                        def score(u):
                            i, lo, v, h, kv = unit(u)
                            if u >= 2:
                                pe.wait_ge(soft_done, 2 * (u - 1))
                            r, kt = slice(lo, lo + 64), (K_WIN if v else K_SEL) + i // 4
                            mm(pt[u % 2][:, 0:P], qT[r, i, 0:P], kvT[r, kt, 0:P], start=True, stop=True)
                            mm(pt[u % 2][:, P:3 * P], qT[r, i, P:SEQ], kvT[r, kt, 0:SEQ], start=True, stop=True).then_inc(score_done, 1)

                        def turn(u):
                            pe.wait_ge(scaled, 2 * u + 2)
                            if u >= 2:
                                pe.wait_ge(pts_ok, u - 1)
                            for a in range(3):
                                last = tr(pt[2 + u % 2][:, a * P:(a + 1) * P], sbuf[:, u % 4, a * P:(a + 1) * P], ident[:])
                            last.then_inc(tr_ok, 1)

                        def values(u):
                            i, lo, v, h, kv = unit(u)
                            ob = pt[4 + i % 2]
                            if u % 4 == 0:
                                if i >= 2:
                                    pe.wait_ge(ot_ok, i - 1)
                                mm(ob[:, 0:SEQ], vci[:, i, :], pct[:], start=True, stop=False, skip_group_check=True)
                            pe.wait_ge(pts_ok, u + 1)
                            vw = slice(v * 256 + kv * 64, v * 256 + kv * 64 + 64)
                            mm(ob[lo:lo + 64, 0:SEQ], vtok[:, 0, vw], pts[:, u % 2, 0:SEQ], start=False, stop=False, skip_group_check=True)
                            mm(ob[lo:lo + 64, P:SEQ], vtok[:, 1, vw], pts[:, u % 2, SEQ:3 * P], start=False, stop=u % 4 >= 1, skip_group_check=True).then_inc(pv_ok, 1)

                        def decode_keys(u):
                            b, p, a = u // 4, (u // 2) % 2, u % 2
                            if u == 0:
                                pe.wait_ge(q_ok, 1)
                            if u % 4 == 0:
                                pe.wait_ge(ld_kv[b % 2], kv_loaded(b))
                            k3 = kvb[:, b % 2, 0:2048].rearrange("p (g c t) -> p g c t", g=NPG, c=2)
                            last = mm(sel_sc[a][:], qbd[:, p, b * P:(b + 1) * P], k3[:, 4 * a:4 * a + 4, p, :],
                                      start=b == 0 and p == 0, stop=b == DB - 1 and p == 1)
                            if u % 4 == 3:
                                last.then_inc(kv_used, 1)

                        for u in range(3):
                            score(u)
                        for u in range(NU):
                            decode_keys(u)
                            turn(u)
                            if u + 3 < NU:
                                score(u + 3)
                            if u >= 1:
                                values(u - 1)
                        values(NU - 1)

                    @block.scalar
                    def _(act):
                        A_ = nc.scalar.activation
                        act.wait_ge(cexp_in, 1)
                        A_(pc[:], pc[:], ACT.Exp).then_inc(cexp, 1)

                        def exps(u):
                            act.wait_ge(soft_done, 2 * u + 2)
                            if u >= 4:
                                act.wait_ge(wgt_ok, u - 3)
                            s = sbuf[:, u % 4, :]
                            A_(s[:, 0:P], s[:, 0:P], ACT.Exp, bias=nm[:, u % 4, 0:1], accum_out=sm[:, u % 4, 0:1]).then_inc(ex_done, 1)
                            A_(s[:, P:3 * P], s[:, P:3 * P], ACT.Exp, bias=nm[:, u % 4, 1:2], accum_out=sm[:, u % 4, 1:2]).then_inc(ex_done, 1)

                        exps(0)
                        exps(1)
                        for u in range(NU):
                            if u + 2 < NU:
                                exps(u + 2)
                            act.wait_ge(tr_ok, u + 1)
                            if u >= 2:
                                act.wait_ge(pv_ok, u - 1)
                            A_(pts[:, u % 2, :], pt[2 + u % 2][:, 0:3 * P], ACT.Copy).then_inc(pts_ok, 1)

                    @block.vector
                    def _(dve):
                        V = nc.vector
                        for a in range(4):
                            i1 = V.tensor_tensor(ctmp[:, a, :].rearrange("p (n l) -> p n l", l=BLK), kvT[:, a, 0:SEQ].rearrange("p (n l) -> p n l", l=BLK),
                                                 wb[:, a:a + 1, :].to_broadcast([P, 4, BLK]), ALU.mult)
                        dve_step(dve, i1)
                        V.tensor_reduce(kc[:].rearrange("p a n -> p (a n)"), ctmp[:].rearrange("p a (n l) -> p (a n) l", l=BLK), AX.X, ALU.add).then_inc(kc_ok, 1)
                        dve_step(dve, V.memset(vx[:], 0.0))
                        dve.wait_ge(kc_ok, 1)
                        for p in range(2):
                            for half in range(2):
                                r, base = slice(64 * half, 64 * half + 64), 288 * p + 16 * half
                                i1 = V.tensor_copy(vx[r, base:base + 272].rearrange("q (r c) -> q r c", c=68)[:, :, 0:4],
                                                   kc[r, 2 + p:3 + p, :].to_broadcast([64, 4, 4]))
                        i1.then_inc(kc_ok, 1)
                        dve.wait_ge(vc_tr, 1)
                        for n in range(4):
                            i1 = V.tensor_copy(vcd[:, 2 * n:2 * n + 2, :].rearrange("p b d -> p (b d)"), pt[4 + n][0:NBP, :])
                        i1.then_inc(vc_taken, 1)
                        for q in range(QT):
                            dve.wait_ge(pre_tr, q + 1)
                            V.tensor_copy(vtok[:, q, :], pt[q][:]).then_inc(pre_tk, 1)
                        dve.wait_ge(pre_tr, 3)
                        V.tensor_copy(vnew[:], pt[2][0:DB, :]).then_inc(pre_tk, 1)
                        dve.wait_ge(pre_tr, 4)
                        dve_step(dve, V.tensor_copy(gtok[:], pt[3][:, 0:96].rearrange("p (q c) -> p q c", q=QT)))
                        dve.wait_ge(csc, 1)
                        dve.wait_ge(ld_ac, 48)
                        f = lambda t: t[:].rearrange("p q h n -> p (q h) n")
                        g = lambda t: t[:].rearrange("p q h -> p (q h)")
                        bc = g(pst).unsqueeze(2).to_broadcast([P, QT * AH, 4])
                        e = lambda t, half: t.rearrange("p (a f c) -> p a f c", f=2, c=16)[:, :, half, :]
                        w = lambda t: t[:].rearrange("p q h n -> p (q h n)")
                        V.tensor_tensor(e(w(pc), 0), e(pt[4][:, 0:QT * AH * 4], 0), e(w(cbias), 0), ALU.add)
                        dve_step(dve, V.tensor_tensor(e(w(pc), 1), e(pt[5][:, 0:QT * AH * 4], 1), e(w(cbias), 1), ALU.add))
                        dve_step(dve, V.tensor_reduce(g(pst), f(pc), AX.X, ALU.max))
                        V.tensor_tensor(f(pc), f(pc), bc, ALU.subtract).then_inc(cexp_in, 1)
                        dve.wait_ge(cexp, 1)
                        dve_step(dve, V.tensor_tensor(f(pc), f(pc), f(cmask), ALU.mult))
                        dve_step(dve, V.tensor_reduce(g(pst), f(pc), AX.X, ALU.add))
                        dve_step(dve, V.tensor_scalar(g(pst), g(pst), 1e-30, None, ALU.max))
                        dve_step(dve, V.reciprocal(g(pst), g(pst)))
                        g3 = gtok[:].rearrange("p q (h c) -> p q h c", c=3)
                        dve_step(dve, V.tensor_tensor(pst[:], pst[:], g3[:, :, :, 0], ALU.mult))
                        V.tensor_tensor(f(pc), f(pc), bc, ALU.mult).then_inc(pc_ok, 1)
                        dve.wait_ge(pre_tr, 5)
                        for a in range(2):
                            i1 = V.tensor_copy(vci[:, 4 * a:4 * a + 4, :], pt[a][0:64, :].rearrange("p (i m) -> p i m", i=4))
                        i1.then_inc(pre_tk, 1)
                        dve.wait_ge(pc_tr, 1)
                        V.tensor_copy(pct[:], pt[2][0:64, 0:SEQ]).then_inc(pre_tk, 1)
                        dve.wait_ge(pre_tk, 5)
                        dve_step(dve, V.memset(wgt[:], 0.0))
                        V.tensor_copy(nm[:], wgt[:]).then_inc(pct_ok, 1)
                        dve.wait_ge(pct_ok, 1)
                        dve.wait_ge(q_zero, 1)
                        for p in range(2):
                            for half in range(2):
                                r = slice(64 * half, 64 * half + 64)
                                i1 = V.tensor_copy(qbd[r, p, :].rearrange("q (b c) -> q b c", c=144)[:, :, 8 * p + 4 * half:8 * p + 4 * half + 4],
                                                   qT[r, 4 * p:4 * p + 4, SEQ:T].rearrange("q r b -> q b r"))
                        i1.then_inc(q_ok, 1)

                        def soft(u):
                            i, lo, v, h, kv = unit(u)
                            dve.wait_ge(score_done, u + 1)
                            if u >= 4:
                                dve.wait_ge(tr_ok, u - 3)
                            s = sbuf[:, u % 4, :]
                            dve_step(dve, V.scalar_tensor_tensor(s, dm[:], -2.0 ** (-8.0 * (h + 1) / AH), pt[u % 2][:, 0:3 * P], ALU.mult, ALU.add))
                            V.tensor_reduce(nm[:, u % 4, 0:1], s[:, 0:P], AX.X, ALU.max, negate=True).then_inc(soft_done, 1)
                            V.tensor_reduce(nm[:, u % 4, 1:2], s[:, P:3 * P], AX.X, ALU.max, negate=True).then_inc(soft_done, 1)

                        def scale(u):
                            i, lo, v, h, kv = unit(u)
                            dve.wait_ge(ex_done, 2 * u + 2)
                            if u >= 4:
                                dve.wait_ge(scaled, 2 * (u - 3))
                            dve_step(dve, V.reciprocal(wgt[:, u % 4, :], sm[:, u % 4, :]))
                            V.tensor_tensor(wgt[:, u % 4, :], wgt[:, u % 4, :], g3[:, :, h, 1 + v], ALU.mult).then_inc(wgt_ok, 1)

                        def out_tile(i):
                            dve.wait_ge(pv_ok, 4 * i + 4)
                            V.tensor_copy(oT[:, i, 0:SEQ], pt[4 + i % 2][:, 0:SEQ]).then_inc(ot_ok, 1)

                        soft(0)
                        soft(1)
                        scale(0)
                        for u in range(NU):
                            if u + 2 < NU:
                                soft(u + 2)
                            if u + 1 < NU:
                                scale(u + 1)
                            if u >= 5 and (u - 5) % 4 == 0:
                                out_tile((u - 5) // 4)
                        out_tile(KD - 1)

            with ExitStack() as st:
                def sb2(name, shape, dt=F32):
                    return st.enter_context(nc.sbuf_tensor(name, shape, dt))

                biasd, biasw, cbd, g4, idx, mb = (sb2(n, s) for n, s in (("bias_dec", [P, PAST]), ("bias_win", [P, WIN]), ("bias_cmp", [P, NBP]),
                                                                       ("same_group", [P, P]), ("block_idx", [P, NBP]), ("batch_mask", [P, DB])))
                gmask, gsel = sb2("gate_mask", [48, AH]), sb2("gate_sel", [48, 3])
                gl = sb2("gate_spread", [48, DB, AH])
                gd = sb2("gate_dec", [P, 3])
                ss, sw = sb2("s_sel", [P, PAST + 1]), sb2("s_win", [P, WIN + 1])
                sc, pcn, nb, tmp = sb2("s_cmp", [P, NBP]), sb2("p_cmp", [P, NBP]), sb2("block_bias", [P, NBP]), sb2("imp_tmp", [P, NBP])
                nmx, sums, rcp, ex_ = sb2("d_negmax", [P, 3]), sb2("d_sum", [P, 3]), sb2("d_rcp", [P, 3]), sb2("excluded", [P, 2])
                pnd = sb2("p_new_diag", [P, 2, DB])
                ptd = sb2("d_probs_T", [P, 12, P])
                k18 = sb2("d_small_keys", [P, 2, DB, 2 + NBP])
                od = ring[0:AH, 1, 2 * CH:2 * CH + DB * 256]
                pcd, pnt = sb2("d_pcmp_T", [NBP, P]), sb2("d_pnew_T", [DB, 2, P])
                pt = sel_sc + [st.enter_context(nc.psum_tensor(f"dt{i}", [P, 512], F32)) for i in range(6)]
                ld_dc, k18_ok, o_head, o_turned, gl_ok, s_small, imp_in, imp_ok, to_exp, exped, p_ok, t_ok, t_taken = (
                    sem("d_" + n) for n in ("ldc", "k18", "o_head", "o_turned", "gl", "s_small", "imp_in", "imp", "to_exp", "exped", "p", "t", "tk"))

                with nc.Block() as block:
                    @block.sync
                    def _(sp):
                        cl = (("bias_dec", biasd), ("bias_win", biasw), ("bias_cmp", cbd), ("same_group", g4), ("block_idx", idx), ("batch_mask", mb),
                              ("gate_mask", gmask), ("gate_sel", gsel))
                        for n, (name, dst) in enumerate(cl):
                            sp.dma_start(dst[:], I[name]).then_inc(ld_dc, 16)
                        for n in range(R_WIN + 2, R_VAL + DB):
                            load_kv(sp, n)

                    @block.tensor
                    def _(pe):
                        tr, mm = nc.tensor.transpose, nc.tensor.matmul
                        pe.wait_ge(k18_ok, 1)
                        for b in range(DB):
                            for p in range(2):
                                mm(pt[3][:, 0:2 + NBP], qbd[:, p, b * P:(b + 1) * P], k18[:, p, b, :], start=b == 0 and p == 0, stop=b == DB - 1 and p == 1)
                        pe.wait_ge(gl_ok, 1)
                        mm(pt[3][:, 18:21], gl[:].rearrange("k b h -> k (b h)"), gsel[:], start=True, stop=True).then_inc(s_small, 1)
                        pe.wait_ge(imp_in, 1)
                        mm(pt[4][:, 0:NBP], g4[:], pcn[:], start=True, stop=True).then_inc(imp_ok, 1)
                        for b in range(DB):
                            n = R_WIN + b // 2
                            if b % 2 == 0:
                                pe.wait_ge(ld_kv[n % 2], kv_loaded(n))
                            kw = kvb[:, n % 2, (b % 2) * 1024:(b % 2 + 1) * 1024].rearrange("p (c t) -> p c t", c=2)
                            for p in range(2):
                                last = mm(pt[2][:], qbd[:, p, b * P:(b + 1) * P], kw[:, p, :], start=b == 0 and p == 0, stop=b == DB - 1 and p == 1)
                            if b % 2 == 1:
                                last.then_inc(kv_used, 1)
                        pe.wait_ge(p_ok, 3)
                        for a in range(8):
                            last = tr(pt[5 * (a // 4)][:, (a % 4) * P:(a % 4 + 1) * P], ss[:, a * P:(a + 1) * P], ident[:])
                        for a in range(4):
                            last = tr(pt[1][:, a * P:(a + 1) * P], sw[:, a * P:(a + 1) * P], ident[:])
                        tr(pt[2][0:NBP, 0:P], sc[:], ident[:])
                        tr(pt[2][0:DB, P:2 * P], pnd[:, 0, :], ident[:])
                        tr(pt[2][0:DB, 2 * P:3 * P], pnd[:, 1, :], ident[:]).then_inc(t_ok, 1)
                        pe.wait_ge(t_taken, 1)
                        for b in range(DB):
                            n, cols = R_VAL + b, slice(b * AH, (b + 1) * AH)
                            o = pt[b // 2][0:AH, (b % 2) * 256:(b % 2 + 1) * 256]
                            for v in range(2):
                                mm(o, pnt[:, v, cols], vnew[:, v * 256:(v + 1) * 256], start=v == 0, stop=False)
                            mm(o, pcd[:, cols], vcd[:, b, :], start=False, stop=False)
                            pe.wait_ge(ld_kv[n % 2], kv_loaded(n))
                            for g in range(12):
                                last = mm(o, ptd[:, g, cols], kvb[:, n % 2, g * 256:(g + 1) * 256], start=False, stop=g == 11)
                            last.then_inc(kv_used, 1)
                        for b in range(DB):
                            if b % 2 == 0:
                                pe.wait_ge(o_head, b // 2 + 1)
                            for p in range(2):
                                last = tr(pt[6 + p][:, b * AH:(b + 1) * AH], od[:, b * 256 + p * P:b * 256 + (p + 1) * P], ident[0:AH, 0:AH])
                        last.then_inc(o_turned, 1)

                    @block.scalar
                    def _(act):
                        A_ = nc.scalar.activation
                        act.wait_ge(to_exp, 1)
                        A_(sc[:], sc[:], ACT.Exp, bias=nmx[:, 0:1], accum_out=sums[:, 0:1]).then_inc(exped, 1)
                        act.wait_ge(to_exp, 2)
                        A_(ss[:], ss[:], ACT.Exp, bias=nmx[:, 1:2], accum_out=sums[:, 1:2]).then_inc(exped, 1)
                        act.wait_ge(to_exp, 3)
                        A_(sw[:], sw[:], ACT.Exp, bias=nmx[:, 2:3], accum_out=sums[:, 2:3]).then_inc(exped, 1)
                        for n in range(DB // 2):
                            act.wait_ge(kv_used, R_VAL + 2 * n + 2)
                            A_(od[:, n * 512:(n + 1) * 512], pt[n][0:AH, :], ACT.Copy).then_inc(o_head, 1)

                    @block.vector
                    def _(dve):
                        V = nc.vector
                        for p in range(2):
                            V.tensor_copy(k18[:, p, :, 0:1], kvT[:, K_SEL + p, SEQ:T].unsqueeze(2))
                            V.tensor_copy(k18[:, p, :, 1:2], kvT[:, K_WIN + p, SEQ:T].unsqueeze(2))
                            i1 = V.tensor_copy(k18[:, p, :, 2:2 + NBP], kcd[:, p, :, :])
                        i1.then_inc(k18_ok, 1)
                        dve.wait_ge(ld_dc, 16 * 8)
                        V.tensor_tensor(gl[:], gT_[:, SEQ:T].unsqueeze(2).to_broadcast([48, DB, AH]), gmask[:].unsqueeze(1).to_broadcast([48, DB, AH]), ALU.mult).then_inc(gl_ok, 1)
                        dve.wait_ge(s_small, 1)
                        V.tensor_copy(gd[:], pt[3][:, 18:21])
                        dve_step(dve, V.tensor_tensor(sc[:], pt[3][:, 2:2 + NBP], cbd[:], ALU.add))
                        V.tensor_reduce(nmx[:, 0:1], sc[:], AX.X, ALU.max, negate=True).then_inc(to_exp, 1)
                        V.tensor_copy(ss[:, PAST:PAST + 1], pt[3][:, 0:1])
                        V.tensor_copy(sw[:, WIN:WIN + 1], pt[3][:, 1:2])
                        V.tensor_tensor(ss[:, 0:512], pt[0][:], biasd[:, 0:512], ALU.add)
                        dve_step(dve, V.tensor_tensor(ss[:, 512:PAST], pt[1][:], biasd[:, 512:PAST], ALU.add))
                        dve.wait_ge(exped, 1)
                        dve_step(dve, V.reciprocal(rcp[:, 0:1], sums[:, 0:1]))
                        V.tensor_scalar(pcn[:], sc[:], rcp[:, 0:1], None, ALU.mult).then_inc(imp_in, 1)
                        dve.wait_ge(imp_in, 1)
                        V.tensor_scalar(sc[:], pcn[:], gd[:, 0:1], None, ALU.mult).then_inc(p_ok, 1)
                        dve.wait_ge(imp_ok, 1)
                        dve_step(dve, V.tensor_copy(tmp[:], pt[4][:, 0:NBP]))
                        dve_step(dve, V.tensor_reduce(ex_[:, 0:1], tmp[:, 1:NBP], AX.X, ALU.min))
                        dve_step(dve, V.tensor_scalar(nb[:], tmp[:], ex_[:, 0:1], None, ALU.is_equal))
                        dve_step(dve, V.tensor_tensor(nb[:], nb[:], idx[:], ALU.mult))
                        dve_step(dve, V.tensor_reduce(ex_[:, 1:2], nb[:, 1:NBP], AX.X, ALU.max))
                        dve_step(dve, V.tensor_scalar(nb[:], idx[:], ex_[:, 1:2], NEG, ALU.is_equal, ALU.mult))
                        s3 = ss[:, 0:PAST].rearrange("p (n l) -> p n l", l=BLK)
                        dve_step(dve, V.tensor_tensor(s3, s3, nb[:].unsqueeze(2).to_broadcast([P, NBP, BLK]), ALU.add))
                        V.tensor_reduce(nmx[:, 1:2], ss[:], AX.X, ALU.max, negate=True).then_inc(to_exp, 1)
                        dve.wait_ge(kv_used, R_VAL)
                        dve_step(dve, V.tensor_tensor(sw[:, 0:WIN], pt[2][:], biasw[:], ALU.add))
                        V.tensor_reduce(nmx[:, 2:3], sw[:], AX.X, ALU.max, negate=True).then_inc(to_exp, 1)
                        for n, (x, v) in enumerate(((ss, 1), (sw, 2))):
                            dve.wait_ge(exped, 2 + n)
                            dve_step(dve, V.reciprocal(rcp[:, v:v + 1], sums[:, v:v + 1]))
                            dve_step(dve, V.tensor_tensor(rcp[:, v:v + 1], rcp[:, v:v + 1], gd[:, v:v + 1], ALU.mult))
                            dve_step(dve, V.tensor_scalar(x[:], x[:], rcp[:, v:v + 1], None, ALU.mult))
                            V.tensor_scalar(pnd[:, v - 1, :], mb[:], x[:, x.shape[1] - 1:x.shape[1]], None, ALU.mult).then_inc(p_ok, 1)
                        dve.wait_ge(t_ok, 1)
                        V.tensor_copy(ptd[:, 0:4, :], pt[0][:].rearrange("p (a c) -> p a c", a=4))
                        V.tensor_copy(ptd[:, 4:8, :], pt[5][:].rearrange("p (a c) -> p a c", a=4))
                        V.tensor_copy(ptd[:, 8:12, :], pt[1][:].rearrange("p (a c) -> p a c", a=4))
                        V.tensor_copy(pcd[:], pt[2][0:NBP, 0:P])
                        V.tensor_copy(pnt[:], pt[2][0:DB, P:3 * P].rearrange("p (a c) -> p a c", a=2)).then_inc(t_taken, 1)
                        dve.wait_ge(o_turned, 1)
                        for p in range(2):
                            for half in range(2):
                                r = slice(64 * half, 64 * half + 64)
                                V.tensor_copy(oT[r, 4 * p:4 * p + 4, SEQ:T],
                                              pt[6 + p][r, 0:P].rearrange("q (b c) -> q b c", c=AH)[:, :, 8 * p + 4 * half:8 * p + 4 * half + 4].rearrange("q b r -> q r b"))

            with ExitStack() as st:
                bank = [st.enter_context(nc.psum_tensor(f"no{i}", [P, 512], F32)) for i in range(4)]
                o_done, o_taken = sem("no_done"), sem("no_taken")
                base = [16 * c for c in chunk_count]
                with nc.Block() as block:
                    @block.tensor
                    def _(pe):
                        for m in range(KD):
                            if m % 4 == 0:
                                pe.wait_ge(ld_chunk[m // 4], base[m // 4] + 16)
                            if m >= 4:
                                pe.wait_ge(o_taken, m - 3)
                            wc = chunk[m // 4].rearrange("p (k n) -> p k n", k=KD)
                            for k in range(KD):
                                last = nc.tensor.matmul(bank[m % 4][:, 0:T], wc[:, k, (m % 4) * P:(m % 4 + 1) * P], oT[:, k, :], start=k == 0, stop=k == KD - 1)
                            last.then_inc(o_done, 1)

                    @block.vector
                    def _(dve):
                        for m in range(KD):
                            dve.wait_ge(o_done, m + 1)
                            nc.vector.scalar_tensor_tensor(xT[:, m, :], xT[:, m, :], ALPHA, bank[m % 4][:, 0:T], ALU.mult, ALU.add).then_inc(o_taken, 1)

                    @block.sync
                    def _(sp):
                        sp.wait_ge(stored, n_stored[0])
                for c in range(2):
                    chunk_count[c] += 1

        tail(1, out=O["y"])
        with nc.Block() as block:
            @block.sync
            def _(sp):
                sp.wait_ge(stored, n_stored[0])


def consts():
    c = {}
    r = np.arange(P)
    c["ident"] = np.eye(P, dtype=np.float32)
    c["ones"] = np.ones((P, P), np.float32)
    tri = (r[:, None] <= r[None, :]).astype(np.float32)
    c["m384"] = np.concatenate([tri, c["ones"], tri], 1)
    c["eps"] = np.full((P, 1), EPS, np.float32)
    c["slot_numbers"] = np.ascontiguousarray(np.broadcast_to(np.arange(1, 65, dtype=np.float32), (P, 64)))
    i4 = np.arange(EG)
    c["lower4"] = np.ascontiguousarray(np.broadcast_to((i4[None, :] < i4[:, None]).astype(np.float32), (P, EG, EG)))
    c["hsel"] = np.repeat(np.eye(NH, dtype=np.float32), HD, axis=1)
    slope = 2.0 ** (-8.0 * np.arange(1, AH + 1) / AH)
    f32 = lambda a: np.ascontiguousarray(a, np.float32)
    far = lambda d: np.where(d >= 0, d, 1e33)
    c["dist_masked"] = f32(np.concatenate([far(r[:, None] - r[None, :]), far(P + r[:, None] - np.arange(SEQ)[None, :])], 1))
    d = (np.arange(QT)[None, :, None] * P + r[:, None, None] - ((np.arange(4) + 1) * BLK - 1)).astype(float)[:, :, None, :]
    c["cmp_mask"] = f32(np.broadcast_to(d >= 0, (P, QT, AH, 4)))
    c["cmp_bias"] = f32(np.where(d >= 0, -slope[None, None, :, None] * d, NEG))
    sl = slope[r % AH][:, None]
    pos = np.arange(PAST)[None, :]
    c["bias_dec"] = f32(-sl * (PAST - pos))
    c["bias_win"] = f32(np.where(np.arange(WIN) >= 1, -sl * (WIN - np.arange(WIN)), NEG))
    c["bias_cmp"] = f32(-sl * (PAST - ((np.arange(NBP) + 1) * BLK - 1)))
    c["same_group"] = f32(r[:, None] // REP == r[None, :] // REP)
    c["block_idx"] = f32(np.broadcast_to(np.arange(NBP), (P, NBP)))
    c["batch_mask"] = f32(r[:, None] // AH == np.arange(DB))
    k = np.arange(3 * AH)[:, None]
    c["gate_mask"], c["gate_sel"] = f32(k // 3 == np.arange(AH)), f32(k % 3 == np.arange(3))
    return c


def kernel(x_prompt, x_sample, state_ssm, state_conv, cache_kv, cache_win, page_table, p_prompt, p_sample,
           ssd_w_in, ssd_conv_w, ssd_conv_b, ssd_dt_bias, ssd_a_log, ssd_d, ssd_norm_g, ssd_w_out,
           nsa_w_in, nsa_pos_w, nsa_w_out, ln1_g, ln1_b, ln2_g, ln2_b, router_w, router_bias,
           moe_w_gate, moe_w_up, moe_w_down, ple_proj, ple_gate):
    import concourse.bacc as bacc
    from concourse.bass_utils import run_bass_kernel_spmd

    A = lambda a: np.asarray(a)
    tiles = lambda a: np.moveaxis(A(a).reshape(-1, P, *A(a).shape[1:]), 0, 1)
    cc = np.ascontiguousarray
    ins = consts()
    ins["xT"] = cc(np.concatenate([A(x_prompt)[0], A(x_sample)[:, 0]], 0).T)
    ins["pT"] = cc(np.concatenate([A(p_prompt)[:, 0], A(p_sample)[:, :, 0]], 1).transpose(0, 2, 1))
    ins["state_ssm"] = A(state_ssm)[0].reshape(DB, DI, NS)
    ins["conv_state"] = cc(tiles(A(state_conv)[0].transpose(2, 1, 0)))
    ins["conv_params"] = cc(tiles(np.concatenate([A(ssd_conv_w)[0], A(ssd_conv_b)], 0).T))
    ins["heads"] = cc(np.stack([A(ssd_dt_bias)[0], A(ssd_a_log)[0], A(ssd_d)[0]], 1))
    ins["norm_g"] = cc(tiles(A(ssd_norm_g)[0]))
    ins["lnp"] = cc(np.stack([A(ln1_g), A(ln1_b), A(ln2_g), A(ln2_b)], 1).reshape(2, 4, KD, P).transpose(3, 0, 1, 2))
    ins["router_w"] = cc(tiles(router_w))
    ins["router_bias"] = cc(np.broadcast_to(A(router_bias), (P, NE)))
    ins["ssd_w_in"], ins["ssd_w_out"] = A(ssd_w_in)[0], A(ssd_w_out)[0]
    for n, w in (("moe_w_gate", moe_w_gate), ("moe_w_up", moe_w_up), ("moe_w_down", moe_w_down)):
        ins[n] = A(w).reshape(2 * NE, *w.shape[2:])
    ins["ple_proj"], ins["ple_gate"] = A(ple_proj), A(ple_gate)
    order = [8 * (i // 4) + i % 4 + 4 * half for i in range(KD) for half in range(2)]
    cols = np.concatenate([np.arange(h * 64, h * 64 + 64) for h in order])
    w = A(nsa_w_in)[0]
    ins["nsa_w_in"] = np.concatenate([w[:, cols], w[:, D:]], 1)
    ins["nsa_w_out"] = A(nsa_w_out)[0][cols]
    pw = A(nsa_pos_w)[0].transpose(0, 2, 1).reshape(4, 2, BLK)
    ins["pos_w"] = cc(np.repeat(pw.transpose(1, 0, 2), 64, axis=0))
    ins["page_table"] = A(page_table).reshape(1, -1)
    kv = A(cache_kv)[0].reshape(-1, PAGE, 4, 256)
    ins["cmp_pages"] = cc(kv[:, :, 0:2].reshape(-1, PAGE, 4, P).transpose(0, 3, 2, 1))
    ins["ksel_pages"] = cc(kv[:, :, 2].reshape(-1, PAGE, 2, P).transpose(0, 3, 2, 1)).reshape(-1, P, 256)
    ins["vsel_pages"] = cc(kv[:, :, 3])
    cw = A(cache_win)[0].reshape(DB, WIN, 2, 256)
    ins["kwin"] = cc(cw[:, :, 0].reshape(DB, WIN, 2, P).transpose(0, 3, 2, 1))
    ins["vwin"] = cc(cw[:, :, 1].reshape(DB, 4, P, 256).transpose(0, 2, 1, 3))
    ins["cache_win"] = cw.reshape(DB, WIN, 512)

    outs = {"conv_prompt": (P, JC, 3), "conv_sample": (P, JC, 3, DB), "ssm_prompt": (DI, NS), "ssm_sample": (DB, DI, NS), "y": (P, KD, T)}
    outs |= {"kv": (P, KVT, T), "win_old": (DB, WIN - 1, 512)}
    nc = bacc.Bacc("TRN2", target_bir_lowering=False, num_devices=1)
    I = {n: nc.dram_tensor("in_" + n, a.shape, mybir.dt.from_np(a.dtype), kind="ExternalInput").ap() for n, a in ins.items()}
    O = {n: nc.dram_tensor("out_" + n, s, F32, kind="ExternalOutput").ap() for n, s in outs.items()}
    trunk(nc, I, O)
    r = run_bass_kernel_spmd(nc, [{"in_" + n: a for n, a in ins.items()}], core_ids=[0]).results[0]
    o = {n: A(r["out_" + n]) for n in outs}
    feat = lambda a: np.moveaxis(a, 1, 0).reshape(-1, *a.shape[2:])
    y = feat(o["y"]).T
    conv_p = feat(o["conv_prompt"]).T[None, None]
    conv_s = feat(o["conv_sample"]).transpose(2, 1, 0)[None]
    ssm_p = o["ssm_prompt"].reshape(1, 1, NH, HD, NS)
    ssm_s = o["ssm_sample"].reshape(1, DB, NH, HD, NS)
    kvo = feat(o["kv"]).T.reshape(T, 6, AKV, 64)
    win_s = np.concatenate([o["win_old"].reshape(DB, WIN - 1, 2, AKV, 64), kvo[SEQ:, None, 4:6]], 1)
    return (y[None, :SEQ], y[SEQ:, None], ssm_p, conv_p, kvo[None, None, :SEQ, 0:4], kvo[None, None, :SEQ, 4:6],
            ssm_s, conv_s, kvo[None, SEQ:, None, 0:4], win_s[None])
```
